# Optimizing a Trainium2 kernel written in Bass

```python
import jax, jax.numpy as jnp
from jax import lax
import numpy as np

D_MODEL = 1024
BATCH = 1
SEQ = 1024
DEPTH = 1

CHUNK = 64
Q_BLOCK = 128
HEAD_DIM = 64
SB_WIDTH = 3 * D_MODEL // 8
SB_HEADS = SB_WIDTH // HEAD_DIM
RW_WIDTH = 3 * D_MODEL // 8
RW_HEADS = RW_WIDTH // HEAD_DIM
RW_DECAY_RANK = 32
RW_A_RANK = 32
RW_GATE_RANK = 64
RW_GN_EPS = 64e-5
RW_SPLIT = (RW_WIDTH, RW_WIDTH, RW_WIDTH, RW_DECAY_RANK, RW_A_RANK, RW_GATE_RANK)
RW_IN_WIDTH = sum(RW_SPLIT)
GLA_VAL_WIDTH = D_MODEL // 4
GLA_KEY_WIDTH = GLA_VAL_WIDTH // 2
GLA_DV = 64
GLA_HEADS = GLA_VAL_WIDTH // GLA_DV
GLA_DK = GLA_KEY_WIDTH // GLA_HEADS
GLA_GATE_RANK = 16
GLA_GATE_NORMALIZER = 16.0
GLA_SPLIT = (GLA_KEY_WIDTH, GLA_KEY_WIDTH, GLA_VAL_WIDTH, GLA_GATE_RANK, GLA_VAL_WIDTH)
GLA_IN_WIDTH = sum(GLA_SPLIT)

MIX_WIDTH = SB_WIDTH + RW_WIDTH + GLA_VAL_WIDTH
IN_WIDTH = 3 * SB_WIDTH + RW_IN_WIDTH + GLA_IN_WIDTH
D_FF = 4 * D_MODEL
EPS = 1e-6

kernel_name = 'hybrid_sb_rwkv7_gla_block'

def split_sizes(t, sizes):
    idx = [int(i) for i in np.cumsum(sizes)[:-1]]
    return jnp.split(t, idx, axis=-1)

def rmsnorm(x, gain):
    xf = x.astype(jnp.float32)
    y = xf * lax.rsqrt(jnp.mean(xf * xf, axis=-1, keepdims=True) + EPS)
    return (y * gain.astype(jnp.float32)).astype(x.dtype)

def head_rmsnorm(o, gain, n_heads):
    B, T, C = o.shape
    oh = o.reshape(B, T, n_heads, C // n_heads)
    return rmsnorm(oh, gain.reshape(n_heads, C // n_heads)).reshape(B, T, C)

def token_shift(p, mu):
    prev = jnp.pad(p, ((0, 0), (1, 0), (0, 0)))[:, :-1]
    return p + (prev - p) * mu

def stick_breaking_attention(q, k, v):
    B, T, C = q.shape
    H = SB_HEADS
    Dh = C // H
    n_blk = T // Q_BLOCK
    qh = q.reshape(B, n_blk, Q_BLOCK, H, Dh).transpose(1, 0, 2, 3, 4)
    kh = k.reshape(B, T, H, Dh)
    vh = v.reshape(B, T, H, Dh)
    key_pos = jnp.arange(T)
    scale = Dh ** -0.5

    def block(args):
        q_blk, blk = args
        z = jnp.einsum('bqhd,bkhd->bhqk', q_blk, kh).astype(jnp.float32) * scale
        q_pos = blk * Q_BLOCK + jnp.arange(Q_BLOCK)
        mask = key_pos[None, :] < q_pos[:, None]
        log_1m_beta = jnp.where(mask, jax.nn.log_sigmoid(-z), 0.0)
        between = lax.cumsum(log_1m_beta, axis=3, reverse=True) - log_1m_beta
        weights = jnp.where(mask, jnp.exp(jax.nn.log_sigmoid(z) + between), 0.0)
        return jnp.einsum('bhqk,bkhd->bqhd', weights.astype(vh.dtype), vh)

    out = lax.map(block, (qh, jnp.arange(n_blk)))
    return out.transpose(1, 0, 2, 3, 4).reshape(B, T, C)

def rwkv7_time_mix(rw_in, mu, w0, w_up, a0, a_up, g_up, k_k, k_a, r_k, gn_g, gn_b):
    B, T, _ = rw_in.shape
    H, N = RW_HEADS, HEAD_DIM
    f32 = jnp.float32
    r, k, v, wd, ad, gd = split_sizes(token_shift(rw_in, mu), RW_SPLIT)
    log_w = -jax.nn.softplus(-(w0 + jnp.tanh(wd) @ w_up).astype(f32)) - 0.5
    decay = jnp.exp(-jnp.exp(log_w))
    a = jax.nn.sigmoid((a0 + ad @ a_up).astype(f32))
    g = jax.nn.sigmoid(gd) @ g_up

    def heads(t):
        return t.astype(f32).reshape(B, T, H, N)

    kk = heads(k * k_k)
    kk = kk * lax.rsqrt(jnp.maximum(jnp.sum(kk * kk, axis=-1, keepdims=True), 1e-12))
    k_mod = k.astype(f32) * (1.0 + (a - 1.0) * k_a)
    rh, kh, vh, wh, ah = heads(r), heads(k_mod), heads(v), heads(decay), heads(a)
    a_vec = -kk
    b_vec = kk * ah

    def step(S, inp):
        r_t, w_t, k_t, v_t, a_t, b_t = inp
        sa = jnp.einsum('bhvk,bhk->bhv', S, a_t)
        S = S * w_t[:, :, None, :] + sa[..., None] * b_t[:, :, None, :] + v_t[..., None] * k_t[:, :, None, :]
        return S, jnp.einsum('bhvk,bhk->bhv', S, r_t)

    xs = tuple(t.transpose(1, 0, 2, 3) for t in (rh, wh, kh, vh, a_vec, b_vec))
    S0 = jnp.zeros((B, H, N, N), f32)
    _, y = lax.scan(step, S0, xs)
    y = y.transpose(1, 0, 2, 3)
    mean = jnp.mean(y, axis=-1, keepdims=True)
    var = jnp.mean(jnp.square(y - mean), axis=-1, keepdims=True)
    yn = (y - mean) * lax.rsqrt(var + RW_GN_EPS) * gn_g.astype(f32).reshape(H, N) + gn_b.astype(f32).reshape(H, N)
    bonus = jnp.sum(rh * kh * r_k.astype(f32).reshape(H, N), axis=-1, keepdims=True) * vh
    out = (yn + bonus).reshape(B, T, H * N) * g.astype(f32)
    return out.astype(rw_in.dtype)

def gla_linear_attention(q, k, v, gd, g, gate_up, gate_b, norm_g):
    B, T, _ = q.shape
    H, DK, DV, C = GLA_HEADS, GLA_DK, GLA_DV, CHUNK
    nc = T // C
    f32 = jnp.float32
    log_alpha = jax.nn.log_sigmoid((gd @ gate_up + gate_b).astype(f32)) / GLA_GATE_NORMALIZER

    def chunks(t, d):
        return t.astype(f32).reshape(B, nc, C, H, d).transpose(1, 0, 3, 2, 4)

    qc = chunks(q, DK) * (DK ** -0.5)
    kc, vc, lc = chunks(k, DK), chunks(v, DV), chunks(log_alpha, DK)
    causal = jnp.tril(jnp.ones((C, C), dtype=bool))

    def step(S, inp):
        q_c, k_c, v_c, la_c = inp
        b = jnp.cumsum(la_c, axis=2)
        o_inter = jnp.einsum('bhtk,bhkv->bhtv', q_c * jnp.exp(b), S)
        diff = b[:, :, :, None, :] - b[:, :, None, :, :]
        decay = jnp.exp(jnp.where(causal[:, :, None], diff, -jnp.inf))
        scores = jnp.einsum('bhtk,bhsk,bhtsk->bhts', q_c, k_c, decay)
        o_intra = jnp.einsum('bhts,bhsv->bhtv', scores, v_c)
        b_last = b[:, :, -1:, :]
        S = S * jnp.exp(b_last)[:, :, 0, :, None] + jnp.einsum('bhsk,bhsv->bhkv', k_c * jnp.exp(b_last - b), v_c)
        return S, o_inter + o_intra

    S0 = jnp.zeros((B, H, DK, DV), f32)
    _, o = lax.scan(step, S0, (qc, kc, vc, lc))
    o = o.transpose(1, 0, 3, 2, 4).reshape(B, T, H * DV)
    o = head_rmsnorm(o, norm_g, H) * jax.nn.silu(g.astype(f32))
    return o.astype(q.dtype)

def setup_inputs(seed: int = 0) -> dict:
    key = jax.random.key(seed)
    ks = jax.random.split(key, 26)
    f32 = jnp.float32
    L = DEPTH

    def nrm(k, shape, scale):
        return jax.random.normal(k, shape, f32) * scale

    def gain(k, shape):
        return 1.0 + 0.05 * jax.random.normal(k, shape, f32)

    return {
        'x': nrm(ks[0], (BATCH, SEQ, D_MODEL), 1.0),
        'pre_mix_g': gain(ks[1], (L, D_MODEL)),
        'w_in': nrm(ks[2], (L, D_MODEL, IN_WIDTH), D_MODEL ** -0.5),
        'sb_norm_g': gain(ks[3], (L, SB_WIDTH)),
        'rw_mu': jax.random.uniform(ks[4], (L, RW_IN_WIDTH), f32, 0.2, 0.8),
        'rw_w0': jax.random.uniform(ks[5], (L, RW_WIDTH), f32, -5.0, 1.0),
        'rw_w_up': nrm(ks[6], (L, RW_DECAY_RANK, RW_WIDTH), 0.5 * RW_DECAY_RANK ** -0.5),
        'rw_a0': nrm(ks[7], (L, RW_WIDTH), 0.1),
        'rw_a_up': nrm(ks[8], (L, RW_A_RANK, RW_WIDTH), 0.5 * RW_A_RANK ** -0.5),
        'rw_g_up': nrm(ks[9], (L, RW_GATE_RANK, RW_WIDTH), RW_GATE_RANK ** -0.5),
        'rw_k_k': 0.85 + 0.05 * jax.random.normal(ks[10], (L, RW_WIDTH), f32),
        'rw_k_a': gain(ks[11], (L, RW_WIDTH)),
        'rw_r_k': nrm(ks[12], (L, RW_WIDTH), 0.1),
        'rw_gn_g': gain(ks[13], (L, RW_WIDTH)),
        'rw_gn_b': nrm(ks[14], (L, RW_WIDTH), 0.01),
        'gla_gate_up': nrm(ks[15], (L, GLA_GATE_RANK, GLA_KEY_WIDTH), GLA_GATE_RANK ** -0.5),
        'gla_gate_b': nrm(ks[16], (L, GLA_KEY_WIDTH), 0.5),
        'gla_norm_g': gain(ks[17], (L, GLA_VAL_WIDTH)),
        'w_out': nrm(ks[18], (L, MIX_WIDTH, D_MODEL), MIX_WIDTH ** -0.5),
        'post_mix_g': gain(ks[19], (L, D_MODEL)),
        'pre_ffn_g': gain(ks[20], (L, D_MODEL)),
        'w_ff1': nrm(ks[21], (L, D_MODEL, D_FF), D_MODEL ** -0.5),
        'w_ff2': nrm(ks[22], (L, D_FF, D_MODEL), D_FF ** -0.5),
        'post_ffn_g': gain(ks[23], (L, D_MODEL)),
    }

def reference(x, pre_mix_g, w_in, sb_norm_g, rw_mu, rw_w0, rw_w_up, rw_a0, rw_a_up, rw_g_up,
              rw_k_k, rw_k_a, rw_r_k, rw_gn_g, rw_gn_b, gla_gate_up, gla_gate_b, gla_norm_g,
              w_out, post_mix_g, pre_ffn_g, w_ff1, w_ff2, post_ffn_g):
    for l in range(DEPTH):
        h = rmsnorm(x, pre_mix_g[l])
        proj = h @ w_in[l]
        sb_in, rw_in, gla_in = split_sizes(proj, (3 * SB_WIDTH, RW_IN_WIDTH, GLA_IN_WIDTH))
        sb_q, sb_k, sb_v = split_sizes(sb_in, (SB_WIDTH, SB_WIDTH, SB_WIDTH))
        o_sb = head_rmsnorm(stick_breaking_attention(sb_q, sb_k, sb_v), sb_norm_g[l], SB_HEADS)
        o_rw = rwkv7_time_mix(rw_in, rw_mu[l], rw_w0[l], rw_w_up[l], rw_a0[l], rw_a_up[l], rw_g_up[l],
                              rw_k_k[l], rw_k_a[l], rw_r_k[l], rw_gn_g[l], rw_gn_b[l])
        g_q, g_k, g_v, g_gd, g_g = split_sizes(gla_in, GLA_SPLIT)
        o_gla = gla_linear_attention(g_q, g_k, g_v, g_gd, g_g, gla_gate_up[l], gla_gate_b[l], gla_norm_g[l])
        mixed = jnp.concatenate([o_sb, o_rw, o_gla], axis=-1) @ w_out[l]
        x = x + rmsnorm(mixed, post_mix_g[l])
        h = rmsnorm(x, pre_ffn_g[l])
        ff = jnp.square(jax.nn.relu(h @ w_ff1[l])) @ w_ff2[l]
        x = x + rmsnorm(ff, post_ffn_g[l])
    return x


_drawn_inputs = setup_inputs


def setup_inputs(seed=0):
    import zlib

    import numpy as np

    out = dict(_drawn_inputs(seed))
    spreads = {}
    factors = {'rw_w_up': 5.736,
     'rw_a0': 3.247,
     'rw_k_k': 4.828,
     'rw_k_a': 3.16,
     'rw_gn_g': 3.516,
     'rw_gn_b': 8.0,
     'gla_norm_g': 4.149}
    for name, (base, spread) in spreads.items():
        noise = np.random.default_rng([zlib.crc32(name.encode()), seed]).standard_normal(out[name].shape)
        drawn = base * np.exp(spread * noise) if base else spread * noise
        out[name] = __import__('jax').numpy.asarray(drawn.astype(out[name].dtype))
    for name, factor in factors.items():
        out[name] = (out[name] * factor).astype(out[name].dtype)
    return out
```

```python
from contextlib import ExitStack

import concourse.bass as bass
from concourse import mybir

ALU = mybir.AluOpType
ACT = mybir.ActivationFunctionType
AX = mybir.AxisListType
F32 = mybir.dt.float32
F32R = mybir.dt.float32r
U32 = mybir.dt.uint32

P = 128
D = 1024
T = 1024
KB = D // P
TB = T // P
HALF = 512
NH = T // HALF
SBW = 384
RWW = 384
PAIRS = 3
IN_W = 3216
MIX = 1024
DFF = 4096
EPS = 1e-6
EXP_LN = "natural_log_exp_and_others"
GN_EPS = 64e-5
C = 64

SB_Q, SB_K, SB_V = 0, 384, 768
RW_R, RW_K, RW_V, RW_LOW = 1152, 1536, 1920, 2304
GLA_Q, GLA_K, GLA_V, GLA_GD, GLA_G = 2432, 2560, 2688, 2944, 2960

PARAMS = (("pre_mix_g", 8), ("sb_norm_g", 3), ("rw_w0", 3), ("rw_a0", 3), ("rw_k_k", 3), ("rw_k_a", 3),
          ("rw_r_k", 3), ("rw_gn_g", 3), ("rw_gn_b", 3), ("rw_mu", 10), ("gla_gate_b", 1), ("gla_norm_g", 2))
RW_COLS = ("w0", "a0", "k_k", "k_a", "r_k", "gn_g", "gn_b", "mu_r", "mu_k", "mu_v")


def param_columns():
    at, out = 0, {}
    for name, n in PARAMS:
        out[name] = at
        at += n
    return out, at


COL, NCOL = param_columns()


class Region:

    def __init__(self, nc, stack, tag):
        self.nc, self.stack, self.tag = nc, stack, tag
        self.semaphores, self.numbers = ExitStack(), []
        stack.callback(self.clear)

    def sb(self, name, shape, dt=F32):
        return self.stack.enter_context(self.nc.sbuf_tensor(f"{self.tag}_{name}", shape, dt))

    def bank(self, name, cols=HALF):
        return self.stack.enter_context(self.nc.psum_tensor(f"{self.tag}_ps_{name}", [P, cols], F32))

    def sem(self, name):
        got = self.semaphores.enter_context(self.nc.semaphore(f"{self.tag}_{name}"))
        self.numbers.append(got.num)
        return got

    def clear(self):
        if self.numbers:
            runs = []
            for n in sorted(self.numbers):
                if runs and runs[-1].stop == n:
                    runs[-1] = range(runs[-1].start, n + 1)
                else:
                    runs.append(range(n, n + 1))
            with self.nc.Block() as block:
                @block.sync
                def _(sp):
                    for run in runs:
                        sp.sem_clear(run)
        self.semaphores.close()


MASKS = ("ones", "above", "from_diag", "below", "to_diag", "same16", "same32", "same64",
         "up16", "up64", "upd64", "low16", "low32", "low64")


def constants(nc, con, args):
    ident, masks = con["ident"], con["masks"]
    m = {name: masks[:, n, :] for n, name in enumerate(MASKS)}
    levels = con["levels"]
    with ExitStack() as st:
        r = Region(nc, st, "con")
        rows = r.sb("rows", [P, P])
        same = [r.sb(f"same{n}", [P, P]) for n in range(2)]
        colp = r.bank("colp")
        loaded, zeroed, filled = r.sem("loaded"), r.sem("zeroed"), r.sem("filled")
        turned, made, cut = r.sem("turned"), r.sem("made"), r.sem("cut")
        block = st.enter_context(nc.Block())

        @block.sync
        def _(sp):
            sp.wait_ge(zeroed, 2)
            for name, n in PARAMS:
                at = COL[name]
                sp.dma_start(rows[at:at + n, :],
                             args[name].rearrange("l (n p) -> (l n) p", p=P)).then_inc(loaded, 16)

        @block.gpsimd
        def _(pool):
            pool.memset(ident[:], 0.0).then_inc(zeroed, 1)
            pool.memset(rows[:], 0.0).then_inc(zeroed, 1)
            pool.wait_ge(zeroed, 2)
            pool.affine_select(out=ident[:], in_=ident[:], compare_op=ALU.not_equal, fill=1.0, base=0,
                               pattern=[[-1, P]], channel_multiplier=1).then_inc(filled, 1)
            pool.memset(m["ones"], 1.0).then_inc(made, 1)
            done = [1]

            def select(out, in_, compare, base, pattern, step):
                pool.wait_ge(made, done[0])
                pool.affine_select(out=out, in_=in_, compare_op=compare, fill=0.0, base=base,
                                   pattern=pattern, channel_multiplier=step).then_inc(made, 1)
                done[0] += 1

            select(m["above"], m["ones"], ALU.is_gt, 0, [[1, P]], -1)
            select(m["from_diag"], m["ones"], ALU.is_ge, 0, [[1, P]], -1)
            select(m["below"], m["ones"], ALU.is_gt, 0, [[-1, P]], 1)
            select(m["to_diag"], m["ones"], ALU.is_ge, 0, [[-1, P]], 1)

            def blocks(out, size):
                n = P // size
                o = out.rearrange("p (n s) -> p n s", s=size)
                select(o, m["ones"].rearrange("p (n s) -> p n s", s=size), ALU.is_ge, 0, [[-size, n], [0, size]], 1)
                select(o, o, ALU.is_ge, size - 1, [[size, n], [0, size]], -1)

            for size in (16, 32, 64):
                blocks(m[f"same{size}"], size)
            for n in range(6):
                if n >= 1:
                    pool.wait_ge(cut, 2 * n)
                blocks(same[n % 2][:], 2 << n)

        @block.tensor
        def _(pe):
            pe.wait_ge(loaded, 16 * len(PARAMS))
            pe.wait_ge(filled, 1)
            pe.transpose(colp[:, 0:P], rows[:], ident[:]).then_inc(turned, 1)

        @block.vector
        def _(dve):
            SELECTS = 5 + 6
            for n in range(6):
                dve.wait_ge(made, SELECTS + 2 * (n + 1))
                before = ident[:] if n == 0 else same[(n - 1) % 2][:]
                dve.tensor_tensor(levels[:, n, :], same[n % 2][:], before, ALU.subtract).then_inc(cut, 1)
                dve.wait_ge(cut, 2 * n + 1)
                dve.tensor_tensor(levels[:, n, :], levels[:, n, :], m["above"], ALU.mult).then_inc(cut, 1)
            done = 12
            for name, a, b, op in (("up16", "same16", "above", ALU.mult), ("up64", "same64", "above", ALU.mult),
                                   ("upd64", "same64", "from_diag", ALU.mult),
                                   ("low16", "same16", "below", ALU.mult),
                                   ("low64", "same64", "same32", ALU.subtract),
                                   ("low32", "same32", "same16", ALU.subtract),
                                   ("low64", "low64", "below", ALU.mult),
                                   ("low32", "low32", "below", ALU.mult)):
                dve.wait_ge(cut, done)
                dve.tensor_tensor(m[name], m[a], m[b], op).then_inc(cut, 1)
                done += 1
            dve.wait_ge(turned, 1)
            dve.tensor_copy(con["col"][:], colp[:, 0:P]).then_inc(cut, 1)


def projection(nc, con, x, w_in, proj):
    ident, col = con["ident"], con["col"]
    PAIRED = IN_W // (2 * P)
    REST = IN_W - PAIRED * 2 * P
    NARROW = REST - P
    with ExitStack() as st:
        r = Region(nc, st, "prj")
        xt = r.sb("xt", [P, TB, D])
        sq = r.sb("sq", [P, D])
        ss, rs = r.sb("ss", [P, TB]), r.sb("rs", [P, TB])
        hH, hL = r.sb("hH", [P, KB, T], F32R), r.sb("hL", [P, KB, T], F32R)
        raw = [r.sb(f"raw{s}", [P, KB, P]) for s in range(2)]
        wH = [r.sb(f"wH{s}", [P, KB, P], F32R) for s in range(2)]
        wL = [r.sb(f"wL{s}", [P, KB, P], F32R) for s in range(2)]
        stage = [r.sb(f"stage{s}", [P, T]) for s in range(2)]
        tbank = [r.bank(f"tb{i}") for i in range(4)]
        bank = [[r.bank(f"b{s}{h}") for h in range(NH)] for s in range(2)]
        x_in = [r.sem(f"x_in{j}") for j in range(TB)]
        squared, rooted, scaled = r.sem("squared"), r.sem("rooted"), r.sem("scaled")
        rdone = r.sem("rdone")
        turned, high, low = r.sem("turned"), r.sem("high"), r.sem("low")
        w_in_s = [r.sem(f"w_in{s}") for s in range(2)]
        w_high, w_low = [r.sem(f"w_high{s}") for s in range(2)], [r.sem(f"w_low{s}") for s in range(2)]
        multiplied = [r.sem(f"mul{s}") for s in range(2)]
        ev0, ev1 = [r.sem(f"ev0_{s}") for s in range(2)], [r.sem(f"ev1_{s}") for s in range(2)]
        stored = [r.sem(f"stored{s}") for s in range(2)]
        x_d = x.rearrange("b (j p) d -> (b j) p d", p=P)
        w_d = w_in.rearrange("l (k p) n -> p (l k) n", p=P)
        block = st.enter_context(nc.Block())

        @block.sync
        def _(sp):
            for j in range(TB):
                sp.dma_start(xt[:, j, :], x_d[j]).then_inc(x_in[j], 16)
            for s in range(2):
                sp.sem_inc(stored[s], 16)
                sp.dma_start(raw[s][:], w_d[:, :, s * P:(s + 1) * P]).then_inc(w_in_s[s], 16)
            def load(s, i, at, n):
                sp.wait_ge(w_high[s], i + 1)
                sp.wait_ge(w_low[s], i + 1)
                sp.dma_start(raw[s][:, :, 0:n], w_d[:, :, bass.ds(at, n)]).then_inc(w_in_s[s], 16)

            def store(s, i, at, n):
                sp.wait_ge(ev0[s], i + 2)
                sp.wait_ge(ev1[s], i + 2)
                sp.dma_start(proj[bass.ds(at, n), :], stage[s][0:n, :]).then_inc(stored[s], 16)

            with sp.Fori(0, PAIRED - 1) as i:
                for s in range(2):
                    load(s, i + 1, (i + 1) * 2 * P + s * P, P)
                for s in range(2):
                    store(s, i, i * 2 * P + s * P, P)
            for s, n in ((0, P), (1, NARROW)):
                load(s, PAIRED, PAIRED * 2 * P + s * P, n)
            for s in range(2):
                store(s, PAIRED - 1, (PAIRED - 1) * 2 * P + s * P, P)
            for s, n in ((0, P), (1, NARROW)):
                store(s, PAIRED, PAIRED * 2 * P + s * P, n)
            for s in range(2):
                sp.wait_ge(stored[s], 16 * (PAIRED + 2))

        @block.scalar
        def _(act):
            for s in range(2):
                act.sem_inc(w_high[s], 1)
                act.sem_inc(ev0[s], 1)
            for j in range(TB):
                act.wait_ge(x_in[j], 16)
                if j:
                    act.wait_ge(squared, j)
                act.activation(sq[:], xt[:, j, :], ACT.Square, accum_out=ss[:, j:j + 1]).then_inc(squared, 1)
            act.wait_ge(rdone, 1)
            act.activation(rs[:], rs[:], ACT.Sqrt).then_inc(rooted, 1)
            for g in range(KB * NH):
                kb, h = g // NH, g % NH
                act.wait_ge(turned, g + 1)
                act.activation(hH[:, kb, h * HALF:(h + 1) * HALF], tbank[g % 4][:], ACT.Copy,
                               scale=col[:, COL["pre_mix_g"] + kb:COL["pre_mix_g"] + kb + 1]).then_inc(high, 1)

            def block_work(s, i, n):
                act.wait_ge(w_in_s[s], i * 16 + 16)
                act.wait_ge(multiplied[s], i + 1)
                act.copy(wH[s][:, :, 0:n], raw[s][:, :, 0:n]).then_inc(w_high[s], 1)

            def take(s, i, n):
                act.wait_ge(multiplied[s], i + 2)
                act.wait_ge(stored[s], i * 16 + 16)
                act.copy(stage[s][0:n, 0:HALF], bank[s][0][0:n, :]).then_inc(ev0[s], 1)

            block_work(0, 0, P)
            block_work(1, 0, P)
            with act.Fori(0, PAIRED - 1) as i:
                for s in range(2):
                    take(s, i, P)
                    block_work(s, i + 1, P)
            for s, n in ((0, P), (1, NARROW)):
                take(s, PAIRED - 1, P)
                block_work(s, PAIRED, n)
            for s, n in ((0, P), (1, NARROW)):
                take(s, PAIRED, n)

        @block.vector
        def _(dve):
            for s in range(2):
                dve.sem_inc(w_low[s], 1)
                dve.sem_inc(ev1[s], 1)
            dve.wait_ge(squared, TB)
            dve.tensor_scalar(rs[:], ss[:], 1.0 / D, EPS, ALU.mult, ALU.add).then_inc(rdone, 1)
            dve.wait_ge(rooted, 1)
            dve.reciprocal(rs[:], rs[:]).then_inc(rdone, 1)
            dve.wait_ge(rdone, 2)
            for j in range(TB):
                dve.tensor_scalar(xt[:, j, :], xt[:, j, :], rs[:, j:j + 1], None, ALU.mult).then_inc(scaled, 1)
            for g in range(KB * NH):
                kb, h = g // NH, g % NH
                dve.wait_ge(high, g + 1)
                hs = slice(h * HALF, (h + 1) * HALF)
                dve.scalar_tensor_tensor(hL[:, kb, hs], tbank[g % 4][:],
                                         col[:, COL["pre_mix_g"] + kb:COL["pre_mix_g"] + kb + 1],
                                         hH[:, kb, hs].bitcast(F32), ALU.mult, ALU.subtract).then_inc(low, 1)

            def split_low(s, i, n):
                dve.wait_ge(w_high[s], i + 2)
                dve.wait_ge(multiplied[s], i + 1)
                dve.tensor_tensor(wL[s][:, :, 0:n], raw[s][:, :, 0:n], wH[s][:, :, 0:n].bitcast(F32),
                                  ALU.subtract).then_inc(w_low[s], 1)

            def take(s, i, n):
                dve.wait_ge(multiplied[s], i + 2)
                dve.wait_ge(stored[s], i * 16 + 16)
                dve.tensor_copy(stage[s][0:n, HALF:T], bank[s][1][0:n, :]).then_inc(ev1[s], 1)

            split_low(0, 0, P)
            split_low(1, 0, P)
            with dve.Fori(0, PAIRED - 1) as i:
                for s in range(2):
                    take(s, i, P)
                    split_low(s, i + 1, P)
            for s, n in ((0, P), (1, NARROW)):
                take(s, PAIRED - 1, P)
                split_low(s, PAIRED, n)
            for s, n in ((0, P), (1, NARROW)):
                take(s, PAIRED, n)

        @block.tensor
        def _(pe):
            for s in range(2):
                pe.sem_inc(multiplied[s], 1)
            pe.wait_ge(scaled, TB)
            for g in range(KB * NH):
                kb, h = g // NH, g % NH
                if g >= 4:
                    pe.wait_ge(low, g - 3)
                for q in range(4):
                    j = h * 4 + q
                    m = pe.transpose(tbank[g % 4][:, q * P:(q + 1) * P], xt[:, j, kb * P:(kb + 1) * P], ident[:])
                m.then_inc(turned, 1)
            pe.wait_ge(low, KB * NH)

            def products(s, i, n):
                pe.wait_ge(w_low[s], i + 2)
                pe.wait_ge(ev0[s], i + 1)
                pe.wait_ge(ev1[s], i + 1)
                for h in range(NH):
                    hs = slice(h * HALF, (h + 1) * HALF)
                    for kb in range(KB):
                        for q, (w, a) in enumerate(((wL, hH), (wH, hL), (wH, hH))):
                            m = pe.matmul(bank[s][h][0:n, :] if n == P else bank[s][h][:, :],
                                          w[s][:, kb, 0:P], a[:, kb, hs],
                                          start=(kb == 0 and q == 0), stop=(kb == KB - 1 and q == 2))
                m.then_inc(multiplied[s], 1)

            with pe.Fori(0, PAIRED) as i:
                for s in range(2):
                    products(s, i, P)
            products(0, PAIRED, P)
            products(1, PAIRED, NARROW)


def broadcast_rows(ap, n=P):
    return ap.to_broadcast((n, ap.shape[1]))


def output_projection(nc, con, x, mixed, w_out, post_g, pre_g, x1, hH, hL):
    ident = con["ident"]
    with ExitStack() as st:
        r = Region(nc, st, "out")
        raw = [r.sb(f"raw{s}", [P, D]) for s in range(4)]
        mH, mL = r.sb("mH", [P, KB, T], F32R), r.sb("mL", [P, KB, T], F32R)
        wH, wL = r.sb("wH", [P, KB, D // 2], F32R), r.sb("wL", [P, KB, D // 2], F32R)
        half0 = r.sb("half0", [P, TB, HALF])
        y, xt = raw[0:2], raw[2:4]
        postB, preB = r.sb("postB", [P, D]), r.sb("preB", [P, D])
        ss = r.sb("ss", [P, TB, 4])
        bank = [r.bank(f"b{i}") for i in range(4)]
        tbank = [r.bank(f"tb{i}") for i in range(4)]
        raw_in = [r.sem(f"raw_in{s}") for s in range(4)]
        gains = r.sem("gains")
        x_in = [r.sem(f"x_in{s}") for s in range(2)]
        high, low = r.sem("high"), r.sem("low")
        multiplied, kept, squared = r.sem("multiplied"), r.sem("kept"), r.sem("squared")
        mean, root, inv = r.sem("mean"), r.sem("root"), r.sem("inv")
        added, squared1 = r.sem("added"), r.sem("squared1")
        normed, turned, hhigh, hlow, stored = (r.sem("normed"), r.sem("turned"), r.sem("hhigh"),
                                               r.sem("hlow"), r.sem("stored"))
        x_d = x.rearrange("b (j p) d -> (b j) p d", p=P)
        x1_d = x1.rearrange("(j p) d -> j p d", p=P)
        m_d = mixed.rearrange("(k p) t -> k p t", p=P)
        w_d = w_out.rearrange("l (k p) n -> (l k) p n", p=P)
        pieces = [("m", k) for k in range(KB)] + [("w0", k) for k in range(KB)] + [("w1", k) for k in range(KB)]
        block = st.enter_context(nc.Block())

        def piece(n):
            kind, k = pieces[n]
            width = T if kind == "m" else HALF
            src = raw[n % 4][:, 0:width]
            if kind == "m":
                return src, mH[:, k, :], mL[:, k, :]
            return src, wH[:, k, :], wL[:, k, :]

        @block.sync
        def _(sp):
            for n, (kind, k) in enumerate(pieces):
                if n >= 4:
                    sp.wait_ge(low, n - 3)
                if kind == "m":
                    sp.dma_start(raw[n % 4][:], m_d[k]).then_inc(raw_in[n % 4], 16)
                else:
                    c = int(kind[1]) * HALF
                    sp.dma_start(raw[n % 4][:, 0:HALF], w_d[k][:, c:c + HALF]).then_inc(raw_in[n % 4], 16)
                if n == 3:
                    sp.dma_start(postB[:], broadcast_rows(post_g)).then_inc(gains, 16)
                    sp.dma_start(preB[:], broadcast_rows(pre_g)).then_inc(gains, 16)
            sp.wait_ge(low, len(pieces))
            for j in range(TB):
                if j >= 2:
                    sp.wait_ge(normed, j - 1)
                    sp.wait_ge(stored, 16 * (j - 1))
                sp.dma_start(xt[j % 2][:], x_d[j]).then_inc(x_in[j % 2], 16)
                if j:
                    sp.wait_ge(added, j)
                    sp.dma_start(x1_d[j - 1], xt[(j - 1) % 2][:]).then_inc(stored, 16)
            sp.wait_ge(added, TB)
            sp.dma_start(x1_d[TB - 1], xt[(TB - 1) % 2][:]).then_inc(stored, 16)
            sp.wait_ge(stored, 16 * TB)

        @block.scalar
        def _(act):
            for n in range(len(pieces)):
                act.wait_ge(raw_in[n % 4], 16 * (n // 4 + 1))
                if n == 2 * KB:
                    act.wait_ge(multiplied, TB)
                src, dst, _ = piece(n)
                act.copy(dst, src).then_inc(high, 1)
            for j in range(TB):
                ys = y[j % 2]
                act.wait_ge(kept, j + 1)
                if j == 0:
                    act.wait_ge(low, len(pieces))
                act.activation(ys[:, 0:HALF], half0[:, j, :], ACT.Square,
                               accum_out=ss[:, j, 0:1]).then_inc(squared, 1)
                act.wait_ge(multiplied, TB + j + 1)
                act.activation(ys[:, HALF:D], bank[j % 4][:], ACT.Square,
                               accum_out=ss[:, j, 1:2]).then_inc(squared, 1)
                act.wait_ge(mean, 2 * j + 1)
                act.activation(ss[:, j, 0:1], ss[:, j, 0:1], ACT.Sqrt).then_inc(root, 1)
                act.wait_ge(added, j + 1)
                act.activation(ys[:], xt[j % 2][:], ACT.Square, accum_out=ss[:, j, 2:3]).then_inc(squared1, 1)
                act.wait_ge(mean, 2 * j + 2)
                act.activation(ss[:, j, 2:3], ss[:, j, 2:3], ACT.Sqrt).then_inc(root, 1)
                for b in range(2):
                    act.wait_ge(turned, 2 * j + b + 1)
                    act.copy(hH[:, 4 * b:4 * b + 4, j * P:(j + 1) * P],
                             tbank[(2 * j + b) % 4][:].rearrange("p (k t) -> p k t", k=4)).then_inc(hhigh, 1)

        @block.vector
        def _(dve):
            for n in range(2 * KB):
                dve.wait_ge(high, n + 1)
                src, h, l = piece(n)
                dve.tensor_tensor(l, src, h.bitcast(F32), ALU.subtract).then_inc(low, 1)
            for j in range(TB):
                dve.wait_ge(multiplied, j + 1)
                dve.tensor_copy(half0[:, j, :], bank[j % 4][:]).then_inc(kept, 1)
            for n in range(2 * KB, 3 * KB):
                dve.wait_ge(high, n + 1)
                src, h, l = piece(n)
                dve.tensor_tensor(l, src, h.bitcast(F32), ALU.subtract).then_inc(low, 1)
            dve.wait_ge(gains, 32)
            done = 0
            for j in range(TB):
                ys, xs = y[j % 2], xt[j % 2]
                s0, s1, s2 = ss[:, j, 0:1], ss[:, j, 1:2], ss[:, j, 2:3]

                dve.wait_ge(squared, 2 * j + 2)
                dve.tensor_tensor(s0, s0, s1, ALU.add).then_inc(inv, 1)
                dve.wait_ge(inv, done + 1)
                dve.tensor_scalar(s0, s0, 1.0 / D, EPS, ALU.mult, ALU.add).then_inc(mean, 1)
                dve.wait_ge(root, 2 * j + 1)
                dve.reciprocal(s0, s0).then_inc(inv, 1)
                dve.wait_ge(inv, done + 2)
                dve.scalar_tensor_tensor(ys[:, 0:HALF], half0[:, j, :], s0, postB[:, 0:HALF],
                                         ALU.mult, ALU.mult).then_inc(inv, 1)
                dve.scalar_tensor_tensor(ys[:, HALF:D], bank[j % 4][:], s0, postB[:, HALF:D],
                                         ALU.mult, ALU.mult).then_inc(inv, 1)
                dve.wait_ge(inv, done + 4)
                dve.wait_ge(x_in[j % 2], 16 * (j // 2 + 1))
                dve.tensor_tensor(xs[:], xs[:], ys[:], ALU.add).then_inc(added, 1)
                dve.wait_ge(squared1, j + 1)
                dve.tensor_scalar(s2, s2, 1.0 / D, EPS, ALU.mult, ALU.add).then_inc(mean, 1)
                dve.wait_ge(root, 2 * j + 2)
                dve.reciprocal(s2, s2).then_inc(inv, 1)
                dve.wait_ge(inv, done + 5)
                done += 5
                dve.scalar_tensor_tensor(ys[:], xs[:], s2, preB[:], ALU.mult, ALU.mult).then_inc(normed, 1)
                for b in range(2):
                    dve.wait_ge(hhigh, 2 * j + b + 1)
                    dst = slice(4 * b, 4 * b + 4)
                    dve.tensor_tensor(hL[:, dst, j * P:(j + 1) * P],
                                      tbank[(2 * j + b) % 4][:].rearrange("p (k t) -> p k t", k=4),
                                      hH[:, dst, j * P:(j + 1) * P].bitcast(F32), ALU.subtract).then_inc(hlow, 1)

        @block.tensor
        def _(pe):
            def product(half, j):
                n = half * TB + j
                b = bank[j % 4]
                if half == 0 and j >= 4:
                    pe.wait_ge(kept, j - 3)
                if half == 1 and j >= 4:
                    pe.wait_ge(normed, j - 3)
                if half == 1 and j == 0:
                    pe.wait_ge(kept, TB)
                for k in range(KB):
                    if j == 0:
                        pe.wait_ge(low, (half + 1) * KB + k + 1)
                    for q, (m, w) in enumerate(((mL, wH), (mH, wL), (mH, wH))):
                        i = pe.matmul(b[:], m[:, k, j * P:(j + 1) * P], w[:, k, :],
                                      start=(k == 0 and q == 0), stop=(k == KB - 1 and q == 2))
                i.then_inc(multiplied, 1)

            def turn(j):
                pe.wait_ge(normed, j + 1)
                for b in range(2):
                    n = 2 * j + b
                    if n >= 4:
                        pe.wait_ge(hlow, n - 3)
                    for k in range(4):
                        kb = 4 * b + k
                        i = pe.transpose(tbank[n % 4][:, k * P:(k + 1) * P],
                                         y[j % 2][:, kb * P:(kb + 1) * P], ident[:])
                    i.then_inc(turned, 1)

            for j in range(TB):
                product(0, j)
            for j in range(TB):
                product(1, j)
                if j >= 1:
                    turn(j - 1)
            turn(TB - 1)


def feed_forward(nc, con, x1, w1, w2, post_g, hH, hL, out):
    FB = 4
    NE = DFF // (FB * P)
    with ExitStack() as st:
        r = Region(nc, st, "ffn")
        raw1 = [r.sb(f"raw1_{s}", [P, KB, P]) for s in range(2)]
        w1H = [r.sb(f"w1H{s}", [P, KB, P], F32R) for s in range(2)]
        w1L = [r.sb(f"w1L{s}", [P, KB, P], F32R) for s in range(2)]
        raw2 = [r.sb(f"raw2_{s}", [P, D]) for s in range(2)]
        w2H, w2L = r.sb("w2H", [P, FB, D], F32R), r.sb("w2L", [P, FB, D], F32R)
        gH, gL = r.sb("gH", [P, FB, T], F32R), r.sb("gL", [P, FB, T], F32R)
        relu, g32 = r.sb("relu", [P, HALF]), r.sb("g32", [P, HALF])
        acc = r.sb("acc", [P, TB, D])
        postB = r.sb("postB", [P, D])
        ss = r.sb("ss", [P, TB])
        bank = [[r.bank(f"b{s}{h}") for h in range(NH)] for s in range(2)]
        ybank = [r.bank(f"y{i}") for i in range(4)]
        xt = [raw1[s][:].rearrange("p k c -> p (k c)") for s in range(2)]
        w1_in = [r.sem(f"w1_in{s}") for s in range(2)]
        w2_in = [r.sem(f"w2_in{s}") for s in range(2)]
        w1_high, w1_low = [r.sem(f"w1_high{s}") for s in range(2)], [r.sem(f"w1_low{s}") for s in range(2)]
        w2_high, w2_low = r.sem("w2_high"), r.sem("w2_low")
        hidden = [r.sem(f"hidden{s}") for s in range(2)]
        rectified, squared, g_high, g_low = r.sem("rectified"), r.sem("squared"), r.sem("g_high"), r.sem("g_low")
        summed, added, cleared, used = r.sem("summed"), r.sem("added"), r.sem("cleared"), r.sem("used")
        gains, x_in = r.sem("gains"), [r.sem(f"x_in{s}") for s in range(2)]
        ysq, mean, root, inv, final = r.sem("ysq"), r.sem("mean"), r.sem("root"), r.sem("inv"), r.sem("final")
        stored = r.sem("stored")
        w1_d = w1.rearrange("l (k p) n -> p (l k) n", p=P)
        w2_d = w2.rearrange("l (f p) n -> (l f) p n", p=P)
        x1_d = x1.rearrange("(j p) d -> j p d", p=P)
        o_d = out.rearrange("b (j p) d -> (b j) p d", p=P)
        w2_flat = w2.rearrange("l f n -> (l f) n")
        block = st.enter_context(nc.Block())
        G = TB * 2

        @block.sync
        def _(sp):
            sp.dma_start(postB[:], broadcast_rows(post_g)).then_inc(gains, 16)

            def load1(s, use, at):
                sp.wait_ge(w1_high[s], use + 1)
                sp.wait_ge(w1_low[s], use + 1)
                sp.dma_start(raw1[s][:], w1_d[:, :, bass.ds(at, P)]).then_inc(w1_in[s], 16)

            def load2(s, use, total, at):
                sp.wait_ge(w2_low, total)
                sp.dma_start(raw2[s][:], w2_flat[bass.ds(at, P), :]).then_inc(w2_in[s], 16)

            for s in range(2):
                load1(s, 0, s * P)

            def slice_loads(e, last):
                for i in range(FB):
                    load2(i % 2, e * 2 + i // 2, e * FB + i + 1, e * (FB * P) + i * P)
                    if i < 2:
                        load1(i, e * 2 + 1, e * (FB * P) + (i + 2) * P)
                    elif not last:
                        load1(i - 2, e * 2 + 2, e * (FB * P) + (i + 2) * P)

            with sp.Fori(0, NE - 1) as e:
                slice_loads(e, False)
            slice_loads(NE - 1, True)
            for j in range(TB):
                if j < 2:
                    sp.wait_ge(w1_high[j], 2 * NE + 1)
                    sp.wait_ge(w1_low[j], 2 * NE + 1)
                else:
                    sp.wait_ge(final, j - 1)
                sp.dma_start(xt[j % 2], x1_d[j]).then_inc(x_in[j % 2], 16)
                if j:
                    sp.wait_ge(final, j)
                    sp.dma_start(o_d[j - 1], acc[:, j - 1, :]).then_inc(stored, 16)
            sp.wait_ge(final, TB)
            sp.dma_start(o_d[TB - 1], acc[:, TB - 1, :]).then_inc(stored, 16)
            sp.wait_ge(stored, 16 * TB)

        W2_AT = {0: (0, 1), 1: (2,), 2: (3,), 3: ()}

        @block.scalar
        def _(act):
            for s in range(2):
                act.sem_inc(w1_high[s], 1)

            def split1(s, use):
                act.wait_ge(w1_in[s], use * 16 + 16)
                act.wait_ge(hidden[s], use + 1)
                act.copy(w1H[s][:], raw1[s][:]).then_inc(w1_high[s], 1)

            def split2(i, e):
                act.wait_ge(w2_in[i % 2], (e * 2 + i // 2) * 16 + 16)
                if i == 0:
                    act.wait_ge(used, e + 1)
                act.copy(w2H[:, i, :], raw2[i % 2][:]).then_inc(w2_high, 1)

            for s in range(2):
                split1(s, 0)

            def slice_work(e, last):
                for i in range(FB):
                    for m in W2_AT[i]:
                        split2(m, e)
                    act.wait_ge(hidden[i % 2], e * 2 + i // 2 + 2)
                    for h in range(NH):
                        n = e * (2 * FB) + 2 * i + h
                        act.activation(relu[:], bank[i % 2][h][:], ACT.Relu).then_inc(rectified, 1)
                        act.wait_ge(rectified, n + 1)
                        act.wait_ge(g_low, n + 1)
                        act.activation(g32[:], relu[:], ACT.Square).then_inc(squared, 1)
                        act.wait_ge(squared, n + 1)
                    if i < 2:
                        split1(i, e * 2 + 1)
                    elif not last:
                        split1(i - 2, e * 2 + 2)

            with act.Fori(0, NE - 1) as e:
                slice_work(e, False)
            slice_work(NE - 1, True)
            for j in range(TB):
                act.wait_ge(added, G * (NE - 1) + 2 * (j + 1) + 1)
                if j:
                    act.wait_ge(ysq, j)
                act.activation(raw2[0][:], acc[:, j, :], ACT.Square,
                               accum_out=ss[:, j:j + 1]).then_inc(ysq, 1)
                act.wait_ge(mean, j + 1)
                act.activation(ss[:, j:j + 1], ss[:, j:j + 1], ACT.Sqrt).then_inc(root, 1)

        @block.gpsimd
        def _(pool):
            pool.memset(acc[:], 0.0).then_inc(cleared, 1)

        @block.vector
        def _(dve):
            for s in range(2):
                dve.sem_inc(w1_low[s], 1)
            dve.sem_inc(w2_low, 2)
            dve.sem_inc(g_low, 1)
            dve.sem_inc(added, 1)
            dve.wait_ge(cleared, 1)

            def split1(s, use):
                dve.wait_ge(w1_high[s], use + 2)
                dve.wait_ge(hidden[s], use + 1)
                dve.tensor_tensor(w1L[s][:], raw1[s][:], w1H[s][:].bitcast(F32), ALU.subtract).then_inc(w1_low[s], 1)

            def split2(i, e):
                dve.wait_ge(w2_high, e * FB + i + 1)
                dve.tensor_tensor(w2L[:, i, :], raw2[i % 2][:], w2H[:, i, :].bitcast(F32),
                                  ALU.subtract).then_inc(w2_low, 1)

            for s in range(2):
                split1(s, 0)

            def slice_work(e, last):
                for i in range(FB):
                    for m in W2_AT[i]:
                        split2(m, e)
                    for h in range(NH):
                        n = e * (2 * FB) + 2 * i + h
                        hs = slice(h * HALF, (h + 1) * HALF)
                        dve.wait_ge(squared, n + 1)
                        dve.tensor_copy(gH[:, i, hs], g32[:]).then_inc(g_high, 1)
                        dve.wait_ge(g_high, n + 1)
                        dve.tensor_tensor(gL[:, i, hs], g32[:], gH[:, i, hs].bitcast(F32),
                                          ALU.subtract).then_inc(g_low, 1)
                    if i < 2:
                        split1(i, e * 2 + 1)
                    elif not last:
                        split1(i - 2, e * 2 + 2)
                for g in range(G):
                    j, dh = g // 2, g % 2
                    ds = slice(dh * HALF, (dh + 1) * HALF)
                    dve.wait_ge(summed, e * G + g + 1)
                    dve.tensor_tensor(acc[:, j, ds], acc[:, j, ds], ybank[g % 4][:], ALU.add).then_inc(added, 1)
                    if last and dh == 1 and j >= 1:
                        finish(j - 1)
                if last:
                    finish(TB - 1)

            def finish(j):
                s0 = ss[:, j:j + 1]
                if j == 0:
                    dve.wait_ge(gains, 16)
                dve.wait_ge(ysq, j + 1)
                dve.tensor_scalar(s0, s0, 1.0 / D, EPS, ALU.mult, ALU.add).then_inc(mean, 1)
                dve.wait_ge(root, j + 1)
                dve.reciprocal(s0, s0).then_inc(inv, 1)
                dve.wait_ge(inv, 2 * j + 1)
                dve.scalar_tensor_tensor(acc[:, j, :], acc[:, j, :], s0, postB[:], ALU.mult, ALU.mult).then_inc(inv, 1)
                dve.wait_ge(inv, 2 * j + 2)
                dve.wait_ge(x_in[j % 2], 16 * (j // 2 + 1))
                dve.tensor_tensor(acc[:, j, :], acc[:, j, :], xt[j % 2], ALU.add).then_inc(final, 1)

            with dve.Fori(0, NE - 1) as e:
                slice_work(e, False)
            slice_work(NE - 1, True)

        @block.tensor
        def _(pe):
            for s in range(2):
                pe.sem_inc(hidden[s], 1)
            pe.sem_inc(used, 1)

            def slice_products(e):
                for i in range(FB):
                    s = i % 2
                    pe.wait_ge(w1_low[s], e * 2 + i // 2 + 2)
                    if i >= 2:
                        pe.wait_ge(rectified, e * (2 * FB) + 2 * (i - 1))
                    for h in range(NH):
                        hs = slice(h * HALF, (h + 1) * HALF)
                        for k in range(KB):
                            for q, (w, a) in enumerate(((w1L, hH), (w1H, hL), (w1H, hH))):
                                m = pe.matmul(bank[s][h][:], w[s][:, k, :], a[:, k, hs],
                                              start=(k == 0 and q == 0), stop=(k == KB - 1 and q == 2))
                    m.then_inc(hidden[s], 1)
                for g in range(G):
                    j, dh = g // 2, g % 2
                    ts, ds = slice(j * P, (j + 1) * P), slice(dh * HALF, (dh + 1) * HALF)
                    pe.wait_ge(added, e * G + g - 2 if g >= 4 else e * G + 1)
                    for i in range(FB):
                        if g < 2:
                            pe.wait_ge(g_low, e * (2 * FB) + 2 * i + 3)
                            pe.wait_ge(w2_low, e * FB + i + 3)
                        for q, (a, w) in enumerate(((gL, w2H), (gH, w2L), (gH, w2H))):
                            m = pe.matmul(ybank[g % 4][:], a[:, i, ts], w[:, i, ds],
                                          start=(i == 0 and q == 0), stop=(i == FB - 1 and q == 2))
                    m.then_inc(summed, 1)
                pe.wait_ge(summed, e * G + G)
                pe.sem_inc(used, 1)

            with pe.Fori(0, NE) as e:
                slice_products(e)


def rwkv(nc, con, args, proj, mixed):
    ident, col = con["ident"], con["col"]
    mask = {name: con["masks"][:, n, :] for n, name in enumerate(MASKS)}
    NG = 4
    NC = T // C
    NT = TB // 2
    DECAY = 0.6065306597126334
    NPC = len(RW_COLS)
    with ExitStack() as st:
        r = Region(nc, st, "rw")
        raw = {n: r.sb(f"raw_{n}", [P, T + 1]) for n in "rkv"}
        low_raw, low = r.sb("low_raw", [P, T + 1]), r.sb("low", [P, T])
        up, start = r.sb("up", [P, P]), r.sb("start", [P, T])
        pc, rest = r.sb("pc", [P, NPC]), r.sb("rest", [P, 4])
        b = [r.sb(f"b{n}", [P, T]) for n in range(11)]
        nat = {n: r.sb(f"nat_{n}", [P, TB, P]) for n in "abkv"}
        state = r.sb("state", [P, NC + 1, C])
        small = r.sb("small", [P, 4, 2 * TB])
        sets = [{n: r.sb(f"{n}{g}", [P, NT, P]) for n in
                 ("s0", "s1", "s2", "s3", "lo32", "lo64", "ak", "rb", "rk", "R", "gu")} for g in range(NG)]
        banks = [r.bank(f"b{n}") for n in range(8)]
        rs_, ks_, vs_ = b[0], b[1], b[2]
        QT = raw["r"][:, 0:T].rearrange("p (j t) -> p j t", t=P)
        MT = raw["k"][:, 0:T].rearrange("p (c k) -> p c k", k=C)
        KW = raw["v"][:, 0:T].rearrange("p (c v) -> p c v", v=C)
        Y = b[3][:].rearrange("p (j f) -> p j f", f=P)
        sems = {}

        def s(name):
            if name not in sems:
                sems[name] = r.sem(name)
            return sems[name]

        low_in, low_cut = s("low_in"), s("low_cut")
        pc_at = {n: k for k, n in enumerate(RW_COLS)}

        def param(name):
            return pc[:, pc_at[name]:pc_at[name] + 1]

        def halves(ap):
            return [ap[:, h * HALF:(h + 1) * HALF] for h in range(NH)]

        ORDER = ("xd", "ld", "ak", "rb", "rk", "x2", "l2", "r2", "x4", "l4", "r3", "l8", "r4", "rt16", "z32",
                 "r32", "rt32", "z64", "r64", "wv", "gu", "qt")

        def bank_of(name, g):
            return banks[2 * g + (ORDER.index(name) % 2 if name != "y" else 0)]

        block = st.enter_context(nc.Block())
        ENGINES = 5

        def pair_end(e, i):
            e.drain().then_inc(s("pair_done"), 1)
            e.wait_ge(s("pair_done"), i * ENGINES + ENGINES)

        @block.sync
        def _(sp):
            sp.dma_start(low_raw[:, 1:T + 1], proj[RW_LOW:RW_LOW + P, :]).then_inc(low_in, 16)
            with sp.Fori(0, PAIRS) as i:
                for n, at in (("k", RW_K), ("r", RW_R), ("v", RW_V)):
                    sp.dma_start(raw[n][:, 1:T + 1], proj[bass.ds(i * P + at, P), :]).then_inc(s("in_" + n), 16)
                for part, p0, p1 in (("rw_w_up", 0, 32), ("rw_a_up", 32, 64), ("rw_g_up", 64, 128)):
                    sp.dma_start(up[p0:p1, :], args[part].rearrange("l p n -> (l p) n")[:, bass.ds(i * P, P)]
                                 ).then_inc(s("in_up"), 16)
                sp.wait_ge(s("mixed"), i + 1)
                sp.sem_inc(s("sp_passed"), 1)
                sp.dma_start(mixed[bass.ds(i * P + SBW, P), :], b[1][:]).then_inc(s("stored"), 16)
                sp.wait_ge(s("stored"), i * 16 + 16)
                sp.sem_inc(s("pair_done"), 1)
                sp.wait_ge(s("pair_done"), i * ENGINES + ENGINES)
                sp.sem_inc(s("sp_passed"), 1)

        @block.gpsimd
        def _(pool):
            for n in "rkv":
                pool.memset(raw[n][:, 0:1], 0.0)
            pool.memset(low_raw[:, 0:1], 0.0)
            pool.memset(state[:, 0, :], 0.0)
            pool.memset(start[:], 1.0).then_inc(s("cleared"), 1)
            pool.wait_ge(s("cleared"), 1)
            pool.memset(start[:].rearrange("p (c t) -> p c t", t=C)[:, :, 0:1], 0.0).then_inc(s("cleared"), 1)
            with pool.Fori(0, PAIRS) as i:
                pool.memset(raw["r"][:, 0:1], 0.0)
                pool.memset(raw["k"][:, 0:1], 0.0)
                pool.memset(raw["v"][:, 0:1], 0.0).then_inc(s("zero_before"), 1)
                for g in range(NG):
                    pool.wait_ge(s("t_xd"), i * NG + g + 1)
                    pool.tensor_tensor(sets[g]["R"][:], sets[g]["s0"][:],
                                       ident[:].unsqueeze(1).to_broadcast([P, NT, P]), ALU.add
                                       ).then_inc(s("t_r1"), 1)
                pair_end(pool, i)

        @block.scalar
        def _(act):
            mu_low = col[:, COL["rw_mu"] + 9:COL["rw_mu"] + 10]
            act.wait_ge(low_in, 16)
            act.wait_ge(low_cut, 1)
            act.activation(low[:], low_raw[:, 1:T + 1], ACT.Copy, scale=rest[:, 3:4]).then_inc(s("low_part"), 1)
            act.wait_ge(low_cut, 2)
            act.activation(low[0:32, :], low[0:32, :], ACT.Tanh)
            act.activation(low[64:128, :], low[64:128, :], ACT.Sigmoid).then_inc(s("low_done"), 1)
            with act.Fori(0, PAIRS) as i:
                act.wait_ge(s("cols"), i + 1)
                for n, dst, k in (("k", ks_, 1), ("r", rs_, 0), ("v", vs_, 2)):
                    act.wait_ge(s("in_" + n), i * 16 + 16)
                    act.activation(dst[:], raw[n][:, 1:T + 1], ACT.Copy, scale=rest[:, k:k + 1]
                                   ).then_inc(s("part_" + n), 1)
                for n, dst, bias in (("w", b[3], "w0"), ("a", b[4], "a0")):
                    act.wait_ge(s("pre_" + n), i + 1)
                    for h in range(NH):
                        act.activation(halves(dst)[h], banks[(0 if n == "w" else 2) + h][:], ACT.Sigmoid,
                                       bias=param(bias)).then_inc(s("sig_" + n), 1)
                act.preload_act_table_set(EXP_LN)
                act.wait_ge(s("shift_k"), i + 1)
                act.activation(b[6][:], ks_[:], ACT.Square, scale=param("k_k")).then_inc(s("ksq"), 1)
                act.wait_ge(s("norm_kept"), i + 1)
                act.activation(b[6][:], b[6][:], ACT.Ln).then_inc(s("ln"), 1)
                act.wait_ge(s("ln"), i + 1)
                act.activation(b[6][:], b[6][:], ACT.Exp, scale=-0.5).then_inc(s("rn"), 1)
                act.wait_ge(s("cumx"), i + 1)
                act.activation(b[9][:], b[7][:], ACT.Exp, scale=-DECAY).then_inc(s("ep"), 1)
                act.activation(b[10][:], b[7][:], ACT.Exp, scale=DECAY).then_inc(s("en"), 1)
                act.activation(b[8][:], b[8][:], ACT.Exp, scale=-DECAY).then_inc(s("ex"), 1)
                for k, n in enumerate("abkv"):
                    for h in range(2):
                        act.wait_ge(s("nat_mm_" + n), i * 2 + h + 1)
                        act.copy(nat[n][:, 4 * h:4 * h + 4, :],
                                 banks[2 * k + h][:].rearrange("p (j f) -> p j f", f=P)).then_inc(s("nat_" + n), 1)

                def take(name, slot, n=P):
                    for g in range(NG):
                        act.wait_ge(s("m_" + name), i * NG + g + 1)
                        act.copy(sets[g][slot][:, :, 0:n], bank_of(name, g)[:, 0:NT * n].rearrange("p (j c) -> p j c", c=n)
                                 ).then_inc(s("t_" + name), 1)

                take("x2", "s2")
                take("l2", "s3")
                take("x4", "s0")
                take("l4", "s1")
                take("l8", "s2")
                take("rt16", "s3")
                take("z32", "s0")
                take("rt32", "s3")
                take("z64", "s0")
                take("wv", "s1", C)
                take("gu", "gu")
                for g in range(NG):
                    h, th = g // 2, g % 2
                    act.wait_ge(s("m_y"), i * NG + g + 1)
                    act.copy(Y[:, 4 * th:4 * th + 4, C * h:C * h + C],
                             bank_of("y", g)[:, 0:NT * C].rearrange("p (j v) -> p j v", v=C)).then_inc(s("y"), 1)
                act.wait_ge(s("centred"), i + 1)
                act.activation(b[5][:], b[3][:], ACT.Square).then_inc(s("ysq"), 1)
                act.wait_ge(s("var"), i + 1)
                act.activation(small[:, 1, :], small[:, 1, :], ACT.Sqrt).then_inc(s("root"), 1)
                for h in range(2):
                    act.wait_ge(s("back"), i * 2 + h + 1)
                    act.activation(halves(b[1])[h], banks[h][:], ACT.Identity, scale=param("gn_g"),
                                   bias=param("gn_b")).then_inc(s("affine"), 1)
                pair_end(act, i)

        @block.vector
        def _(dve):
            mu_low = col[:, COL["rw_mu"] + 9:COL["rw_mu"] + 10]
            dve.tensor_scalar(rest[:, 3:4], mu_low, -1.0, 1.0, ALU.mult, ALU.add).then_inc(low_cut, 1)
            dve.wait_ge(s("low_part"), 1)
            dve.wait_ge(s("cleared"), 2)
            dve.scalar_tensor_tensor(low[:], low_raw[:, 0:T], mu_low, low[:], ALU.mult, ALU.add).then_inc(low_cut, 1)
            with dve.Fori(0, PAIRS) as i:
                def one(name):
                    dve.wait_ge(s(name), i + 1)

                dve.tensor_copy(pc[:].rearrange("p (n o) -> p n o", o=1),
                                col[:, COL["rw_w0"]:COL["rw_w0"] + 3 * NPC].rearrange("p (n q) -> p n q", q=3)
                                [:, :, bass.ds(i, 1)]).then_inc(s("cols_raw"), 1)
                one("cols_raw")
                dve.tensor_scalar(rest[:, 0:3], pc[:, 7:10], -1.0, 1.0, ALU.mult, ALU.add).then_inc(s("cols"), 1)
                one("zero_before")
                for n, dst in (("k", ks_), ("r", rs_), ("v", vs_)):
                    one("part_" + n)
                    dve.scalar_tensor_tensor(dst[:], raw[n][:, 0:T], param("mu_" + n), dst[:],
                                             ALU.mult, ALU.add).then_inc(s("shift_" + n), 1)
                one("shift_k")
                dve.tensor_scalar(b[5][:], ks_[:], param("k_k"), None, ALU.mult).then_inc(s("kx"), 1)
                dve.wait_ge(s("sig_w"), i * 2 + 2)
                dve.tensor_tensor_scan(b[7][:], start[:], b[3][:], 0.0, ALU.mult, ALU.add).then_inc(s("cum"), 1)
                one("cum")
                dve.tensor_tensor(b[8][:], b[7][:], b[3][:], ALU.subtract).then_inc(s("cumx"), 1)
                one("norm_mm")
                for h in range(2):
                    m = dve.tensor_scalar(halves(b[6])[h], banks[4 + h][:], 1e-12, None, ALU.max)
                m.then_inc(s("norm_kept"), 1)
                one("rn")
                one("kx")
                dve.tensor_tensor(b[5][:], b[5][:], b[6][:], ALU.mult).then_inc(s("kk"), 1)
                one("kk")
                one("ex")
                dve.scalar_tensor_tensor(b[8][:], b[5][:], -1.0, b[8][:], ALU.mult, ALU.mult).then_inc(s("at"), 1)
                dve.wait_ge(s("sig_a"), i * 2 + 2)
                dve.tensor_tensor(b[6][:], b[5][:], b[4][:], ALU.mult).then_inc(s("bvec"), 1)
                one("bvec")
                dve.tensor_tensor(b[6][:], b[6][:], b[10][:], ALU.mult).then_inc(s("bt"), 1)
                dve.tensor_scalar(b[4][:], b[4][:], -1.0, param("k_a"), ALU.add, ALU.mult).then_inc(s("am"), 1)
                one("am")
                dve.scalar_tensor_tensor(b[4][:], b[4][:], 1.0, ks_[:], ALU.add, ALU.mult).then_inc(s("km"), 1)
                one("km")
                one("bt")
                dve.tensor_tensor(b[10][:], b[10][:], b[4][:], ALU.mult).then_inc(s("kt"), 1)
                one("shift_r")
                dve.tensor_tensor(b[7][:], rs_[:], b[9][:], ALU.mult).then_inc(s("rt"), 1)
                dve.scalar_tensor_tensor(b[3][:], rs_[:], param("r_k"), b[4][:], ALU.mult, ALU.mult
                                         ).then_inc(s("rkk"), 1)
                one("bonus_mm")
                one("shift_v")
                for h in range(2):
                    m = dve.tensor_tensor(halves(rs_)[h], halves(vs_)[h], banks[6 + h][:], ALU.mult)
                m.then_inc(s("bonus"), 1)

                def grp(name, g):
                    dve.wait_ge(s(name), i * NG + g + 1)

                def masked(name, outs):
                    for g in range(NG):
                        grp("m_" + name, g)
                        for slot, m in outs:
                            k = dve.tensor_tensor(sets[g][slot][:], bank_of(name, g)[:].rearrange("p (j c) -> p j c", c=P),
                                                  mask[m].unsqueeze(1).to_broadcast([P, NT, P]), ALU.mult)
                        k.then_inc(s("t_" + name), 1)

                def add_to_r(name, before):
                    for g in range(NG):
                        grp("m_" + name, g)
                        grp("t_" + before, g)
                        R = sets[g]["R"][:]
                        dve.tensor_tensor(R, R, bank_of(name, g)[:].rearrange("p (j c) -> p j c", c=P), ALU.add
                                          ).then_inc(s("t_" + name), 1)

                masked("xd", (("s0", "up16"),))
                masked("ld", (("s1", "low16"), ("lo32", "low32"), ("lo64", "low64")))
                masked("ak", (("ak", "up64"),))
                masked("rb", (("rb", "upd64"),))
                masked("rk", (("rk", "upd64"),))
                add_to_r("r2", "r1")
                add_to_r("r3", "r2")
                add_to_r("r4", "r3")
                add_to_r("r32", "r4")
                add_to_r("r64", "r32")
                for g in range(NG):
                    h, th = g // 2, g % 2
                    hs, js = slice(C * h, C * h + C), slice(NT * th, NT * th + NT)
                    grp("m_qt", g)
                    dve.tensor_tensor(QT[hs, js, :], bank_of("qt", g)[hs, :].rearrange("p (j t) -> p j t", t=P),
                                      b[7][hs, th * HALF:(th + 1) * HALF].rearrange("p (j t) -> p j t", t=P),
                                      ALU.add).then_inc(s("t_qt"), 1)
                for g in range(NG):
                    h, th = g // 2, g % 2
                    hs = slice(C * h, C * h + C)
                    grp("m_mk", g)
                    for c in range(2):
                        both = banks[2 * g + c][hs, :].rearrange("p (j f) -> p j f", f=P)
                        of = lambda ap: ap.rearrange("p (j two) k -> p j two k", two=2)[hs, NT * th:NT * (th + 1), c, :]
                        last = b[9][hs, :].rearrange("p (j two t) -> p j two t", two=2, t=C)
                        dve.tensor_tensor(of(MT), both[:, :, 0:C], ident[hs, hs].unsqueeze(1).to_broadcast([C, NT, C]),
                                          ALU.add)
                        m = dve.tensor_tensor(of(KW), both[:, :, C:P],
                                              last[:, NT * th:NT * (th + 1), c, C - 1:C].to_broadcast([C, NT, C]),
                                              ALU.mult)
                    m.then_inc(s("t_mk"), 1)
                grp("t_mk", NG - 1)
                for c in range(NC):
                    dve.wait_ge(s("step_mm"), i * NC + c + 1)
                    dve.scalar_tensor_tensor(state[:, c + 1, :], banks[c % 2][:, 0:C],
                                             b[9][:, c * C + C - 1:c * C + C], KW[:, c, :],
                                             ALU.mult, ALU.add).then_inc(s("step"), 1)
                dve.wait_ge(s("y"), i * NG + NG)
                y3 = b[3][:].rearrange("p (n v) -> p n v", v=C)
                bc = lambda q: small[:, q, :].unsqueeze(2).to_broadcast([P, 2 * TB, C])
                dve.tensor_reduce(small[:, 0, :], y3, AX.X, ALU.add).then_inc(s("ysum"), 1)
                one("ysum")
                dve.tensor_scalar(small[:, 0, :], small[:, 0, :], 1.0 / C, None, ALU.mult).then_inc(s("mean"), 1)
                one("mean")
                dve.tensor_tensor(y3, y3, bc(0), ALU.subtract).then_inc(s("centred"), 1)
                one("ysq")
                dve.tensor_reduce(small[:, 1, :], b[5][:].rearrange("p (n v) -> p n v", v=C), AX.X, ALU.add
                                  ).then_inc(s("vsum"), 1)
                one("vsum")
                dve.tensor_scalar(small[:, 1, :], small[:, 1, :], 1.0 / C, GN_EPS, ALU.mult, ALU.add
                                  ).then_inc(s("var"), 1)
                one("root")
                dve.reciprocal(small[:, 2, :], small[:, 1, :]).then_inc(s("rstd"), 1)
                one("rstd")
                dve.tensor_tensor(y3, y3, bc(2), ALU.mult).then_inc(s("normed"), 1)
                dve.wait_ge(s("affine"), i * 2 + 2)
                dve.tensor_tensor(b[1][:], b[1][:], rs_[:], ALU.add).then_inc(s("biased"), 1)
                one("biased")
                one("gate_mm")
                for h in range(2):
                    m = dve.tensor_tensor(halves(b[1])[h], halves(b[1])[h], banks[2 + h][:], ALU.mult)
                m.then_inc(s("mixed"), 1)
                pair_end(dve, i)

        @block.tensor
        def _(pe):
            pe.wait_ge(s("low_done"), 1)
            pe.wait_ge(low_cut, 2)
            with pe.Fori(0, PAIRS) as i:
                def one(name):
                    pe.wait_ge(s(name), i + 1)

                pe.wait_ge(s("in_up"), i * 48 + 48)
                for n, p0, p1, k in (("w", 0, 32, 0), ("a", 32, 64, 2)):
                    for h in range(NH):
                        m = pe.matmul(banks[k + h][:], up[p0:p1, :], halves(low)[h][p0:p1, :], start=True, stop=True)
                    m.then_inc(s("pre_" + n), 1)
                one("ksq")
                for h in range(NH):
                    m = pe.matmul(banks[4 + h][:], mask["same64"], halves(b[6])[h], start=True, stop=True)
                m.then_inc(s("norm_mm"), 1)
                one("rkk")
                for h in range(NH):
                    m = pe.matmul(banks[6 + h][:], mask["same64"], halves(b[3])[h], start=True, stop=True)
                m.then_inc(s("bonus_mm"), 1)
                for k, (n, src, made) in enumerate((("a", b[8], "at"), ("b", b[6], "bt"), ("k", b[10], "kt"),
                                                    ("v", vs_, "shift_v"))):
                    one(made)
                    if k == 3:
                        one("bonus")
                    for h in range(2):
                        for q in range(4):
                            j = 4 * h + q
                            m = pe.transpose(banks[2 * k + h][:, q * P:(q + 1) * P], src[:, j * P:(j + 1) * P], ident[:])
                        m.then_inc(s("nat_mm_" + n), 1)
                for n in "abkv":
                    pe.wait_ge(s("nat_" + n), i * 2 + 2)
                one("rt")

                def grp(name, g):
                    pe.wait_ge(s(name), i * NG + g + 1)

                def step(name, needs, product):
                    n = ORDER.index(name)
                    for g in range(NG):
                        if n >= 2:
                            grp("t_" + ORDER[n - 2], g)
                        for need in needs:
                            grp("t_" + need, g)
                        bk = bank_of(name, g)
                        for j in range(NT):
                            m = product(g, sets[g], j, bk)
                        m.then_inc(s("m_" + name), 1)

                def scores(left, right):
                    def product(g, q, j, bk):
                        h, th = g // 2, g % 2
                        hs = slice(C * h, C * h + C)
                        ts = slice((NT * th + j) * P, (NT * th + j + 1) * P)
                        return pe.matmul(bk[:, j * P:(j + 1) * P], left[hs, ts], right[hs, ts], start=True, stop=True)
                    return product

                def square(left, right):
                    def product(g, q, j, bk):
                        return pe.matmul(bk[:, j * P:(j + 1) * P], q[left][:, j, :], q[right][:, j, :],
                                         start=True, stop=True)
                    return product

                def turned(src):
                    def product(g, q, j, bk):
                        return pe.transpose(bk[:, j * P:(j + 1) * P], q[src][:, j, :], ident[:])
                    return product

                def tile_of(g, j):
                    return NT * (g % 2) + j, slice(C * (g // 2), C * (g // 2) + C)

                step("xd", (), scores(b[6], b[8]))
                step("ld", (), scores(b[8], b[6]))
                step("ak", (), scores(b[10], b[8]))
                step("rb", (), scores(b[6], b[7]))
                step("rk", (), scores(b[10], b[7]))
                step("x2", ("ld",), square("s1", "s0"))
                step("l2", (), square("s0", "s1"))
                step("r2", ("l2", "r1"), square("s3", "R"))
                step("x4", ("x2",), square("s3", "s2"))
                step("l4", (), square("s2", "s3"))
                step("r3", ("l4", "r2"), square("s1", "R"))
                step("l8", ("x4",), square("s0", "s1"))
                step("r4", ("l8", "r3"), square("s2", "R"))
                step("rt16", ("r4",), turned("R"))
                step("z32", (), square("lo32", "R"))
                step("r32", ("z32", "rt16"), square("s3", "s0"))
                step("rt32", ("r32",), turned("R"))
                step("z64", (), square("lo64", "R"))
                step("r64", ("z64", "rt32"), square("s3", "s0"))

                def keys_values(g, q, j, bk):
                    t, hs = tile_of(g, j)
                    return pe.matmul(bk[:, j * C:(j + 1) * C], q["ak"][:, j, :], nat["v"][:, t, hs], start=True, stop=True)

                step("wv", ("ak",), keys_values)

                def updates(g, q, j, bk):
                    t, hs = tile_of(g, j)
                    pe.matmul(bk[:, j * P:j * P + C], q["R"][:, j, :], nat["a"][:, t, hs], start=True, stop=True)
                    return pe.matmul(bk[:, j * P + C:(j + 1) * P], q["R"][:, j, :], q["s1"][:, j, 0:C],
                                     start=True, stop=True)

                step("gu", ("wv", "r64"), updates)

                def readers(g, q, j, bk):
                    t, hs = tile_of(g, j)
                    return pe.matmul(bk[hs, j * P:(j + 1) * P], q["gu"][:, j, 0:C], q["rb"][:, j, :], start=True, stop=True)

                step("qt", ("gu", "rb"), readers)

                for g in range(NG):
                    q = sets[g]
                    grp("t_gu", g)
                    grp("t_qt", g)
                    pe.sem_inc(s("pe_passed"), 1)
                    for c in range(2):
                        cs = slice(C * c, C * c + C)
                        for j in range(NT):
                            t, hs = tile_of(g, j)
                            m = pe.matmul(banks[2 * g + c][hs, j * P:j * P + C], q["gu"][cs, j, 0:C],
                                          nat["b"][cs, t, hs], start=True, stop=True)
                            o = banks[2 * g + c][hs, j * P + C:(j + 1) * P]
                            pe.matmul(o, nat["b"][cs, t, hs], q["gu"][cs, j, C:P], start=True, stop=False)
                            m = pe.matmul(o, nat["k"][cs, t, hs], nat["v"][cs, t, hs], start=False, stop=True)
                    m.then_inc(s("m_mk"), 1)
                grp("t_mk", NG - 1)
                for c in range(NC):
                    if c:
                        pe.wait_ge(s("step"), i * NC + c)
                    pe.sem_inc(s("pe_passed"), 1)
                    for h in range(2):
                        hs = slice(C * h, C * h + C)
                        m = pe.matmul(banks[c % 2][hs, 0:C], MT[hs, c, :], state[hs, c, :], start=True, stop=True)
                    m.then_inc(s("step_mm"), 1)
                pe.wait_ge(s("step"), i * NC + NC)
                grp("t_rk", NG - 1)
                for g in range(NG):
                    q, bk = sets[g], bank_of("y", g)
                    for j in range(NT):
                        t, hs = tile_of(g, j)
                        o = slice(j * C, (j + 1) * C)
                        pe.matmul(bk[:, o], q["rb"][:, j, :], q["gu"][:, j, C:P], start=True, stop=False)
                        pe.matmul(bk[:, o], q["rk"][:, j, :], nat["v"][:, t, hs], start=False, stop=True)
                        for c in range(2):
                            cs = slice(C * c, C * c + C)
                            m = pe.matmul(bk[cs, o], QT[hs, t, cs], state[hs, 2 * t + c, :], start=False, stop=True,
                                          skip_group_check=True)
                    m.then_inc(s("m_y"), 1)
                one("normed")
                for h in range(2):
                    for q in range(4):
                        j = 4 * h + q
                        m = pe.transpose(banks[h][:, q * P:(q + 1) * P], Y[:, j, :], ident[:])
                    m.then_inc(s("back"), 1)
                for h in range(NH):
                    m = pe.matmul(banks[2 + h][:], up[64:128, :], halves(low)[h][64:128, :], start=True, stop=True)
                m.then_inc(s("gate_mm"), 1)
                pair_end(pe, i)


def gla(nc, con, args, proj, mixed):
    ident, col, levels = con["ident"], con["col"], con["levels"]
    NL = 6
    H, DK, DV = 4, 32, 64
    NC = T // C
    WV = H * DV
    with ExitStack() as st:
        r = Region(nc, st, "gla")
        q, k = r.sb("q", [P, T]), r.sb("k", [P, T])
        vT = [r.sb(f"vT{n}", [P, T]) for n in range(2)]
        gT = [r.sb(f"gT{n}", [P, T]) for n in range(2)]
        sg = [r.sb(f"sg{n}", [P, T]) for n in range(2)]
        gd, gate_up = r.sb("gd", [16, T]), r.sb("gup", [16, P])
        x, e, cum, start = r.sb("x", [P, T]), r.sb("e", [P, T]), r.sb("cum", [P, T]), r.sb("start", [P, T])
        D_ = [r.sb(f"D{n}", [P, T]) for n in range(2)]
        qf = [r.sb(f"qf{n}", [P, T]) for n in range(2)]
        kf = [r.sb(f"kf{n}", [P, T]) for n in range(2)]
        qin, kout = r.sb("qin", [P, T]), r.sb("kout", [P, T])
        A = r.sb("A", [P, H, TB, P])
        knat, vnat = r.sb("knat", [P, TB, P]), r.sb("vnat", [P, TB, WV])
        heads = r.sb("heads", [P, WV])
        KV = r.sb("KV", [P, NC, WV])
        S = r.sb("S", [P, NC + 1, WV])
        small = r.sb("small", [P, 2, TB * H])
        O, osq = KV, S
        banks = [r.bank(f"b{n}") for n in range(8)]
        sems = {}

        def s(name):
            if name not in sems:
                sems[name] = r.sem(name)
            return sems[name]

        block = st.enter_context(nc.Block())
        LOADS = [(q, GLA_Q, P, "q"), (k, GLA_K, P, "k"), (vT[0], GLA_V, P, "v"), (vT[1], GLA_V + P, P, "v"),
                 (gT[0], GLA_G, P, "g"), (gT[1], GLA_G + P, P, "g")]

        @block.sync
        def _(sp):
            sp.dma_start(gd[:], proj[GLA_GD:GLA_GD + 16, :]).then_inc(s("in_gd"), 16)
            sp.dma_start(gate_up[:], args["gla_gate_up"].rearrange("l p n -> (l p) n")).then_inc(s("in_gd"), 16)
            for dst, at, n, name in LOADS:
                sp.dma_start(dst[:], proj[at:at + n, :]).then_inc(s("in_" + name), 16)
            for n in range(2):
                sp.wait_ge(s("mixed"), n + 1)
                sp.dma_start(mixed[SBW + RWW + n * P:SBW + RWW + (n + 1) * P, :], qf[n][:]).then_inc(s("stored"), 16)
            sp.wait_ge(s("stored"), 32)

        @block.gpsimd
        def _(pool):
            pool.memset(start[:], 1.0).then_inc(s("ones"), 1)
            pool.wait_ge(s("ones"), 1)
            pool.memset(start[:].rearrange("p (c t) -> p c t", t=C)[:, :, 0:1], 0.0).then_inc(s("start"), 1)
            for n in range(2):
                pool.memset(qf[n][:], 0.0)
                pool.memset(kf[n][:], 0.0)
            pool.memset(A[:].rearrange("p h j t -> p (h j t)"), 0.0).then_inc(s("zeroed"), 1)
            pool.memset(heads[:], 0.0).then_inc(s("heads"), 1)
            pool.wait_ge(s("heads"), 1)
            for h in range(H):
                pool.memset(heads[DK * h:DK * h + DK, DV * h:DV * h + DV], 1.0).then_inc(s("heads"), 1)
                pool.wait_ge(s("heads"), h + 2)
            pool.memset(S[:, 0, :], 0.0).then_inc(s("heads"), 1)

        @block.scalar
        def _(act):
            act.wait_ge(s("in_g"), 32)
            for n in range(2):
                act.activation(sg[n][:], gT[n][:], ACT.Sigmoid).then_inc(s("sigmoid"), 1)
            act.preload_act_table_set(EXP_LN)
            act.wait_ge(s("gate_mm"), 1)
            bias = col[:, COL["gla_gate_b"]:COL["gla_gate_b"] + 1]
            for h in range(NH):
                hs = slice(h * HALF, (h + 1) * HALF)
                act.activation(e[:, hs], banks[h][:], ACT.Abs, bias=bias)
                act.activation(x[:, hs], banks[h][:], ACT.Identity, bias=bias).then_inc(s("arg"), 1)
            act.wait_ge(s("arg"), 2)
            act.activation(e[:], e[:], ACT.Exp, scale=-1.0).then_inc(s("exp"), 1)
            act.wait_ge(s("exp"), 1)
            act.activation(e[:], e[:], ACT.Ln, bias=1.0).then_inc(s("log"), 1)
            act.wait_ge(s("in_q"), 16)
            act.activation(q[:], q[:], ACT.Copy, scale=float(DK) ** -0.5).then_inc(s("q"), 1)
            act.wait_ge(s("cum"), 1)
            act.activation(qin[:], cum[:], ACT.Exp, scale=-1.0 / 16).then_inc(s("from_start"), 1)
            act.wait_ge(s("to_last"), 1)
            act.activation(kout[:], kout[:], ACT.Exp, scale=-1.0 / 16).then_inc(s("to_end"), 1)
            act.wait_ge(s("softplus"), 1)
            act.activation(e[:, 0:NC], cum[:].rearrange("p (c t) -> p c t", t=C)[:, :, C - 1], ACT.Exp,
                           scale=-1.0 / 16).then_inc(s("decay"), 1)

            def factor(n):
                act.wait_ge(s("diff"), n + 1)
                act.activation(D_[n % 2][:], D_[n % 2][:], ACT.Exp, scale=-1.0 / 16).then_inc(s("factor"), 1)

            factor(0)
            factor(1)
            for m in range(2):
                for h in range(2):
                    act.wait_ge(s("vnat_mm"), 2 * m + h + 1)
                    act.copy(vnat[:, 4 * h:4 * h + 4, m * P:(m + 1) * P],
                             banks[2 * m + h][:].rearrange("p (j f) -> p j f", f=P)).then_inc(s("vnat"), 1)
            for h in range(2):
                act.wait_ge(s("knat_mm"), h + 1)
                act.copy(knat[:, 4 * h:4 * h + 4, :], banks[4 + h][:].rearrange("p (j f) -> p j f", f=P)
                         ).then_inc(s("knat"), 1)
            for n in range(2, NL):
                factor(n)
            for n in range(4):
                act.wait_ge(s("o_mm"), n + 1)
                act.copy(O[:, 2 * n:2 * n + 2, :], banks[n][:].rearrange("p (j v) -> p j v", v=WV)).then_inc(s("o"), 1)
            act.wait_ge(s("o"), 4)
            act.activation(osq[:, 0:TB, :], O[:, 0:TB, :], ACT.Square).then_inc(s("osq"), 1)
            act.wait_ge(s("mean"), 1)
            act.activation(small[:, 0, :], small[:, 0, :], ACT.Sqrt).then_inc(s("root"), 1)
            for m in range(2):
                for h in range(NH):
                    act.wait_ge(s("back"), 2 * m + h + 1)
                    act.activation(qf[m][:, h * HALF:(h + 1) * HALF], banks[4 + 2 * m + h][:], ACT.Copy,
                                   scale=col[:, COL["gla_norm_g"] + m:COL["gla_norm_g"] + m + 1]).then_inc(s("gained"), 1)

        @block.vector
        def _(dve):
            w = lambda name, n=1: dve.wait_ge(s(name), n)
            w("sigmoid", 2)
            for n in range(2):
                dve.tensor_tensor(sg[n][:], sg[n][:], gT[n][:], ALU.mult).then_inc(s("silu"), 1)
            w("arg", 2)
            dve.tensor_scalar(x[:], x[:], -1.0, 0.0, ALU.mult, ALU.max).then_inc(s("rect"), 1)
            w("rect")
            w("log")
            dve.tensor_tensor(x[:], x[:], e[:], ALU.add).then_inc(s("softplus"), 1)
            w("softplus")
            w("start")
            dve.tensor_tensor_scan(cum[:], start[:], x[:], 0.0, ALU.mult, ALU.add).then_inc(s("cum"), 1)
            w("cum")
            c3 = lambda ap: ap.rearrange("p (c t) -> p c t", t=C)
            dve.tensor_tensor(c3(kout[:]), c3(cum[:])[:, :, C - 1:C].to_broadcast([P, NC, C]), c3(cum[:]),
                              ALU.subtract).then_inc(s("to_last"), 1)

            def differences(n):
                m = 1 << n
                v = lambda ap: ap.rearrange("p (b two m) -> p b two m", two=2, m=m)
                cu, d = v(cum[:]), v(D_[n % 2][:])
                nb = T // (2 * m)
                mid = cu[:, :, 0, m - 1:m].to_broadcast([P, nb, m])
                if n >= 2:
                    w("kf", n - 1)
                dve.tensor_tensor(d[:, :, 0, :], mid, cu[:, :, 0, :], ALU.subtract)
                dve.tensor_tensor(d[:, :, 1, :], cu[:, :, 1, :], mid, ALU.subtract).then_inc(s("diff"), 1)

            differences(0)
            w("q")
            w("from_start")
            dve.tensor_tensor(qin[:], qin[:], q[:], ALU.mult).then_inc(s("qin"), 1)
            w("to_end")
            w("in_k", 16)
            dve.tensor_tensor(kout[:], kout[:], k[:], ALU.mult).then_inc(s("kout"), 1)
            w("zeroed")

            def factors(n):
                m = 1 << n
                v = lambda ap, half: ap.rearrange("p (b two m) -> p b two m", two=2, m=m)[:, :, half, :]
                w("factor", n + 1)
                if n >= 2:
                    w("level_mm", 8 * (n - 1))
                dve.tensor_tensor(v(qf[n % 2][:], 1), v(D_[n % 2][:], 1), v(q[:], 1), ALU.mult)
                dve.tensor_tensor(v(kf[n % 2][:], 0), v(D_[n % 2][:], 0), v(k[:], 0), ALU.mult).then_inc(s("kf"), 1)

            def take(n):
                for g in range(8):
                    h, th = g // 2, g % 2
                    w("level_mm", 8 * n + g + 1)
                    msk = (levels[:, n, :] if n < NL else ident[:]).bitcast(U32)
                    dve.copy_predicated(A[:, h, 4 * th:4 * th + 4, :], msk.unsqueeze(1).to_broadcast([P, 4, P]),
                                        banks[g][:].rearrange("p (j t) -> p j t", t=P)).then_inc(s("taken"), 1)

            differences(1)
            factors(0)
            factors(1)
            for n in range(NL):
                if n + 2 < NL:
                    differences(n + 2)
                take(n)
                if n + 2 < NL:
                    factors(n + 2)
            take(NL)
            w("heads", H + 2)
            for n in range(8):
                w("kv_mm", n + 1)
                t, c = n // 2, n % 2
                dst = KV[:].rearrange("p (j two) v -> p j two v", two=2)[:, 2 * t:2 * t + 2, c, :]
                dve.tensor_tensor(dst, banks[n][:].rearrange("p (j v) -> p j v", v=WV),
                                  heads[:].unsqueeze(1).to_broadcast([P, 2, WV]), ALU.mult).then_inc(s("kv"), 1)
            w("decay")
            for c in range(NC):
                if c:
                    w("state", c)
                else:
                    w("kv", 8)
                dve.scalar_tensor_tensor(S[:, c + 1, :], S[:, c, :], e[:, c:c + 1], KV[:, c, :],
                                         ALU.mult, ALU.add).then_inc(s("state"), 1)
            w("osq")
            dve.tensor_reduce(small[:, 0, :], osq[:, 0:TB, :].rearrange("p j (h v) -> p (j h) v", v=DV), AX.X, ALU.add
                              ).then_inc(s("ssum"), 1)
            w("ssum")
            dve.tensor_scalar(small[:, 0, :], small[:, 0, :], 1.0 / DV, EPS, ALU.mult, ALU.add).then_inc(s("mean"), 1)
            w("root")
            dve.reciprocal(small[:, 1, :], small[:, 0, :]).then_inc(s("rstd"), 1)
            w("rstd")
            o3 = O[:, 0:TB, :].rearrange("p j (h v) -> p (j h) v", v=DV)
            dve.tensor_tensor(o3, o3, small[:, 1, :].unsqueeze(2).to_broadcast([P, TB * H, DV]), ALU.mult
                              ).then_inc(s("normed"), 1)
            for m in range(2):
                w("gained", 2 * m + 2)
                dve.tensor_tensor(qf[m][:], qf[m][:], sg[m][:], ALU.mult).then_inc(s("mixed"), 1)

        @block.tensor
        def _(pe):
            w = lambda name, n=1: pe.wait_ge(s(name), n)
            w("in_gd", 32)
            for h in range(NH):
                m = pe.matmul(banks[h][:], gate_up[:], gd[:, h * HALF:(h + 1) * HALF], start=True, stop=True)
            m.then_inc(s("gate_mm"), 1)
            w("in_v", 32)
            for n in range(2):
                for h in range(2):
                    if 2 * n + h < 2:
                        w("arg", 2)
                    for j in range(4):
                        m = pe.transpose(banks[2 * n + h][:, j * P:(j + 1) * P],
                                         vT[n][:, (4 * h + j) * P:(4 * h + j + 1) * P], ident[:])
                    m.then_inc(s("vnat_mm"), 1)
            w("kout")
            for h in range(2):
                for j in range(4):
                    m = pe.transpose(banks[4 + h][:, j * P:(j + 1) * P],
                                     kout[:, (4 * h + j) * P:(4 * h + j + 1) * P], ident[:])
                m.then_inc(s("knat_mm"), 1)
            w("vnat", 4)
            w("knat", 2)
            for n in range(NL + 1):
                if n < NL:
                    w("kf", n + 1)
                else:
                    w("in_k", 16)
                    w("q")
                for g in range(8):
                    h, th = g // 2, g % 2
                    if n:
                        w("taken", 8 * (n - 1) + g + 1)
                    rows = slice(DK * h, DK * h + DK)
                    for j in range(4):
                        ts = slice((4 * th + j) * P, (4 * th + j + 1) * P)
                        left, right = (kf[n % 2], qf[n % 2]) if n < NL else (k, q)
                        m = pe.matmul(banks[g][:, j * P:(j + 1) * P], left[rows, ts], right[rows, ts],
                                      start=True, stop=True)
                    m.then_inc(s("level_mm"), 1)
            for n in range(8):
                t, c = n // 2, n % 2
                w("taken", 8 * NL + n + 1)
                cs = slice(C * c, C * c + C)
                for j in range(2):
                    m = pe.matmul(banks[n][:, j * WV:(j + 1) * WV], knat[cs, 2 * t + j, :], vnat[cs, 2 * t + j, :],
                                  start=True, stop=True)
                m.then_inc(s("kv_mm"), 1)
            w("kv", 8)
            w("qin")
            for n in range(4):
                w("state", min(4 * n + 4, NC))
                for jj in range(2):
                    j = 2 * n + jj
                    o = slice(jj * WV, (jj + 1) * WV)
                    for c in range(2):
                        pe.matmul(banks[n][C * c:C * c + C, o], qin[:, j * P + C * c:j * P + C * c + C],
                                  S[:, 2 * j + c, :], start=True, stop=True)
                    for h in range(H):
                        m = pe.matmul(banks[n][:, jj * WV + DV * h:jj * WV + DV * h + DV], A[:, h, j, :],
                                      vnat[:, j, DV * h:DV * h + DV], start=False, stop=True, skip_group_check=True)
                m.then_inc(s("o_mm"), 1)
            w("normed")
            for m_ in range(2):
                for h in range(2):
                    for jj in range(4):
                        j = 4 * h + jj
                        m = pe.transpose(banks[4 + 2 * m_ + h][:, jj * P:(jj + 1) * P],
                                         O[:, j, m_ * P:(m_ + 1) * P], ident[:])
                    m.then_inc(s("back"), 1)


def stick_breaking(nc, con, args, proj, mixed):
    ident, col = con["ident"], con["col"]
    mask = {name: con["masks"][:, n, :] for n, name in enumerate(MASKS)}
    DH = 64
    QC = T // HALF
    PER = HALF // P
    CAP = float(2 ** 60)
    UNITS = []
    for c in range(QC):
        for kb in range(PER * (c + 1) - 1, -1, -1):
            for h in range(2):
                UNITS.append((h, c, kb, max(0, (kb - PER * c) * P), kb == PER * (c + 1) - 1))
    NU = len(UNITS)
    NZ, AHEAD = 4, 2
    with ExitStack() as st:
        r = Region(nc, st, "sb")
        qd, kd = [r.sb(f"qd{h}", [P, T]) for h in range(2)], [r.sb(f"kd{h}", [P, T]) for h in range(2)]
        vp = r.sb("vp", [P, T])
        kS = [r.sb(f"kS{h}", [P, T], F32R) for h in range(2)]
        qH, qL = [r.sb(f"qH{h}", [P, T], F32R) for h in range(2)], [r.sb(f"qL{h}", [P, T], F32R) for h in range(2)]
        vn = r.sb("vn", [P, TB, P])
        E = [r.sb(f"E{n}", [P, HALF]) for n in range(4)]
        SP = [r.sb(f"SP{n}", [P, HALF]) for n in range(4)]
        R = [[r.sb(f"R{h}{n}", [P, HALF]) for n in range(2)] for h in range(2)]
        W = [r.sb(f"W{n}", [P, HALF]) for n in range(4)]
        tri, ones = r.sb("tri", [P, P]), r.sb("ones", [P, P])
        O, osq = r.sb("O", [P, TB, P]), r.sb("osq", [P, TB, P])
        outT = r.sb("outT", [P, T])
        small = r.sb("small", [P, 2, 2 * TB])
        small_gain = r.sb("gain", [P, 1])
        Z = [r.bank(f"Z{n}") for n in range(NZ)]
        OB = [[r.bank(f"O{h}{c}") for c in range(QC)] for h in range(2)]
        sems = {}

        def s(name):
            if name not in sems:
                sems[name] = r.sem(name)
            return sems[name]

        ENGINES = 5
        block = st.enter_context(nc.Block())

        def pair_end(e, i):
            e.drain().then_inc(s("pair_done"), 1)
            e.wait_ge(s("pair_done"), i * ENGINES + ENGINES)

        def span(u):
            h, c, kb, off, first = UNITS[u]
            return slice(off, HALF)

        @block.sync
        def _(sp):
            with sp.Fori(0, PAIRS) as i:
                for h in range(2):
                    for half in range(2):
                        rows = slice(DH * half, DH * half + DH)
                        sp.dma_start(kd[h][rows, :], proj[bass.ds(i * P + SB_K + DH * h, DH), :]).then_inc(s("in_k"), 16)
                        sp.dma_start(qd[h][rows, :], proj[bass.ds(i * P + SB_Q + DH * h, DH), :]).then_inc(s("in_q"), 16)
                sp.dma_start(vp[:], proj[bass.ds(i * P + SB_V, P), :]).then_inc(s("in_v"), 16)
                sp.wait_ge(s("mixed"), i * 2 + 2)
                sp.sem_inc(s("sp_passed"), 1)
                sp.dma_start(mixed[bass.ds(i * P, P), :], outT[:]).then_inc(s("stored"), 16)
                sp.wait_ge(s("stored"), i * 16 + 16)
                sp.sem_inc(s("pair_done"), 1)
                sp.wait_ge(s("pair_done"), i * ENGINES + ENGINES)
                sp.sem_inc(s("sp_passed"), 1)

        @block.gpsimd
        def _(pool):
            with pool.Fori(0, PAIRS) as i:
                nth = [0, 0]
                for u in range(NU):
                    h, c, kb, off, first = UNITS[u]
                    new, old = R[h][(nth[h] + 1) % 2], R[h][nth[h] % 2]
                    nth[h] += 1
                    pool.wait_ge(s("sp"), i * NU + u + 1)
                    if u >= 4:
                        pool.wait_ge(s("tri_mm"), i * NU + u - 1)
                    if kb > 0:
                        if first:
                            pool.sem_inc(s("pool_passed"), 1)
                            pool.tensor_copy(new[:, off:], SP[u % 4][:, off:]).then_inc(s("sum"), 1)
                        else:
                            pool.wait_ge(s("sum"), i * NU + u - 1)
                            pool.tensor_tensor(new[:, off:], old[:, off:], SP[u % 4][:, off:], ALU.add
                                               ).then_inc(s("sum"), 1)
                        if off:
                            pool.memset(new[:, off - P:off], 0.0)
                    else:
                        pool.sem_inc(s("sum"), 1)
                    if kb >= PER * c:
                        pool.wait_ge(s("weight"), i * NU + u + 1)
                        pool.sem_inc(s("pool_passed"), 1)
                        w = W[u % 4][:, off:off + P]
                        pool.affine_select(out=w, in_=w, compare_op=ALU.is_gt, fill=0.0, base=0,
                                           pattern=[[1, P]], channel_multiplier=-1)
                    pool.drain().then_inc(s("cut"), 1)
                pair_end(pool, i)

        @block.scalar
        def _(act):
            with act.Fori(0, PAIRS) as i:
                act.preload_act_table_set(EXP_LN)
                act.wait_ge(s("in_k"), i * 64 + 64)
                act.wait_ge(s("in_q"), i * 64 + 64)
                for h in range(2):
                    act.copy(kS[h][:], kd[h][:]).then_inc(s("k_high"), 1)
                    act.activation(qH[h][:], qd[h][:], ACT.Copy, scale=DH ** -0.5).then_inc(s("q_high"), 1)
                for n in range(2):
                    act.wait_ge(s("v_mm"), i * 2 + n + 1)
                    act.copy(vn[:, 4 * n:4 * n + 4, :], Z[n][:].rearrange("p (j f) -> p j f", f=P)).then_inc(s("v"), 1)

                def exp_of_z(u):
                    act.wait_ge(s("z"), i * NU + u + 1)
                    if u >= 4:
                        act.wait_ge(s("sp"), i * NU + u - 3)
                    act.activation(E[u % 4][:, span(u)], Z[u % NZ][:, span(u)], ACT.Exp).then_inc(s("exp"), 1)

                def log_of_e(u):
                    act.wait_ge(s("capped"), i * NU + u + 1)
                    act.activation(E[u % 4][:, span(u)], E[u % 4][:, span(u)], ACT.Ln, bias=1.0).then_inc(s("log"), 1)

                def weight(u):
                    act.wait_ge(s("tri_mm"), i * NU + u + 1)
                    if u >= 4:
                        act.wait_ge(s("v_mul"), i * NU + u - 3)
                    act.activation(W[u % 4][:, span(u)], Z[u % NZ][:, span(u)], ACT.Exp).then_inc(s("weight"), 1)

                for u in range(-AHEAD, NU):
                    if u + AHEAD < NU:
                        exp_of_z(u + AHEAD)
                    if u >= 0:
                        weight(u)
                    if u + AHEAD < NU:
                        log_of_e(u + AHEAD)
                for h in range(2):
                    for c in range(QC):
                        act.wait_ge(s("v_mul"), i * NU + NU)
                        act.copy(O[:, PER * c:PER * (c + 1), DH * h:DH * h + DH],
                                 OB[h][c][:, 0:PER * DH].rearrange("p (j v) -> p j v", v=DH)).then_inc(s("o"), 1)
                act.wait_ge(s("o"), i * 4 + 4)
                act.activation(osq[:], O[:], ACT.Square).then_inc(s("osq"), 1)
                act.wait_ge(s("mean"), i + 1)
                act.activation(small[:, 0, :], small[:, 0, :], ACT.Sqrt).then_inc(s("root"), 1)
                act.wait_ge(s("gain"), i + 1)
                for n in range(2):
                    act.wait_ge(s("back"), i * 2 + n + 1)
                    act.activation(outT[:, n * HALF:(n + 1) * HALF], Z[n][:], ACT.Copy, scale=small_gain[:]
                                   ).then_inc(s("mixed"), 1)
                pair_end(act, i)

        @block.vector
        def _(dve):
            dve.tensor_scalar(tri[:], mask["to_diag"], -1.0, None, ALU.mult)
            dve.tensor_scalar(ones[:], mask["ones"], -1.0, None, ALU.mult).then_inc(s("signs"), 1)
            with dve.Fori(0, PAIRS) as i:
                dve.tensor_copy(small_gain[:], col[:, bass.ds(i + COL["sb_norm_g"], 1)]).then_inc(s("gain"), 1)
                for h in range(2):
                    dve.wait_ge(s("k_high"), i * 2 + h + 1)
                    dve.tensor_tensor(kS[h][DH:P, :], kd[h][DH:P, :], kS[h][DH:P, :].bitcast(F32), ALU.subtract
                                      ).then_inc(s("k"), 1)
                    dve.wait_ge(s("q_high"), i * 2 + h + 1)
                    dve.scalar_tensor_tensor(qL[h][:], qd[h][:], DH ** -0.5, qH[h][:].bitcast(F32),
                                             ALU.mult, ALU.subtract).then_inc(s("q"), 1)

                def cap(u):
                    dve.wait_ge(s("exp"), i * NU + u + 1)
                    dve.tensor_scalar(E[u % 4][:, span(u)], E[u % 4][:, span(u)], CAP, None, ALU.min
                                      ).then_inc(s("capped"), 1)

                def softplus(u):
                    h, c, kb, off, first = UNITS[u]
                    dve.wait_ge(s("log"), i * NU + u + 1)
                    if u >= 4:
                        dve.wait_ge(s("tri_mm"), i * NU + u - 3)
                        dve.wait_ge(s("sum"), i * NU + u - 3)
                    diag = kb >= PER * c
                    m = dve.tensor_tensor(SP[u % 4][:, span(u)], Z[u % NZ][:, span(u)], E[u % 4][:, span(u)], ALU.max)
                    if diag:
                        m.then_inc(s("diag"), 1)
                        D = sum(1 for x in UNITS[:u + 1] if x[2] >= PER * x[1])
                        ND = sum(1 for x in UNITS if x[2] >= PER * x[1])
                        dve.wait_ge(s("diag"), i * ND + D)
                        w = SP[u % 4][:, off:off + P]
                        m = dve.tensor_tensor(w, w, mask["above"], ALU.mult)
                    m.then_inc(s("sp"), 1)

                for u in range(NU):
                    cap(u)
                    softplus(u)
                dve.wait_ge(s("osq"), i + 1)
                dve.tensor_reduce(small[:, 0, :], osq[:].rearrange("p j (h v) -> p (j h) v", v=DH), AX.X, ALU.add
                                  ).then_inc(s("ssum"), 1)
                dve.wait_ge(s("ssum"), i + 1)
                dve.tensor_scalar(small[:, 0, :], small[:, 0, :], 1.0 / DH, EPS, ALU.mult, ALU.add).then_inc(s("mean"), 1)
                dve.wait_ge(s("root"), i + 1)
                dve.reciprocal(small[:, 1, :], small[:, 0, :]).then_inc(s("rstd"), 1)
                dve.wait_ge(s("rstd"), i + 1)
                o3 = O[:].rearrange("p j (h v) -> p (j h) v", v=DH)
                dve.tensor_tensor(o3, o3, small[:, 1, :].unsqueeze(2).to_broadcast([P, 2 * TB, DH]), ALU.mult
                                  ).then_inc(s("normed"), 1)
                pair_end(dve, i)

        @block.tensor
        def _(pe):
            pe.wait_ge(s("signs"), 1)
            with pe.Fori(0, PAIRS) as i:
                pe.wait_ge(s("in_v"), i * 16 + 16)
                for n in range(2):
                    for j in range(4):
                        m = pe.transpose(Z[n][:, j * P:(j + 1) * P], vp[:, (4 * n + j) * P:(4 * n + j + 1) * P], ident[:])
                    m.then_inc(s("v_mm"), 1)
                pe.wait_ge(s("k"), i * 2 + 2)
                pe.wait_ge(s("q"), i * 2 + 2)
                pe.wait_ge(s("v"), i * 2 + 2)

                def scores(u):
                    h, c, kb, off, first = UNITS[u]
                    if u >= NZ:
                        pe.wait_ge(s("weight"), i * NU + u - NZ + 1)
                    qs = slice(c * HALF + off, (c + 1) * HALF)
                    pe.matmul(Z[u % NZ][:, span(u)], kS[h][:, kb * P:(kb + 1) * P], qL[h][:, qs], start=True, stop=False)
                    pe.matmul(Z[u % NZ][:, span(u)], kS[h][:, kb * P:(kb + 1) * P], qH[h][:, qs], start=False, stop=True
                              ).then_inc(s("z"), 1)

                nth = [0, 0]

                def sums(u):
                    h, c, kb, off, first = UNITS[u]
                    rd = R[h][nth[h] % 2]
                    nth[h] += 1
                    pe.wait_ge(s("sp"), i * NU + u + 1)
                    z = Z[u % NZ][:, span(u)]
                    m = pe.matmul(z, tri[:], SP[u % 4][:, span(u)], start=False, stop=True, skip_group_check=True)
                    if not first:
                        pe.wait_ge(s("cut"), i * NU + u - 1)
                        m = pe.matmul(z, ones[:], rd[:, span(u)], start=False, stop=True, skip_group_check=True)
                    m.then_inc(s("tri_mm"), 1)

                opened = set()

                def values(u):
                    h, c, kb, off, first = UNITS[u]
                    pe.wait_ge(s("cut"), i * NU + u + 1)
                    pe.wait_ge(s("weight"), i * NU + u + 1)
                    for j in range(off // P, PER):
                        m = pe.matmul(OB[h][c][:, j * DH:(j + 1) * DH], W[u % 4][:, j * P:(j + 1) * P],
                                      vn[:, kb, DH * h:DH * h + DH], start=(h, c) not in opened, stop=True,
                                      skip_group_check=True)
                        opened.add((h, c))
                    m.then_inc(s("v_mul"), 1)

                for u in range(-AHEAD, NU + 1):
                    if u + AHEAD < NU:
                        scores(u + AHEAD)
                    if 0 <= u < NU:
                        sums(u)
                    if u >= 1:
                        values(u - 1)
                pe.wait_ge(s("normed"), i + 1)
                for n in range(2):
                    for j in range(4):
                        m = pe.transpose(Z[n][:, j * P:(j + 1) * P], O[:, 4 * n + j, :], ident[:])
                    m.then_inc(s("back"), 1)
                pair_end(pe, i)


def hybrid_block(nc, args, out):
    proj = nc.dram_tensor("projected", [IN_W, T], F32, kind="Internal").ap()
    mixed = nc.dram_tensor("mixed", [MIX, T], F32, kind="Internal").ap()
    x1 = nc.dram_tensor("x_after_mixers", [T, D], F32, kind="Internal").ap()
    with ExitStack() as st:
        r = Region(nc, st, "all")
        con = {"ident": r.sb("ident", [P, P]), "col": r.sb("col", [P, P])}
        with ExitStack() as mixers:
            m = Region(nc, mixers, "mix")
            con["masks"], con["levels"] = m.sb("masks", [P, len(MASKS), P]), m.sb("levels", [P, 6, P])
            constants(nc, con, args)
            projection(nc, con, args["x"], args["w_in"], proj)
            rwkv(nc, con, args, proj, mixed)
            gla(nc, con, args, proj, mixed)
            stick_breaking(nc, con, args, proj, mixed)
        hH, hL = r.sb("hH", [P, KB, T], F32R), r.sb("hL", [P, KB, T], F32R)
        output_projection(nc, con, args["x"], mixed, args["w_out"], args["post_mix_g"], args["pre_ffn_g"],
                          x1, hH, hL)
        feed_forward(nc, con, x1, args["w_ff1"], args["w_ff2"], args["post_ffn_g"], hH, hL, out)


_INS = ["x", "pre_mix_g", "w_in", "sb_norm_g", "rw_mu", "rw_w0", "rw_w_up", "rw_a0", "rw_a_up", "rw_g_up",
        "rw_k_k", "rw_k_a", "rw_r_k", "rw_gn_g", "rw_gn_b", "gla_gate_up", "gla_gate_b", "gla_norm_g",
        "w_out", "post_mix_g", "pre_ffn_g", "w_ff1", "w_ff2", "post_ffn_g"]


def kernel(**inputs):
    import numpy as np
    import concourse.bacc as bacc
    from concourse.bass_utils import run_bass_kernel_spmd

    nc = bacc.Bacc("TRN2", target_bir_lowering=False, num_devices=1)
    arrays, args = {}, {}
    for name in _INS:
        a = np.ascontiguousarray(inputs[name])
        arrays[f"in_{name}"] = a
        args[name] = nc.dram_tensor(f"in_{name}", a.shape, mybir.dt.from_np(a.dtype), kind="ExternalInput").ap()
    out = nc.dram_tensor("out_x", [1, T, D], F32, kind="ExternalOutput").ap()
    hybrid_block(nc, args, out)
    r = run_bass_kernel_spmd(nc, [arrays], core_ids=[0])
    return r.results[0]["out_x"]
```

```python
from contextlib import ExitStack

import concourse.bass as bass
from concourse import mybir

ALU = mybir.AluOpType
ACT = mybir.ActivationFunctionType
AX = mybir.AxisListType
F32 = mybir.dt.float32
F32R = mybir.dt.float32r
U32 = mybir.dt.uint32

P = 128
D = 1024
T = 1024
KB = D // P
TB = T // P
HALF = 512
NH = T // HALF
SBW = 384
RWW = 384
PAIRS = 3
IN_W = 3216
MIX = 1024
DFF = 4096
EPS = 1e-6
EXP_LN = "natural_log_exp_and_others"
GN_EPS = 64e-5
C = 64

SB_Q, SB_K, SB_V = 0, 384, 768
RW_R, RW_K, RW_V, RW_LOW = 1152, 1536, 1920, 2304
GLA_Q, GLA_K, GLA_V, GLA_GD, GLA_G = 2432, 2560, 2688, 2944, 2960

PARAMS = (("pre_mix_g", 8), ("sb_norm_g", 3), ("rw_w0", 3), ("rw_a0", 3), ("rw_k_k", 3), ("rw_k_a", 3),
          ("rw_r_k", 3), ("rw_gn_g", 3), ("rw_gn_b", 3), ("rw_mu", 10), ("gla_gate_b", 1), ("gla_norm_g", 2))
RW_COLS = ("w0", "a0", "k_k", "k_a", "r_k", "gn_g", "gn_b", "mu_r", "mu_k", "mu_v")


def param_columns():
    at, out = 0, {}
    for name, n in PARAMS:
        out[name] = at
        at += n
    return out, at


COL, NCOL = param_columns()


class Region:

    def __init__(self, nc, stack, tag):
        self.nc, self.stack, self.tag = nc, stack, tag
        self.semaphores, self.numbers = ExitStack(), []
        stack.callback(self.clear)

    def sb(self, name, shape, dt=F32):
        return self.stack.enter_context(self.nc.sbuf_tensor(f"{self.tag}_{name}", shape, dt))

    def bank(self, name, cols=HALF):
        return self.stack.enter_context(self.nc.psum_tensor(f"{self.tag}_ps_{name}", [P, cols], F32))

    def sem(self, name):
        got = self.semaphores.enter_context(self.nc.semaphore(f"{self.tag}_{name}"))
        self.numbers.append(got.num)
        return got

    def clear(self):
        if self.numbers:
            runs = []
            for n in sorted(self.numbers):
                if runs and runs[-1].stop == n:
                    runs[-1] = range(runs[-1].start, n + 1)
                else:
                    runs.append(range(n, n + 1))
            with self.nc.Block() as block:
                @block.sync
                def _(sp):
                    for run in runs:
                        sp.sem_clear(run)
        self.semaphores.close()


MASKS = ("ones", "above", "from_diag", "below", "to_diag", "same16", "same32", "same64",
         "up16", "up64", "upd64", "low16", "low32", "low64")


def constants(nc, con, args):
    ident, masks = con["ident"], con["masks"]
    m = {name: masks[:, n, :] for n, name in enumerate(MASKS)}
    levels = con["levels"]
    with ExitStack() as st:
        r = Region(nc, st, "con")
        rows = r.sb("rows", [P, P])
        same = [r.sb(f"same{n}", [P, P]) for n in range(2)]
        colp = r.bank("colp")
        loaded, zeroed, filled = r.sem("loaded"), r.sem("zeroed"), r.sem("filled")
        turned, made, cut = r.sem("turned"), r.sem("made"), r.sem("cut")
        block = st.enter_context(nc.Block())

        @block.sync
        def _(sp):
            sp.wait_ge(zeroed, 2)
            for name, n in PARAMS:
                at = COL[name]
                sp.dma_start(rows[at:at + n, :],
                             args[name].rearrange("l (n p) -> (l n) p", p=P)).then_inc(loaded, 16)

        @block.gpsimd
        def _(pool):
            pool.memset(ident[:], 0.0).then_inc(zeroed, 1)
            pool.memset(rows[:], 0.0).then_inc(zeroed, 1)
            pool.wait_ge(zeroed, 2)
            pool.affine_select(out=ident[:], in_=ident[:], compare_op=ALU.not_equal, fill=1.0, base=0,
                               pattern=[[-1, P]], channel_multiplier=1).then_inc(filled, 1)
            pool.memset(m["ones"], 1.0).then_inc(made, 1)
            done = [1]

            def select(out, in_, compare, base, pattern, step):
                pool.wait_ge(made, done[0])
                pool.affine_select(out=out, in_=in_, compare_op=compare, fill=0.0, base=base,
                                   pattern=pattern, channel_multiplier=step).then_inc(made, 1)
                done[0] += 1

            select(m["above"], m["ones"], ALU.is_gt, 0, [[1, P]], -1)
            select(m["from_diag"], m["ones"], ALU.is_ge, 0, [[1, P]], -1)
            select(m["below"], m["ones"], ALU.is_gt, 0, [[-1, P]], 1)
            select(m["to_diag"], m["ones"], ALU.is_ge, 0, [[-1, P]], 1)

            def blocks(out, size):
                n = P // size
                o = out.rearrange("p (n s) -> p n s", s=size)
                select(o, m["ones"].rearrange("p (n s) -> p n s", s=size), ALU.is_ge, 0, [[-size, n], [0, size]], 1)
                select(o, o, ALU.is_ge, size - 1, [[size, n], [0, size]], -1)

            for size in (16, 32, 64):
                blocks(m[f"same{size}"], size)
            for n in range(6):
                if n >= 1:
                    pool.wait_ge(cut, 2 * n)
                blocks(same[n % 2][:], 2 << n)

        @block.tensor
        def _(pe):
            pe.wait_ge(loaded, 16 * len(PARAMS))
            pe.wait_ge(filled, 1)
            pe.transpose(colp[:, 0:P], rows[:], ident[:]).then_inc(turned, 1)

        @block.vector
        def _(dve):
            SELECTS = 5 + 6
            for n in range(6):
                dve.wait_ge(made, SELECTS + 2 * (n + 1))
                before = ident[:] if n == 0 else same[(n - 1) % 2][:]
                dve.tensor_tensor(levels[:, n, :], same[n % 2][:], before, ALU.subtract).then_inc(cut, 1)
                dve.wait_ge(cut, 2 * n + 1)
                dve.tensor_tensor(levels[:, n, :], levels[:, n, :], m["above"], ALU.mult).then_inc(cut, 1)
            done = 12
            for name, a, b, op in (("up16", "same16", "above", ALU.mult), ("up64", "same64", "above", ALU.mult),
                                   ("upd64", "same64", "from_diag", ALU.mult),
                                   ("low16", "same16", "below", ALU.mult),
                                   ("low64", "same64", "same32", ALU.subtract),
                                   ("low32", "same32", "same16", ALU.subtract),
                                   ("low64", "low64", "below", ALU.mult),
                                   ("low32", "low32", "below", ALU.mult)):
                dve.wait_ge(cut, done)
                dve.tensor_tensor(m[name], m[a], m[b], op).then_inc(cut, 1)
                done += 1
            dve.wait_ge(turned, 1)
            dve.tensor_copy(con["col"][:], colp[:, 0:P]).then_inc(cut, 1)


def projection(nc, con, x, w_in, proj):
    ident, col = con["ident"], con["col"]
    PAIRED = IN_W // (2 * P)
    REST = IN_W - PAIRED * 2 * P
    NARROW = REST - P
    with ExitStack() as st:
        r = Region(nc, st, "prj")
        xt = r.sb("xt", [P, TB, D])
        sq = r.sb("sq", [P, D])
        ss, rs = r.sb("ss", [P, TB]), r.sb("rs", [P, TB])
        hH, hL = r.sb("hH", [P, KB, T], F32R), r.sb("hL", [P, KB, T], F32R)
        raw = [r.sb(f"raw{s}", [P, KB, P]) for s in range(2)]
        wH = [r.sb(f"wH{s}", [P, KB, P], F32R) for s in range(2)]
        wL = [r.sb(f"wL{s}", [P, KB, P], F32R) for s in range(2)]
        stage = [r.sb(f"stage{s}", [P, T]) for s in range(2)]
        tbank = [r.bank(f"tb{i}") for i in range(4)]
        bank = [[r.bank(f"b{s}{h}") for h in range(NH)] for s in range(2)]
        x_in = [r.sem(f"x_in{j}") for j in range(TB)]
        squared, rooted, scaled = r.sem("squared"), r.sem("rooted"), r.sem("scaled")
        rdone = r.sem("rdone")
        turned, high, low = r.sem("turned"), r.sem("high"), r.sem("low")
        w_in_s = [r.sem(f"w_in{s}") for s in range(2)]
        w_high, w_low = [r.sem(f"w_high{s}") for s in range(2)], [r.sem(f"w_low{s}") for s in range(2)]
        multiplied = [r.sem(f"mul{s}") for s in range(2)]
        ev0, ev1 = [r.sem(f"ev0_{s}") for s in range(2)], [r.sem(f"ev1_{s}") for s in range(2)]
        stored = [r.sem(f"stored{s}") for s in range(2)]
        x_d = x.rearrange("b (j p) d -> (b j) p d", p=P)
        w_d = w_in.rearrange("l (k p) n -> p (l k) n", p=P)
        block = st.enter_context(nc.Block())

        @block.sync
        def _(sp):
            for j in range(TB):
                sp.dma_start(xt[:, j, :], x_d[j]).then_inc(x_in[j], 16)
            for s in range(2):
                sp.sem_inc(stored[s], 16)
                sp.dma_start(raw[s][:], w_d[:, :, s * P:(s + 1) * P]).then_inc(w_in_s[s], 16)
            def load(s, i, at, n):
                sp.wait_ge(w_high[s], i + 1)
                sp.wait_ge(w_low[s], i + 1)
                sp.dma_start(raw[s][:, :, 0:n], w_d[:, :, bass.ds(at, n)]).then_inc(w_in_s[s], 16)

            def store(s, i, at, n):
                sp.wait_ge(ev0[s], i + 2)
                sp.wait_ge(ev1[s], i + 2)
                sp.dma_start(proj[bass.ds(at, n), :], stage[s][0:n, :]).then_inc(stored[s], 16)

            with sp.Fori(0, PAIRED - 1) as i:
                for s in range(2):
                    load(s, i + 1, (i + 1) * 2 * P + s * P, P)
                for s in range(2):
                    store(s, i, i * 2 * P + s * P, P)
            for s, n in ((0, P), (1, NARROW)):
                load(s, PAIRED, PAIRED * 2 * P + s * P, n)
            for s in range(2):
                store(s, PAIRED - 1, (PAIRED - 1) * 2 * P + s * P, P)
            for s, n in ((0, P), (1, NARROW)):
                store(s, PAIRED, PAIRED * 2 * P + s * P, n)
            for s in range(2):
                sp.wait_ge(stored[s], 16 * (PAIRED + 2))

        @block.scalar
        def _(act):
            for s in range(2):
                act.sem_inc(w_high[s], 1)
                act.sem_inc(ev0[s], 1)
            for j in range(TB):
                act.wait_ge(x_in[j], 16)
                if j:
                    act.wait_ge(squared, j)
                act.activation(sq[:], xt[:, j, :], ACT.Square, accum_out=ss[:, j:j + 1]).then_inc(squared, 1)
            act.wait_ge(rdone, 1)
            act.activation(rs[:], rs[:], ACT.Sqrt).then_inc(rooted, 1)
            for g in range(KB * NH):
                kb, h = g // NH, g % NH
                act.wait_ge(turned, g + 1)
                act.activation(hH[:, kb, h * HALF:(h + 1) * HALF], tbank[g % 4][:], ACT.Copy,
                               scale=col[:, COL["pre_mix_g"] + kb:COL["pre_mix_g"] + kb + 1]).then_inc(high, 1)

            def block_work(s, i, n):
                act.wait_ge(w_in_s[s], i * 16 + 16)
                act.wait_ge(multiplied[s], i + 1)
                act.copy(wH[s][:, :, 0:n], raw[s][:, :, 0:n]).then_inc(w_high[s], 1)

            def take(s, i, n):
                act.wait_ge(multiplied[s], i + 2)
                act.wait_ge(stored[s], i * 16 + 16)
                act.copy(stage[s][0:n, 0:HALF], bank[s][0][0:n, :]).then_inc(ev0[s], 1)

            block_work(0, 0, P)
            block_work(1, 0, P)
            with act.Fori(0, PAIRED - 1) as i:
                for s in range(2):
                    take(s, i, P)
                    block_work(s, i + 1, P)
            for s, n in ((0, P), (1, NARROW)):
                take(s, PAIRED - 1, P)
                block_work(s, PAIRED, n)
            for s, n in ((0, P), (1, NARROW)):
                take(s, PAIRED, n)

        @block.vector
        def _(dve):
            for s in range(2):
                dve.sem_inc(w_low[s], 1)
                dve.sem_inc(ev1[s], 1)
            dve.wait_ge(squared, TB)
            dve.tensor_scalar(rs[:], ss[:], 1.0 / D, EPS, ALU.mult, ALU.add).then_inc(rdone, 1)
            dve.wait_ge(rooted, 1)
            dve.reciprocal(rs[:], rs[:]).then_inc(rdone, 1)
            dve.wait_ge(rdone, 2)
            for j in range(TB):
                dve.tensor_scalar(xt[:, j, :], xt[:, j, :], rs[:, j:j + 1], None, ALU.mult).then_inc(scaled, 1)
            for g in range(KB * NH):
                kb, h = g // NH, g % NH
                dve.wait_ge(high, g + 1)
                hs = slice(h * HALF, (h + 1) * HALF)
                dve.scalar_tensor_tensor(hL[:, kb, hs], tbank[g % 4][:],
                                         col[:, COL["pre_mix_g"] + kb:COL["pre_mix_g"] + kb + 1],
                                         hH[:, kb, hs].bitcast(F32), ALU.mult, ALU.subtract).then_inc(low, 1)

            def split_low(s, i, n):
                dve.wait_ge(w_high[s], i + 2)
                dve.wait_ge(multiplied[s], i + 1)
                dve.tensor_tensor(wL[s][:, :, 0:n], raw[s][:, :, 0:n], wH[s][:, :, 0:n].bitcast(F32),
                                  ALU.subtract).then_inc(w_low[s], 1)

            def take(s, i, n):
                dve.wait_ge(multiplied[s], i + 2)
                dve.wait_ge(stored[s], i * 16 + 16)
                dve.tensor_copy(stage[s][0:n, HALF:T], bank[s][1][0:n, :]).then_inc(ev1[s], 1)

            split_low(0, 0, P)
            split_low(1, 0, P)
            with dve.Fori(0, PAIRED - 1) as i:
                for s in range(2):
                    take(s, i, P)
                    split_low(s, i + 1, P)
            for s, n in ((0, P), (1, NARROW)):
                take(s, PAIRED - 1, P)
                split_low(s, PAIRED, n)
            for s, n in ((0, P), (1, NARROW)):
                take(s, PAIRED, n)

        @block.tensor
        def _(pe):
            for s in range(2):
                pe.sem_inc(multiplied[s], 1)
            pe.wait_ge(scaled, TB)
            for g in range(KB * NH):
                kb, h = g // NH, g % NH
                if g >= 4:
                    pe.wait_ge(low, g - 3)
                for q in range(4):
                    j = h * 4 + q
                    m = pe.transpose(tbank[g % 4][:, q * P:(q + 1) * P], xt[:, j, kb * P:(kb + 1) * P], ident[:])
                m.then_inc(turned, 1)
            pe.wait_ge(low, KB * NH)

            def products(s, i, n):
                pe.wait_ge(w_low[s], i + 2)
                pe.wait_ge(ev0[s], i + 1)
                pe.wait_ge(ev1[s], i + 1)
                for h in range(NH):
                    hs = slice(h * HALF, (h + 1) * HALF)
                    for kb in range(KB):
                        for q, (w, a) in enumerate(((wL, hH), (wH, hL), (wH, hH))):
                            m = pe.matmul(bank[s][h][0:n, :] if n == P else bank[s][h][:, :],
                                          w[s][:, kb, 0:P], a[:, kb, hs],
                                          start=(kb == 0 and q == 0), stop=(kb == KB - 1 and q == 2))
                m.then_inc(multiplied[s], 1)

            with pe.Fori(0, PAIRED) as i:
                for s in range(2):
                    products(s, i, P)
            products(0, PAIRED, P)
            products(1, PAIRED, NARROW)


def broadcast_rows(ap, n=P):
    return ap.to_broadcast((n, ap.shape[1]))


def output_projection(nc, con, x, mixed, w_out, post_g, pre_g, x1, hH, hL):
    ident = con["ident"]
    with ExitStack() as st:
        r = Region(nc, st, "out")
        raw = [r.sb(f"raw{s}", [P, D]) for s in range(4)]
        mH, mL = r.sb("mH", [P, KB, T], F32R), r.sb("mL", [P, KB, T], F32R)
        wH, wL = r.sb("wH", [P, KB, D // 2], F32R), r.sb("wL", [P, KB, D // 2], F32R)
        half0 = r.sb("half0", [P, TB, HALF])
        y, xt = raw[0:2], raw[2:4]
        postB, preB = r.sb("postB", [P, D]), r.sb("preB", [P, D])
        ss = r.sb("ss", [P, TB, 4])
        bank = [r.bank(f"b{i}") for i in range(4)]
        tbank = [r.bank(f"tb{i}") for i in range(4)]
        raw_in = [r.sem(f"raw_in{s}") for s in range(4)]
        gains = r.sem("gains")
        x_in = [r.sem(f"x_in{s}") for s in range(2)]
        high, low = r.sem("high"), r.sem("low")
        multiplied, kept, squared = r.sem("multiplied"), r.sem("kept"), r.sem("squared")
        mean, root, inv = r.sem("mean"), r.sem("root"), r.sem("inv")
        added, squared1 = r.sem("added"), r.sem("squared1")
        normed, turned, hhigh, hlow, stored = (r.sem("normed"), r.sem("turned"), r.sem("hhigh"),
                                               r.sem("hlow"), r.sem("stored"))
        x_d = x.rearrange("b (j p) d -> (b j) p d", p=P)
        x1_d = x1.rearrange("(j p) d -> j p d", p=P)
        m_d = mixed.rearrange("(k p) t -> k p t", p=P)
        w_d = w_out.rearrange("l (k p) n -> (l k) p n", p=P)
        pieces = [("m", k) for k in range(KB)] + [("w0", k) for k in range(KB)] + [("w1", k) for k in range(KB)]
        block = st.enter_context(nc.Block())

        def piece(n):
            kind, k = pieces[n]
            width = T if kind == "m" else HALF
            src = raw[n % 4][:, 0:width]
            if kind == "m":
                return src, mH[:, k, :], mL[:, k, :]
            return src, wH[:, k, :], wL[:, k, :]

        @block.sync
        def _(sp):
            for n, (kind, k) in enumerate(pieces):
                if n >= 4:
                    sp.wait_ge(low, n - 3)
                if kind == "m":
                    sp.dma_start(raw[n % 4][:], m_d[k]).then_inc(raw_in[n % 4], 16)
                else:
                    c = int(kind[1]) * HALF
                    sp.dma_start(raw[n % 4][:, 0:HALF], w_d[k][:, c:c + HALF]).then_inc(raw_in[n % 4], 16)
                if n == 3:
                    sp.dma_start(postB[:], broadcast_rows(post_g)).then_inc(gains, 16)
                    sp.dma_start(preB[:], broadcast_rows(pre_g)).then_inc(gains, 16)
            sp.wait_ge(low, len(pieces))
            for j in range(TB):
                if j >= 2:
                    sp.wait_ge(normed, j - 1)
                    sp.wait_ge(stored, 16 * (j - 1))
                sp.dma_start(xt[j % 2][:], x_d[j]).then_inc(x_in[j % 2], 16)
                if j:
                    sp.wait_ge(added, j)
                    sp.dma_start(x1_d[j - 1], xt[(j - 1) % 2][:]).then_inc(stored, 16)
            sp.wait_ge(added, TB)
            sp.dma_start(x1_d[TB - 1], xt[(TB - 1) % 2][:]).then_inc(stored, 16)
            sp.wait_ge(stored, 16 * TB)

        @block.scalar
        def _(act):
            for n in range(len(pieces)):
                act.wait_ge(raw_in[n % 4], 16 * (n // 4 + 1))
                if n == 2 * KB:
                    act.wait_ge(multiplied, TB)
                src, dst, _ = piece(n)
                act.copy(dst, src).then_inc(high, 1)
            for j in range(TB):
                ys = y[j % 2]
                act.wait_ge(kept, j + 1)
                if j == 0:
                    act.wait_ge(low, len(pieces))
                act.activation(ys[:, 0:HALF], half0[:, j, :], ACT.Square,
                               accum_out=ss[:, j, 0:1]).then_inc(squared, 1)
                act.wait_ge(multiplied, TB + j + 1)
                act.activation(ys[:, HALF:D], bank[j % 4][:], ACT.Square,
                               accum_out=ss[:, j, 1:2]).then_inc(squared, 1)
                act.wait_ge(mean, 2 * j + 1)
                act.activation(ss[:, j, 0:1], ss[:, j, 0:1], ACT.Sqrt).then_inc(root, 1)
                act.wait_ge(added, j + 1)
                act.activation(ys[:], xt[j % 2][:], ACT.Square, accum_out=ss[:, j, 2:3]).then_inc(squared1, 1)
                act.wait_ge(mean, 2 * j + 2)
                act.activation(ss[:, j, 2:3], ss[:, j, 2:3], ACT.Sqrt).then_inc(root, 1)
                for b in range(2):
                    act.wait_ge(turned, 2 * j + b + 1)
                    act.copy(hH[:, 4 * b:4 * b + 4, j * P:(j + 1) * P],
                             tbank[(2 * j + b) % 4][:].rearrange("p (k t) -> p k t", k=4)).then_inc(hhigh, 1)

        @block.vector
        def _(dve):
            for n in range(2 * KB):
                dve.wait_ge(high, n + 1)
                src, h, l = piece(n)
                dve.tensor_tensor(l, src, h.bitcast(F32), ALU.subtract).then_inc(low, 1)
            for j in range(TB):
                dve.wait_ge(multiplied, j + 1)
                dve.tensor_copy(half0[:, j, :], bank[j % 4][:]).then_inc(kept, 1)
            for n in range(2 * KB, 3 * KB):
                dve.wait_ge(high, n + 1)
                src, h, l = piece(n)
                dve.tensor_tensor(l, src, h.bitcast(F32), ALU.subtract).then_inc(low, 1)
            dve.wait_ge(gains, 32)
            done = 0
            for j in range(TB):
                ys, xs = y[j % 2], xt[j % 2]
                s0, s1, s2 = ss[:, j, 0:1], ss[:, j, 1:2], ss[:, j, 2:3]

                dve.wait_ge(squared, 2 * j + 2)
                dve.tensor_tensor(s0, s0, s1, ALU.add).then_inc(inv, 1)
                dve.wait_ge(inv, done + 1)
                dve.tensor_scalar(s0, s0, 1.0 / D, EPS, ALU.mult, ALU.add).then_inc(mean, 1)
                dve.wait_ge(root, 2 * j + 1)
                dve.reciprocal(s0, s0).then_inc(inv, 1)
                dve.wait_ge(inv, done + 2)
                dve.scalar_tensor_tensor(ys[:, 0:HALF], half0[:, j, :], s0, postB[:, 0:HALF],
                                         ALU.mult, ALU.mult).then_inc(inv, 1)
                dve.scalar_tensor_tensor(ys[:, HALF:D], bank[j % 4][:], s0, postB[:, HALF:D],
                                         ALU.mult, ALU.mult).then_inc(inv, 1)
                dve.wait_ge(inv, done + 4)
                dve.wait_ge(x_in[j % 2], 16 * (j // 2 + 1))
                dve.tensor_tensor(xs[:], xs[:], ys[:], ALU.add).then_inc(added, 1)
                dve.wait_ge(squared1, j + 1)
                dve.tensor_scalar(s2, s2, 1.0 / D, EPS, ALU.mult, ALU.add).then_inc(mean, 1)
                dve.wait_ge(root, 2 * j + 2)
                dve.reciprocal(s2, s2).then_inc(inv, 1)
                dve.wait_ge(inv, done + 5)
                done += 5
                dve.scalar_tensor_tensor(ys[:], xs[:], s2, preB[:], ALU.mult, ALU.mult).then_inc(normed, 1)
                for b in range(2):
                    dve.wait_ge(hhigh, 2 * j + b + 1)
                    dst = slice(4 * b, 4 * b + 4)
                    dve.tensor_tensor(hL[:, dst, j * P:(j + 1) * P],
                                      tbank[(2 * j + b) % 4][:].rearrange("p (k t) -> p k t", k=4),
                                      hH[:, dst, j * P:(j + 1) * P].bitcast(F32), ALU.subtract).then_inc(hlow, 1)

        @block.tensor
        def _(pe):
            def product(half, j):
                n = half * TB + j
                b = bank[j % 4]
                if half == 0 and j >= 4:
                    pe.wait_ge(kept, j - 3)
                if half == 1 and j >= 4:
                    pe.wait_ge(normed, j - 3)
                if half == 1 and j == 0:
                    pe.wait_ge(kept, TB)
                for k in range(KB):
                    if j == 0:
                        pe.wait_ge(low, (half + 1) * KB + k + 1)
                    for q, (m, w) in enumerate(((mL, wH), (mH, wL), (mH, wH))):
                        i = pe.matmul(b[:], m[:, k, j * P:(j + 1) * P], w[:, k, :],
                                      start=(k == 0 and q == 0), stop=(k == KB - 1 and q == 2))
                i.then_inc(multiplied, 1)

            def turn(j):
                pe.wait_ge(normed, j + 1)
                for b in range(2):
                    n = 2 * j + b
                    if n >= 4:
                        pe.wait_ge(hlow, n - 3)
                    for k in range(4):
                        kb = 4 * b + k
                        i = pe.transpose(tbank[n % 4][:, k * P:(k + 1) * P],
                                         y[j % 2][:, kb * P:(kb + 1) * P], ident[:])
                    i.then_inc(turned, 1)

            for j in range(TB):
                product(0, j)
            for j in range(TB):
                product(1, j)
                if j >= 1:
                    turn(j - 1)
            turn(TB - 1)


def feed_forward(nc, con, x1, w1, w2, post_g, hH, hL, out):
    FB = 4
    NE = DFF // (FB * P)
    with ExitStack() as st:
        r = Region(nc, st, "ffn")
        raw1 = [r.sb(f"raw1_{s}", [P, KB, P]) for s in range(2)]
        w1H = [r.sb(f"w1H{s}", [P, KB, P], F32R) for s in range(2)]
        w1L = [r.sb(f"w1L{s}", [P, KB, P], F32R) for s in range(2)]
        raw2 = [r.sb(f"raw2_{s}", [P, D]) for s in range(2)]
        w2H, w2L = r.sb("w2H", [P, FB, D], F32R), r.sb("w2L", [P, FB, D], F32R)
        gH, gL = r.sb("gH", [P, FB, T], F32R), r.sb("gL", [P, FB, T], F32R)
        relu, g32 = r.sb("relu", [P, HALF]), r.sb("g32", [P, HALF])
        acc = r.sb("acc", [P, TB, D])
        postB = r.sb("postB", [P, D])
        ss = r.sb("ss", [P, TB])
        bank = [[r.bank(f"b{s}{h}") for h in range(NH)] for s in range(2)]
        ybank = [r.bank(f"y{i}") for i in range(4)]
        xt = [raw1[s][:].rearrange("p k c -> p (k c)") for s in range(2)]
        w1_in = [r.sem(f"w1_in{s}") for s in range(2)]
        w2_in = [r.sem(f"w2_in{s}") for s in range(2)]
        w1_high, w1_low = [r.sem(f"w1_high{s}") for s in range(2)], [r.sem(f"w1_low{s}") for s in range(2)]
        w2_high, w2_low = r.sem("w2_high"), r.sem("w2_low")
        hidden = [r.sem(f"hidden{s}") for s in range(2)]
        rectified, squared, g_high, g_low = r.sem("rectified"), r.sem("squared"), r.sem("g_high"), r.sem("g_low")
        summed, added, cleared, used = r.sem("summed"), r.sem("added"), r.sem("cleared"), r.sem("used")
        gains, x_in = r.sem("gains"), [r.sem(f"x_in{s}") for s in range(2)]
        ysq, mean, root, inv, final = r.sem("ysq"), r.sem("mean"), r.sem("root"), r.sem("inv"), r.sem("final")
        stored = r.sem("stored")
        w1_d = w1.rearrange("l (k p) n -> p (l k) n", p=P)
        w2_d = w2.rearrange("l (f p) n -> (l f) p n", p=P)
        x1_d = x1.rearrange("(j p) d -> j p d", p=P)
        o_d = out.rearrange("b (j p) d -> (b j) p d", p=P)
        w2_flat = w2.rearrange("l f n -> (l f) n")
        block = st.enter_context(nc.Block())
        G = TB * 2

        @block.sync
        def _(sp):
            sp.dma_start(postB[:], broadcast_rows(post_g)).then_inc(gains, 16)

            def load1(s, use, at):
                sp.wait_ge(w1_high[s], use + 1)
                sp.wait_ge(w1_low[s], use + 1)
                sp.dma_start(raw1[s][:], w1_d[:, :, bass.ds(at, P)]).then_inc(w1_in[s], 16)

            def load2(s, use, total, at):
                sp.wait_ge(w2_low, total)
                sp.dma_start(raw2[s][:], w2_flat[bass.ds(at, P), :]).then_inc(w2_in[s], 16)

            for s in range(2):
                load1(s, 0, s * P)

            def slice_loads(e, last):
                for i in range(FB):
                    load2(i % 2, e * 2 + i // 2, e * FB + i + 1, e * (FB * P) + i * P)
                    if i < 2:
                        load1(i, e * 2 + 1, e * (FB * P) + (i + 2) * P)
                    elif not last:
                        load1(i - 2, e * 2 + 2, e * (FB * P) + (i + 2) * P)

            with sp.Fori(0, NE - 1) as e:
                slice_loads(e, False)
            slice_loads(NE - 1, True)
            for j in range(TB):
                if j < 2:
                    sp.wait_ge(w1_high[j], 2 * NE + 1)
                    sp.wait_ge(w1_low[j], 2 * NE + 1)
                else:
                    sp.wait_ge(final, j - 1)
                sp.dma_start(xt[j % 2], x1_d[j]).then_inc(x_in[j % 2], 16)
                if j:
                    sp.wait_ge(final, j)
                    sp.dma_start(o_d[j - 1], acc[:, j - 1, :]).then_inc(stored, 16)
            sp.wait_ge(final, TB)
            sp.dma_start(o_d[TB - 1], acc[:, TB - 1, :]).then_inc(stored, 16)
            sp.wait_ge(stored, 16 * TB)

        W2_AT = {0: (0, 1), 1: (2,), 2: (3,), 3: ()}

        @block.scalar
        def _(act):
            for s in range(2):
                act.sem_inc(w1_high[s], 1)

            def split1(s, use):
                act.wait_ge(w1_in[s], use * 16 + 16)
                act.wait_ge(hidden[s], use + 1)
                act.copy(w1H[s][:], raw1[s][:]).then_inc(w1_high[s], 1)

            def split2(i, e):
                act.wait_ge(w2_in[i % 2], (e * 2 + i // 2) * 16 + 16)
                if i == 0:
                    act.wait_ge(used, e + 1)
                act.copy(w2H[:, i, :], raw2[i % 2][:]).then_inc(w2_high, 1)

            for s in range(2):
                split1(s, 0)

            def slice_work(e, last):
                for i in range(FB):
                    for m in W2_AT[i]:
                        split2(m, e)
                    act.wait_ge(hidden[i % 2], e * 2 + i // 2 + 2)
                    for h in range(NH):
                        n = e * (2 * FB) + 2 * i + h
                        act.activation(relu[:], bank[i % 2][h][:], ACT.Relu).then_inc(rectified, 1)
                        act.wait_ge(rectified, n + 1)
                        act.wait_ge(g_low, n + 1)
                        act.activation(g32[:], relu[:], ACT.Square).then_inc(squared, 1)
                        act.wait_ge(squared, n + 1)
                    if i < 2:
                        split1(i, e * 2 + 1)
                    elif not last:
                        split1(i - 2, e * 2 + 2)

            with act.Fori(0, NE - 1) as e:
                slice_work(e, False)
            slice_work(NE - 1, True)
            for j in range(TB):
                act.wait_ge(added, G * (NE - 1) + 2 * (j + 1) + 1)
                if j:
                    act.wait_ge(ysq, j)
                act.activation(raw2[0][:], acc[:, j, :], ACT.Square,
                               accum_out=ss[:, j:j + 1]).then_inc(ysq, 1)
                act.wait_ge(mean, j + 1)
                act.activation(ss[:, j:j + 1], ss[:, j:j + 1], ACT.Sqrt).then_inc(root, 1)

        @block.gpsimd
        def _(pool):
            pool.memset(acc[:], 0.0).then_inc(cleared, 1)

        @block.vector
        def _(dve):
            for s in range(2):
                dve.sem_inc(w1_low[s], 1)
            dve.sem_inc(w2_low, 2)
            dve.sem_inc(g_low, 1)
            dve.sem_inc(added, 1)
            dve.wait_ge(cleared, 1)

            def split1(s, use):
                dve.wait_ge(w1_high[s], use + 2)
                dve.wait_ge(hidden[s], use + 1)
                dve.tensor_tensor(w1L[s][:], raw1[s][:], w1H[s][:].bitcast(F32), ALU.subtract).then_inc(w1_low[s], 1)

            def split2(i, e):
                dve.wait_ge(w2_high, e * FB + i + 1)
                dve.tensor_tensor(w2L[:, i, :], raw2[i % 2][:], w2H[:, i, :].bitcast(F32),
                                  ALU.subtract).then_inc(w2_low, 1)

            for s in range(2):
                split1(s, 0)

            def slice_work(e, last):
                for i in range(FB):
                    for m in W2_AT[i]:
                        split2(m, e)
                    for h in range(NH):
                        n = e * (2 * FB) + 2 * i + h
                        hs = slice(h * HALF, (h + 1) * HALF)
                        dve.wait_ge(squared, n + 1)
                        dve.tensor_copy(gH[:, i, hs], g32[:]).then_inc(g_high, 1)
                        dve.wait_ge(g_high, n + 1)
                        dve.tensor_tensor(gL[:, i, hs], g32[:], gH[:, i, hs].bitcast(F32),
                                          ALU.subtract).then_inc(g_low, 1)
                    if i < 2:
                        split1(i, e * 2 + 1)
                    elif not last:
                        split1(i - 2, e * 2 + 2)
                for g in range(G):
                    j, dh = g // 2, g % 2
                    ds = slice(dh * HALF, (dh + 1) * HALF)
                    dve.wait_ge(summed, e * G + g + 1)
                    dve.tensor_tensor(acc[:, j, ds], acc[:, j, ds], ybank[g % 4][:], ALU.add).then_inc(added, 1)
                    if last and dh == 1 and j >= 1:
                        finish(j - 1)
                if last:
                    finish(TB - 1)

            def finish(j):
                s0 = ss[:, j:j + 1]
                if j == 0:
                    dve.wait_ge(gains, 16)
                dve.wait_ge(ysq, j + 1)
                dve.tensor_scalar(s0, s0, 1.0 / D, EPS, ALU.mult, ALU.add).then_inc(mean, 1)
                dve.wait_ge(root, j + 1)
                dve.reciprocal(s0, s0).then_inc(inv, 1)
                dve.wait_ge(inv, 2 * j + 1)
                dve.scalar_tensor_tensor(acc[:, j, :], acc[:, j, :], s0, postB[:], ALU.mult, ALU.mult).then_inc(inv, 1)
                dve.wait_ge(inv, 2 * j + 2)
                dve.wait_ge(x_in[j % 2], 16 * (j // 2 + 1))
                dve.tensor_tensor(acc[:, j, :], acc[:, j, :], xt[j % 2], ALU.add).then_inc(final, 1)

            with dve.Fori(0, NE - 1) as e:
                slice_work(e, False)
            slice_work(NE - 1, True)

        @block.tensor
        def _(pe):
            for s in range(2):
                pe.sem_inc(hidden[s], 1)
            pe.sem_inc(used, 1)

            def slice_products(e):
                for i in range(FB):
                    s = i % 2
                    pe.wait_ge(w1_low[s], e * 2 + i // 2 + 2)
                    if i >= 2:
                        pe.wait_ge(rectified, e * (2 * FB) + 2 * (i - 1))
                    for h in range(NH):
                        hs = slice(h * HALF, (h + 1) * HALF)
                        for k in range(KB):
                            for q, (w, a) in enumerate(((w1L, hH), (w1H, hL), (w1H, hH))):
                                m = pe.matmul(bank[s][h][:], w[s][:, k, :], a[:, k, hs],
                                              start=(k == 0 and q == 0), stop=(k == KB - 1 and q == 2))
                    m.then_inc(hidden[s], 1)
                for g in range(G):
                    j, dh = g // 2, g % 2
                    ts, ds = slice(j * P, (j + 1) * P), slice(dh * HALF, (dh + 1) * HALF)
                    pe.wait_ge(added, e * G + g - 2 if g >= 4 else e * G + 1)
                    for i in range(FB):
                        if g < 2:
                            pe.wait_ge(g_low, e * (2 * FB) + 2 * i + 3)
                            pe.wait_ge(w2_low, e * FB + i + 3)
                        for q, (a, w) in enumerate(((gL, w2H), (gH, w2L), (gH, w2H))):
                            m = pe.matmul(ybank[g % 4][:], a[:, i, ts], w[:, i, ds],
                                          start=(i == 0 and q == 0), stop=(i == FB - 1 and q == 2))
                    m.then_inc(summed, 1)
                pe.wait_ge(summed, e * G + G)
                pe.sem_inc(used, 1)

            with pe.Fori(0, NE) as e:
                slice_products(e)


def rwkv(nc, con, args, proj, mixed):
    ident, col = con["ident"], con["col"]
    mask = {name: con["masks"][:, n, :] for n, name in enumerate(MASKS)}
    NG = 4
    NC = T // C
    NT = TB // 2
    DECAY = 0.6065306597126334
    NPC = len(RW_COLS)
    B16 = 16
    with ExitStack() as st:
        r = Region(nc, st, "rw")
        raw = {n: r.sb(f"raw_{n}", [P, T + 1]) for n in "rkv"}
        low_raw, low = r.sb("low_raw", [P, T + 1]), r.sb("low", [P, T])
        up, start = r.sb("up", [P, P]), r.sb("start", [P, T])
        pc, rest = r.sb("pc", [P, NPC]), r.sb("rest", [P, 4])
        b = [r.sb(f"b{n}", [P, T]) for n in range(11)]
        bonus, gate_up = r.sb("bonus", [P, T]), r.sb("gate_up", [P, P])
        at_head, rt_head = r.sb("at_head", [P, 2, T]), r.sb("rt_head", [P, 2, T])
        wc, gn = r.sb("wc", [P, NC]), r.sb("gn", [P, 2])
        nat = {n: r.sb(f"nat_{n}", [P, TB, P]) for n in "abkv"}
        state = r.sb("state", [P, NC + 1, C])
        small = r.sb("small", [P, 4, 2 * TB])
        slots = {n: r.sb(n, [P, NG, NT, P]) for n in
                 ("s0", "s1", "s3", "lo32", "lo64", "ak", "rb", "rk", "R", "gu")}
        NB = NG * NT
        diag, back16 = r.sb("diag", [P, NB, B16]), r.sb("back16", [P, NB, B16])
        mine, inverse = r.sb("mine", [P, B16, B16]), r.sb("inverse", [P, B16, B16])
        unit16 = r.sb("unit16", [P, B16, B16])
        work16 = slots["s0"][:, 0, 0:2].rearrange("p j c -> p (j c)").rearrange("p (s t) -> p s t", t=B16)
        diag_d = nc.dram_tensor("rw_diagonal_blocks", [P, NB, B16], F32, kind="Internal").ap()
        back_d = nc.dram_tensor("rw_inverted_blocks", [P, NB, B16], F32, kind="Internal").ap()
        sets = [{n: slots[n][:, g] for n in slots} for g in range(NG)]
        banks = [r.bank(f"b{n}") for n in range(8)]
        rs_, ks_, vs_ = b[0], b[1], b[2]

        def part(slot, n):
            return slots[slot][:, 2 * n:2 * n + 2].rearrange("p a j c -> p (a j c)")

        QT = part("lo32", 0).rearrange("p (j t) -> p j t", t=P)
        MT = part("lo32", 1).rearrange("p (c k) -> p c k", k=C)
        KW = part("lo64", 0).rearrange("p (c v) -> p c v", v=C)
        y_flat, out, y_sq = part("lo64", 1), part("ak", 0), part("ak", 1)
        Y = y_flat.rearrange("p (j f) -> p j f", f=P)
        sems = {}

        def s(name):
            if name not in sems:
                sems[name] = r.sem(name)
            return sems[name]

        low_in, low_cut = s("low_in"), s("low_cut")
        pc_at = {n: k for k, n in enumerate(RW_COLS)}

        def param(name):
            return pc[:, pc_at[name]:pc_at[name] + 1]

        def halves(ap):
            return [ap[:, h * HALF:(h + 1) * HALF] for h in range(NH)]

        ORDER = ("xd", "ak", "rb", "rk", "ld", "wv", "z32", "rt16", "r32", "rt32", "z64", "r64", "gu", "qt")

        def bank_of(name, g):
            return banks[2 * g + (ORDER.index(name) % 2 if name != "y" else 0)]

        def of_head(h):
            return mask["same64"][:, C * h:C * h + 1]

        def every_second(ap, g, c):
            h, th = g // 2, g % 2
            return ap.rearrange("p (j two) k -> p j two k", two=2)[C * h:C * h + C, NT * th:NT * (th + 1), c, :]

        block = st.enter_context(nc.Block())
        LAST = PAIRS - 1

        SCAN, SIDE, TURN = banks[1:4:2], banks[5:8:2], {"a": (1, 3), "b": (0, 2), "k": (1, 3), "v": (0, 2)}
        GATE = (banks[4], banks[6])

        @block.sync
        def _(sp):
            sp.sem_inc(s("stored"), 16)
            sp.dma_start(low_raw[:, 1:T + 1], proj[RW_LOW:RW_LOW + P, :]).then_inc(low_in, 16)

            def load(k, reused):
                if reused:
                    sp.wait_ge(s("pre_w"), k)
                    sp.wait_ge(s("pre_a"), k)
                for part_, p0, p1 in (("rw_w_up", 0, 32), ("rw_a_up", 32, 64)):
                    sp.dma_start(up[p0:p1, :], args[part_].rearrange("l p n -> (l p) n")[:, bass.ds(k * P, P)]
                                 ).then_inc(s("in_up"), 16)
                for n, at in (("k", RW_K), ("r", RW_R), ("v", RW_V)):
                    if reused:
                        sp.wait_ge(s("shift_" + n), k)
                    sp.dma_start(raw[n][:, 1:T + 1], proj[bass.ds(k * P + at, P), :]).then_inc(s("in_" + n), 16)

            def finish(i):
                sp.wait_ge(s("mixed"), i + 1)
                sp.sem_inc(s("sp_passed"), 1)
                sp.dma_start(mixed[bass.ds(i * P + SBW, P), :], out).then_inc(s("stored"), 16)

            def load_gate(i):
                sp.dma_start(gate_up[64:128, :], args["rw_g_up"].rearrange("l p n -> (l p) n")[:, bass.ds(i * P, P)]
                             ).then_inc(s("in_gate"), 16)

            def blocks(i):
                sp.wait_ge(s("diag"), i * NG + NG)
                sp.sem_inc(s("sp_passed"), 1)
                sp.dma_start(diag_d, diag[:]).then_inc(s("diag_out"), 16)
                sp.wait_ge(s("diag_out"), i * 16 + 16)
                for n in range(P // B16):
                    rows = slice(n * B16, n * B16 + B16)
                    sp.dma_start(mine[rows], diag_d[rows].rearrange("s n t -> n s t")).then_inc(s("diag_in"), 16)
                sp.wait_ge(s("inverse"), i + 1)
                sp.sem_inc(s("sp_passed"), 1)
                for n in range(P // B16):
                    rows = slice(n * B16, n * B16 + B16)
                    sp.dma_start(back_d[rows].rearrange("s n t -> n s t"), inverse[rows]).then_inc(s("back_out"), 16)
                sp.wait_ge(s("back_out"), i * (16 * P // B16) + 16 * P // B16)
                sp.dma_start(back16[:], back_d).then_inc(s("back_in"), 16)

            load(0, False)
            load_gate(0)
            with sp.Fori(0, LAST) as i:
                blocks(i)
                load(i + 1, True)
                finish(i)
                sp.wait_ge(s("gate_mm"), i + 1)
                load_gate(i + 1)
            blocks(LAST)
            finish(LAST)
            sp.wait_ge(s("stored"), 16 * PAIRS + 16)

        @block.gpsimd
        def _(pool):
            for n in "rkv":
                pool.memset(raw[n][:, 0:1], 0.0)
            pool.memset(low_raw[:, 0:1], 0.0)
            pool.memset(state[:, 0, :], 0.0)
            pool.memset(unit16[:], 0.0)
            pool.memset(start[:], 1.0).then_inc(s("cleared"), 1)
            pool.wait_ge(s("cleared"), 1)
            pool.memset(start[:].rearrange("p (c t) -> p c t", t=C)[:, :, 0:1], 0.0).then_inc(s("cleared"), 1)
            pool.memset(unit16[:].rearrange("p s t -> p (s t)")[:, 0::B16 + 1], 1.0).then_inc(s("cleared"), 1)

            def apart(k):
                pool.wait_ge(s("rt"), k + 1)
                for h in range(2):
                    pool.tensor_tensor(rt_head[:, h, :], b[7][:], of_head(h).to_broadcast([P, T]), ALU.mult
                                       ).then_inc(s("rt_head"), 1)

            apart(0)

            def core(i):
                pool.wait_ge(s("bonus_made"), i + 1)
                pool.wait_ge(s("biased"), i + 1)
                pool.sem_inc(s("pool_passed"), 1)
                pool.tensor_copy(bonus[:], b[4][:]).then_inc(s("bonus"), 1)

            with pool.Fori(0, LAST) as i:
                core(i)
                pool.wait_ge(s("m_ld"), i * NG + NG)
                apart(i + 1)
            core(LAST)

        @block.scalar
        def _(act):
            act.wait_ge(low_in, 16)
            act.wait_ge(low_cut, 1)
            act.activation(low[:], low_raw[:, 1:T + 1], ACT.Copy, scale=rest[:, 3:4]).then_inc(s("low_part"), 1)
            act.wait_ge(low_cut, 2)
            act.activation(low[0:32, :], low[0:32, :], ACT.Tanh)
            act.activation(low[64:128, :], low[64:128, :], ACT.Sigmoid).then_inc(s("low_done"), 1)

            def scan_step(i, c):
                act.wait_ge(s("step_mm"), i * NC + c + 1)
                if c == 0:
                    act.wait_ge(s("wc"), i + 1)
                act.activation(state[:, c + 1, :], SCAN[c % 2][:, 0:C], ACT.Copy, scale=wc[:, c:c + 1]
                               ).then_inc(s("step"), 1)

            def prepare(k, scan):
                def step(c):
                    if scan is not None:
                        scan_step(scan, c)

                def mix(n, dst, q):
                    act.wait_ge(s("in_" + n), k * 16 + 16)
                    act.activation(dst[:], raw[n][:, 1:T + 1], ACT.Copy, scale=rest[:, q:q + 1]
                                   ).then_inc(s("part_" + n), 1)

                def sigmoid(n, dst, bias, h):
                    act.wait_ge(s("pre_" + n), k + 1)
                    act.activation(halves(dst)[h], SIDE[h][:], ACT.Sigmoid, bias=param(bias)
                                   ).then_inc(s("sig_" + n), 1)

                act.wait_ge(s("cols"), k + 1)
                step(0)
                mix("k", ks_, 1)
                step(1)
                sigmoid("w", b[3], "w0", 0)
                step(2)
                sigmoid("w", b[3], "w0", 1)
                step(3)
                act.wait_ge(s("shift_k"), k + 1)
                act.activation(b[6][:], ks_[:], ACT.Square, scale=param("k_k")).then_inc(s("ksq"), 1)
                step(4)
                if scan is not None:
                    act.wait_ge(s("bonus"), k)
                sigmoid("a", b[4], "a0", 0)
                step(5)
                sigmoid("a", b[4], "a0", 1)
                act.preload_act_table_set(EXP_LN)
                step(6)
                mix("r", rs_, 0)
                step(7)
                mix("v", vs_, 2)
                step(8)
                act.wait_ge(s("norm_kept"), k + 1)
                act.activation(b[6][:], b[6][:], ACT.Ln).then_inc(s("ln"), 1)
                act.wait_ge(s("ln"), k + 1)
                step(9)
                act.activation(b[6][:], b[6][:], ACT.Exp, scale=-0.5).then_inc(s("rn"), 1)
                step(10)
                act.wait_ge(s("cumx"), k + 1)
                act.activation(b[8][:], b[8][:], ACT.Exp, scale=-DECAY).then_inc(s("ex"), 1)
                step(11)
                act.activation(b[10][:], b[7][:], ACT.Exp, scale=DECAY).then_inc(s("en"), 1)
                step(12)
                act.activation(b[9][:], b[7][:], ACT.Exp, scale=-DECAY).then_inc(s("ep"), 1)
                for c in range(13, NC):
                    step(c)

            def take_turned(n, k):
                for h in range(2):
                    act.wait_ge(s("nat_mm_" + n), k * 2 + h + 1)
                    act.copy(nat[n][:, 4 * h:4 * h + 4, :],
                             banks[TURN[n][h]][:].rearrange("p (j f) -> p j f", f=P)).then_inc(s("nat_" + n), 1)

            def apart(k):
                act.wait_ge(s("at"), k + 1)
                for h in range(2):
                    act.activation(at_head[:, h, :], b[8][:], ACT.Copy, scale=of_head(h)).then_inc(s("at_head"), 1)

            def core(i):
                def take(name, slot, n=P):
                    for g in range(NG):
                        act.wait_ge(s("m_" + name), i * NG + g + 1)
                        act.copy(sets[g][slot][:, :, 0:n], bank_of(name, g)[:, 0:NT * n].rearrange("p (j c) -> p j c", c=n)
                                 ).then_inc(s("t_" + name), 1)

                take("wv", "s1", C)
                take("z32", "s0")
                take("rt16", "s3")
                take("rt32", "s3")
                take("z64", "s0")
                take("gu", "gu")
                for g in range(NG):
                    h, th = g // 2, g % 2
                    hs = slice(C * h, C * h + C)
                    act.wait_ge(s("t_mt"), i * NG + g + 1)
                    for c in range(2):
                        m = act.copy(every_second(KW, g, c),
                                     banks[2 * g + c][hs, :].rearrange("p (j f) -> p j f", f=P)[:, :, C:P])
                    m.then_inc(s("t_kw"), 1)

            def norm(i, last):
                for th in range(2):
                    act.wait_ge(s(f"m_y{th}"), i + 1)
                    for h in range(2):
                        act.copy(Y[:, 4 * th:4 * th + 4, C * h:C * h + C],
                                 bank_of("y", 2 * h + th)[:, 0:NT * C].rearrange("p (j v) -> p j v", v=C)
                                 ).then_inc(s("y"), 1)
                if not last:
                    take_turned("a", i + 1)
                    take_turned("b", i + 1)
                act.wait_ge(s("centred"), i + 1)
                act.activation(y_sq, y_flat, ACT.Square).then_inc(s("ysq"), 1)
                if not last:
                    apart(i + 1)
                    take_turned("k", i + 1)
                act.wait_ge(s("var"), i + 1)
                act.activation(small[:, 1, :], small[:, 1, :], ACT.Ln).then_inc(s("root"), 1)
                act.wait_ge(s("root"), i * 2 + 1)
                act.activation(small[:, 2, :], small[:, 1, :], ACT.Exp, scale=-0.5).then_inc(s("root"), 1)
                act.wait_ge(s("gn"), i + 1)
                for h in range(2):
                    act.wait_ge(s("back"), i * 2 + h + 1)
                    act.activation(halves(out)[h], SIDE[h][:], ACT.Identity, scale=gn[:, 0:1],
                                   bias=gn[:, 1:2]).then_inc(s("affine"), 1)
                if not last:
                    take_turned("v", i + 1)

            prepare(0, None)
            apart(0)
            for n in "abkv":
                take_turned(n, 0)
            with act.Fori(0, LAST) as i:
                core(i)
                prepare(i + 1, i)
                norm(i, False)
            core(LAST)
            for c in range(NC):
                scan_step(LAST, c)
            norm(LAST, True)

        @block.vector
        def _(dve):
            mu_low = col[:, COL["rw_mu"] + 9:COL["rw_mu"] + 10]
            dve.sem_inc(s("biased"), 1)
            dve.tensor_scalar(rest[:, 3:4], mu_low, -1.0, 1.0, ALU.mult, ALU.add).then_inc(low_cut, 1)
            dve.wait_ge(s("low_part"), 1)
            dve.wait_ge(s("cleared"), 3)
            dve.scalar_tensor_tensor(low[:], low_raw[:, 0:T], mu_low, low[:], ALU.mult, ALU.add).then_inc(low_cut, 1)
            all_columns = col[:, COL["rw_w0"]:COL["rw_w0"] + 3 * NPC].rearrange("p (n q) -> p n q", q=3)

            def prepare(k):
                def one(name):
                    dve.wait_ge(s(name), k + 1)

                dve.tensor_copy(pc[:].rearrange("p (n o) -> p n o", o=1), all_columns[:, :, bass.ds(k, 1)]
                                ).then_inc(s("cols_raw"), 1)
                one("cols_raw")
                dve.tensor_scalar(rest[:, 0:3], pc[:, 7:10], -1.0, 1.0, ALU.mult, ALU.add).then_inc(s("cols"), 1)

                def shift(n, dst):
                    one("part_" + n)
                    dve.scalar_tensor_tensor(dst[:], raw[n][:, 0:T], param("mu_" + n), dst[:],
                                             ALU.mult, ALU.add).then_inc(s("shift_" + n), 1)

                shift("k", ks_)
                one("shift_k")
                dve.tensor_scalar(b[5][:], ks_[:], param("k_k"), None, ALU.mult).then_inc(s("kx"), 1)
                dve.wait_ge(s("sig_w"), k * 2 + 2)
                dve.tensor_tensor_scan(b[7][:], start[:], b[3][:], 0.0, ALU.mult, ALU.add).then_inc(s("cum"), 1)
                one("cum")
                dve.tensor_tensor(b[8][:], b[7][:], b[3][:], ALU.subtract).then_inc(s("cumx"), 1)
                one("norm_mm")
                for h in range(2):
                    m = dve.tensor_scalar(halves(b[6])[h], SIDE[h][:], 1e-12, None, ALU.max)
                m.then_inc(s("norm_kept"), 1)
                dve.wait_ge(s("sig_a"), k * 2 + 2)
                one("cumx")
                dve.tensor_scalar(b[3][:], b[4][:], -1.0, param("k_a"), ALU.add, ALU.mult).then_inc(s("am"), 1)
                one("am")
                dve.scalar_tensor_tensor(b[3][:], b[3][:], 1.0, ks_[:], ALU.add, ALU.mult).then_inc(s("km"), 1)
                shift("r", rs_)
                shift("v", vs_)
                one("rn")
                one("kx")
                dve.tensor_tensor(b[5][:], b[5][:], b[6][:], ALU.mult).then_inc(s("kk"), 1)
                one("kk")
                dve.tensor_tensor(b[6][:], b[5][:], b[4][:], ALU.mult).then_inc(s("bvec"), 1)
                one("ex")
                dve.scalar_tensor_tensor(b[8][:], b[5][:], -1.0, b[8][:], ALU.mult, ALU.mult).then_inc(s("at"), 1)
                one("km")
                one("shift_r")
                one("bvec")
                dve.scalar_tensor_tensor(b[4][:], rs_[:], param("r_k"), b[3][:], ALU.mult, ALU.mult
                                         ).then_inc(s("rkk"), 1)
                one("en")
                dve.tensor_tensor(b[6][:], b[6][:], b[10][:], ALU.mult).then_inc(s("bt"), 1)
                one("bt")
                dve.tensor_tensor(b[10][:], b[10][:], b[3][:], ALU.mult).then_inc(s("kt"), 1)
                one("ep")
                dve.tensor_tensor(b[7][:], rs_[:], b[9][:], ALU.mult).then_inc(s("rt"), 1)
                one("bonus_mm")
                one("shift_v")
                for h in range(2):
                    m = dve.tensor_tensor(halves(b[4])[h], halves(vs_)[h], SIDE[h][:], ALU.mult)
                m.then_inc(s("bonus_made"), 1)

            def invert(i):
                dve.wait_ge(s("diag_in"), i * (16 * P // B16) + 16 * P // B16)
                R = inverse[:]
                dve.tensor_copy(R, unit16[:]).then_inc(s("column"), 1)
                for t in range(1, B16):
                    dve.wait_ge(s("column"), i * (2 * B16 - 2) + 2 * t - 1)
                    dve.tensor_tensor(work16[:, 0:t, 0:t], R[:, 0:t, 0:t],
                                      mine[:, 0:t, t].unsqueeze(1).to_broadcast([P, t, t]), ALU.mult
                                      ).then_inc(s("column"), 1)
                    dve.wait_ge(s("column"), i * (2 * B16 - 2) + 2 * t)
                    dve.tensor_reduce(R[:, 0:t, t], work16[:, 0:t, 0:t], AX.X, ALU.add
                                      ).then_inc(s("column" if t < B16 - 1 else "inverse"), 1)

            def core(i):
                dve.tensor_copy(wc[:], b[9][:].rearrange("p (c t) -> p c t", t=C)[:, :, C - 1]
                                ).then_inc(s("wc"), 1)
                dve.tensor_copy(gn[:].rearrange("p (n o) -> p n o", o=1),
                                all_columns[:, pc_at["gn_g"]:pc_at["gn_g"] + 2, bass.ds(i, 1)]).then_inc(s("gn"), 1)

                def grp(name, g):
                    dve.wait_ge(s(name), i * NG + g + 1)

                def masked(name, outs):
                    for g in range(NG):
                        grp("m_" + name, g)
                        for slot, m in outs:
                            k = dve.tensor_tensor(sets[g][slot], bank_of(name, g)[:].rearrange("p (j c) -> p j c", c=P),
                                                  mask[m].unsqueeze(1).to_broadcast([P, NT, P]), ALU.mult)
                        k.then_inc(s("t_" + name), 1)

                def add_to_r(name, before):
                    for g in range(NG):
                        grp("m_" + name, g)
                        grp("t_" + before, g)
                        R = sets[g]["R"]
                        dve.tensor_tensor(R, R, bank_of(name, g)[:].rearrange("p (j c) -> p j c", c=P), ALU.add
                                          ).then_inc(s("t_" + name), 1)

                for g in range(NG):
                    grp("m_xd", g)
                    dve.tensor_tensor(sets[g]["s0"], bank_of("xd", g)[:].rearrange("p (j c) -> p j c", c=P),
                                      mask["up16"].unsqueeze(1).to_broadcast([P, NT, P]), ALU.mult
                                      ).then_inc(s("t_xd"), 1)
                    grp("t_xd", g)
                    dve.tensor_reduce(diag[:, NT * g:NT * g + NT, :],
                                      sets[g]["s0"].rearrange("p j (n c) -> p j c n", c=B16), AX.X, ALU.add
                                      ).then_inc(s("diag"), 1)
                dve.wait_ge(s("stored"), i * 16 + 16)
                masked("ak", (("ak", "up64"),))
                masked("rb", (("rb", "upd64"),))
                masked("rk", (("rk", "upd64"),))
                invert(i)
                masked("ld", (("lo32", "low32"), ("lo64", "low64")))
                dve.wait_ge(s("back_in"), i * 16 + 16)
                for g in range(NG):
                    in_blocks = lambda ap: ap.rearrange("p (n c) -> p n c", c=B16)
                    dve.tensor_tensor(sets[g]["R"].rearrange("p j (n c) -> p j n c", c=B16),
                                      back16[:, NT * g:NT * g + NT, :].unsqueeze(2)
                                      .to_broadcast([P, NT, P // B16, B16]),
                                      in_blocks(mask["same16"]).unsqueeze(1).to_broadcast([P, NT, P // B16, B16]),
                                      ALU.mult).then_inc(s("t_r16"), 1)
                add_to_r("r32", "r16")
                add_to_r("r64", "r32")
                for g in range(NG):
                    h, th = g // 2, g % 2
                    hs, js = slice(C * h, C * h + C), slice(NT * th, NT * th + NT)
                    grp("m_qt", g)
                    dve.tensor_tensor(QT[hs, js, :], bank_of("qt", g)[hs, :].rearrange("p (j t) -> p j t", t=P),
                                      b[7][hs, th * HALF:(th + 1) * HALF].rearrange("p (j t) -> p j t", t=P),
                                      ALU.add).then_inc(s("t_qt"), 1)
                for g in range(NG):
                    h, th = g // 2, g % 2
                    hs = slice(C * h, C * h + C)
                    grp("m_mk", g)
                    for c in range(2):
                        m = dve.tensor_tensor(every_second(MT, g, c),
                                              banks[2 * g + c][hs, :].rearrange("p (j f) -> p j f", f=P)[:, :, 0:C],
                                              ident[hs, hs].unsqueeze(1).to_broadcast([C, NT, C]), ALU.add)
                    m.then_inc(s("t_mt"), 1)

            def norm(i):
                def one(name):
                    dve.wait_ge(s(name), i + 1)

                dve.wait_ge(s("y"), i * NG + NG)
                y3 = y_flat.rearrange("p (n v) -> p n v", v=C)
                bc = lambda q: small[:, q, :].unsqueeze(2).to_broadcast([P, 2 * TB, C])
                dve.tensor_reduce(small[:, 0, :], y3, AX.X, ALU.add).then_inc(s("ysum"), 1)
                one("ysum")
                dve.tensor_scalar(small[:, 0, :], small[:, 0, :], 1.0 / C, None, ALU.mult).then_inc(s("mean"), 1)
                one("mean")
                dve.tensor_tensor(y3, y3, bc(0), ALU.subtract).then_inc(s("centred"), 1)
                one("ysq")
                dve.tensor_reduce(small[:, 1, :], y_sq.rearrange("p (n v) -> p n v", v=C), AX.X, ALU.add
                                  ).then_inc(s("vsum"), 1)
                one("vsum")
                dve.tensor_scalar(small[:, 1, :], small[:, 1, :], 1.0 / C, GN_EPS, ALU.mult, ALU.add
                                  ).then_inc(s("var"), 1)
                dve.wait_ge(s("root"), i * 2 + 2)
                dve.tensor_tensor(y3, y3, bc(2), ALU.mult).then_inc(s("normed"), 1)
                dve.wait_ge(s("affine"), i * 2 + 2)
                one("bonus")
                dve.tensor_tensor(out, out, bonus[:], ALU.add).then_inc(s("biased"), 1)
                dve.wait_ge(s("biased"), i + 2)
                one("gate_mm")
                for h in range(2):
                    m = dve.tensor_tensor(halves(out)[h], halves(out)[h], GATE[h][:], ALU.mult)
                m.then_inc(s("mixed"), 1)

            prepare(0)
            with dve.Fori(0, LAST) as i:
                core(i)
                prepare(i + 1)
                norm(i)
            core(LAST)
            norm(LAST)

        @block.tensor
        def _(pe):
            pe.wait_ge(s("low_done"), 1)
            pe.wait_ge(low_cut, 2)

            def low_rank(k, n):
                if n == "w":
                    pe.wait_ge(s("in_up"), k * 32 + 32)
                else:
                    pe.wait_ge(s("sig_w"), k * 2 + 2)
                p0, p1 = (0, 32) if n == "w" else (32, 64)
                for h in range(NH):
                    m = pe.matmul(SIDE[h][:], up[p0:p1, :], halves(low)[h][p0:p1, :], start=True, stop=True)
                m.then_inc(s("pre_" + n), 1)

            def norms(k):
                pe.wait_ge(s("ksq"), k + 1)
                pe.wait_ge(s("sig_a"), k * 2 + 2)
                for h in range(NH):
                    m = pe.matmul(SIDE[h][:], mask["same64"], halves(b[6])[h], start=True, stop=True)
                m.then_inc(s("norm_mm"), 1)

            def bonuses(k):
                pe.wait_ge(s("rkk"), k + 1)
                pe.wait_ge(s("norm_kept"), k + 1)
                for h in range(NH):
                    m = pe.matmul(SIDE[h][:], mask["same64"], halves(b[4])[h], start=True, stop=True)
                m.then_inc(s("bonus_mm"), 1)

            def turn(n, k):
                src, made = {"a": (b[8], "at"), "b": (b[6], "bt"), "k": (b[10], "kt"), "v": (vs_, "shift_v")}[n]
                pe.wait_ge(s(made), k + 1)
                if n in "kv":
                    pe.wait_ge(s("nat_a" if n == "k" else "nat_b"), k * 2 + 2)
                for h in range(2):
                    for q in range(4):
                        j = 4 * h + q
                        m = pe.transpose(banks[TURN[n][h]][:, q * P:(q + 1) * P], src[:, j * P:(j + 1) * P], ident[:])
                    m.then_inc(s("nat_mm_" + n), 1)

            def core(i, after):
                def one(name):
                    pe.wait_ge(s(name), i + 1)

                for n in "abkv":
                    pe.wait_ge(s("nat_" + n), i * 2 + 2)
                one("bonus_made")
                if after:
                    pe.wait_ge(s("affine"), i * 2)
                    pe.wait_ge(s("mixed"), i)
                one("rt")

                def grp(name, g):
                    pe.wait_ge(s(name), i * NG + g + 1)

                def step(name, needs, product):
                    n = ORDER.index(name)
                    for g in range(NG):
                        if n >= 2:
                            grp("t_" + ORDER[n - 2], g)
                        for need in needs:
                            grp("t_" + need, g)
                        bk = bank_of(name, g)
                        for j in range(NT):
                            m = product(g, sets[g], j, bk)
                        m.then_inc(s("m_" + name), 1)

                def scores(left, right):
                    def product(g, q, j, bk):
                        h, th = g // 2, g % 2
                        ts = slice((NT * th + j) * P, (NT * th + j + 1) * P)
                        l, r_ = [x[:, h, ts] if x in (at_head, rt_head) else x[:, ts] for x in (left, right)]
                        return pe.matmul(bk[:, j * P:(j + 1) * P], l, r_, start=True, stop=True)
                    return product

                def square(left, right):
                    def product(g, q, j, bk):
                        return pe.matmul(bk[:, j * P:(j + 1) * P], q[left][:, j, :], q[right][:, j, :],
                                         start=True, stop=True)
                    return product

                def turned(src):
                    def product(g, q, j, bk):
                        return pe.transpose(bk[:, j * P:(j + 1) * P], q[src][:, j, :], ident[:])
                    return product

                def tile_of(g, j):
                    return NT * (g % 2) + j, slice(C * (g // 2), C * (g // 2) + C)

                pe.wait_ge(s("at_head"), i * 2 + 2)
                step("xd", (), scores(b[6], at_head))
                step("ak", (), scores(b[10], at_head))
                pe.wait_ge(s("rt_head"), i * 2 + 2)
                step("rb", (), scores(b[6], rt_head))
                step("rk", (), scores(b[10], rt_head))
                step("ld", (), scores(at_head, b[6]))

                def keys_values(g, q, j, bk):
                    t, hs = tile_of(g, j)
                    return pe.matmul(bk[:, j * C:(j + 1) * C], q["ak"][:, j, :], nat["v"][:, t, hs], start=True, stop=True)

                step("wv", ("ak",), keys_values)
                step("z32", ("ld", "r16"), square("lo32", "R"))
                step("rt16", ("r16",), turned("R"))
                step("r32", ("z32", "rt16"), square("s3", "s0"))
                step("rt32", ("r32",), turned("R"))
                step("z64", (), square("lo64", "R"))
                step("r64", ("z64", "rt32"), square("s3", "s0"))

                def updates(g, q, j, bk):
                    t, hs = tile_of(g, j)
                    pe.matmul(bk[:, j * P:j * P + C], q["R"][:, j, :], nat["a"][:, t, hs], start=True, stop=True)
                    return pe.matmul(bk[:, j * P + C:(j + 1) * P], q["R"][:, j, :], q["s1"][:, j, 0:C],
                                     start=True, stop=True)

                step("gu", ("wv", "r64"), updates)

                def readers(g, q, j, bk):
                    t, hs = tile_of(g, j)
                    return pe.matmul(bk[hs, j * P:(j + 1) * P], q["gu"][:, j, 0:C], q["rb"][:, j, :], start=True, stop=True)

                step("qt", ("gu", "rb"), readers)

                for g in range(NG):
                    q = sets[g]
                    grp("t_gu", g)
                    grp("t_qt", g)
                    pe.sem_inc(s("pe_passed"), 1)
                    for c in range(2):
                        cs = slice(C * c, C * c + C)
                        for j in range(NT):
                            t, hs = tile_of(g, j)
                            m = pe.matmul(banks[2 * g + c][hs, j * P:j * P + C], q["gu"][cs, j, 0:C],
                                          nat["b"][cs, t, hs], start=True, stop=True)
                            o = banks[2 * g + c][hs, j * P + C:(j + 1) * P]
                            pe.matmul(o, nat["b"][cs, t, hs], q["gu"][cs, j, C:P], start=True, stop=False)
                            m = pe.matmul(o, nat["k"][cs, t, hs], nat["v"][cs, t, hs], start=False, stop=True)
                    m.then_inc(s("m_mk"), 1)
            def scan_step(i, c):
                if c == 0:
                    pe.wait_ge(s("t_mt"), i * NG + NG)
                    pe.wait_ge(s("t_kw"), i * NG + NG)
                    pe.sem_inc(s("pe_passed"), 1)
                for h in range(2):
                    hs = slice(C * h, C * h + C)
                    pe.matmul(SCAN[c % 2][hs, 0:C], ident[hs, hs], KW[hs, c, :], start=True, stop=False)
                if c:
                    pe.wait_ge(s("step"), i * NC + c)
                    pe.sem_inc(s("pe_passed"), 1)
                for h in range(2):
                    hs = slice(C * h, C * h + C)
                    m = pe.matmul(SCAN[c % 2][hs, 0:C], MT[hs, c, :], state[hs, c, :], start=False, stop=True)
                m.then_inc(s("step_mm"), 1)

            def outputs(i, n):
                t, h = n // 2, n % 2
                if n == 0:
                    pe.wait_ge(s("t_rk"), i * NG + NG)
                    pe.sem_inc(s("pe_passed"), 1)
                th, j = t // NT, t % NT
                o = slice(j * C, (j + 1) * C)
                q, bk, hs = sets[2 * h + th], bank_of("y", 2 * h + th), slice(C * h, C * h + C)
                pe.matmul(bk[:, o], q["rb"][:, j, :], q["gu"][:, j, C:P], start=True, stop=False)
                pe.matmul(bk[:, o], q["rk"][:, j, :], nat["v"][:, t, hs], start=False, stop=True)
                for c in range(2):
                    cs = slice(C * c, C * c + C)
                    m = pe.matmul(bk[cs, o], QT[hs, t, cs], state[hs, 2 * t + c, :], start=False, stop=True,
                                  skip_group_check=True)
                if h == 1 and j == NT - 1:
                    m.then_inc(s(f"m_y{th}"), 1)

            def finish(i, last):
                if not last:
                    bonuses(i + 1)
                    pe.wait_ge(s("step"), i * NC + NC)
                    turn("a", i + 1)
                pe.wait_ge(s("y"), i * NG + NG)
                pe.wait_ge(s("in_gate"), i * 16 + 16)
                for h in range(NH):
                    m = pe.matmul(GATE[h][:], gate_up[64:128, :], halves(low)[h][64:128, :], start=True, stop=True)
                m.then_inc(s("gate_mm"), 1)
                if not last:
                    turn("b", i + 1)
                    turn("k", i + 1)
                    pe.wait_ge(s("bonus_made"), i + 2)
                pe.wait_ge(s("normed"), i + 1)
                for h in range(2):
                    for q in range(4):
                        j = 4 * h + q
                        m = pe.transpose(SIDE[h][:, q * P:(q + 1) * P], Y[:, j, :], ident[:])
                    m.then_inc(s("back"), 1)
                if not last:
                    turn("v", i + 1)

            low_rank(0, "w")
            low_rank(0, "a")
            norms(0)
            bonuses(0)
            for n in "abkv":
                turn(n, 0)
            core(0, False)
            with pe.Fori(0, LAST) as i:
                for c in range(NC):
                    scan_step(i, c)
                    if c:
                        outputs(i, c - 1)
                    if c == 0:
                        low_rank(i + 1, "w")
                    if c == 3:
                        low_rank(i + 1, "a")
                    if c == 7:
                        norms(i + 1)
                outputs(i, NC - 1)
                finish(i, False)
                core(i + 1, True)
            for c in range(NC):
                scan_step(LAST, c)
                if c:
                    outputs(LAST, c - 1)
            outputs(LAST, NC - 1)
            finish(LAST, True)


def gla(nc, con, args, proj, mixed):
    ident, col, levels = con["ident"], con["col"], con["levels"]
    NL = 6
    H, DK, DV = 4, 32, 64
    NC = T // C
    WV = H * DV
    with ExitStack() as st:
        r = Region(nc, st, "gla")
        q, k = r.sb("q", [P, T]), r.sb("k", [P, T])
        vT = [r.sb(f"vT{n}", [P, T]) for n in range(2)]
        gT = [r.sb(f"gT{n}", [P, T]) for n in range(2)]
        sg = [r.sb(f"sg{n}", [P, T]) for n in range(2)]
        gd, gate_up = r.sb("gd", [16, T]), r.sb("gup", [16, P])
        x, e, cum, start = r.sb("x", [P, T]), r.sb("e", [P, T]), r.sb("cum", [P, T]), r.sb("start", [P, T])
        D_ = [r.sb(f"D{n}", [P, T]) for n in range(2)]
        qf = [r.sb(f"qf{n}", [P, T // 2]) for n in range(2)]
        result = [r.sb(f"result{n}", [P, T]) for n in range(2)]
        own = r.sb("own", [P, T // P * H])
        qb = [r.sb(f"qb{n}", [P, TB, H, C]) for n in range(2)]
        kf = [r.sb(f"kf{n}", [P, T]) for n in range(2)]
        qin, kout = r.sb("qin", [P, T]), r.sb("kout", [P, T])
        A = r.sb("A", [P, TB, H, P])
        knat, vnat = r.sb("knat", [P, TB, P]), r.sb("vnat", [P, TB, WV])
        heads = r.sb("heads", [P, WV])
        KV = r.sb("KV", [P, NC, WV])
        S = r.sb("S", [P, NC + 1, WV])
        small = r.sb("small", [P, 2, TB * H])
        O, osq = KV, S
        banks = [r.bank(f"b{n}") for n in range(8)]
        sems = {}

        def s(name):
            if name not in sems:
                sems[name] = r.sem(name)
            return sems[name]

        block = st.enter_context(nc.Block())
        LOADS = [(q, GLA_Q, P, "q"), (k, GLA_K, P, "k"), (vT[0], GLA_V, P, "v"), (vT[1], GLA_V + P, P, "v"),
                 (gT[0], GLA_G, P, "g"), (gT[1], GLA_G + P, P, "g")]

        @block.sync
        def _(sp):
            sp.dma_start(gd[:], proj[GLA_GD:GLA_GD + 16, :]).then_inc(s("in_gd"), 16)
            sp.dma_start(gate_up[:], args["gla_gate_up"].rearrange("l p n -> (l p) n")).then_inc(s("in_gd"), 16)
            for dst, at, n, name in LOADS:
                sp.dma_start(dst[:], proj[at:at + n, :]).then_inc(s("in_" + name), 16)
            for n in range(2):
                sp.wait_ge(s("mixed"), n + 1)
                sp.dma_start(mixed[SBW + RWW + n * P:SBW + RWW + (n + 1) * P, :], result[n][:]).then_inc(s("stored"), 16)
            sp.wait_ge(s("stored"), 32)

        @block.gpsimd
        def _(pool):
            pool.memset(start[:], 1.0).then_inc(s("ones"), 1)
            pool.wait_ge(s("ones"), 1)
            pool.memset(start[:].rearrange("p (c t) -> p c t", t=C)[:, :, 0:1], 0.0).then_inc(s("start"), 1)
            for n in range(2):
                pool.memset(qb[n][:].rearrange("p j h t -> p (j h t)"), 0.0)
                m = pool.memset(kf[n][:], 0.0)
            m.then_inc(s("zeroed"), 1)
            pool.memset(heads[:], 0.0).then_inc(s("heads"), 1)
            pool.wait_ge(s("heads"), 1)
            for h in range(H):
                pool.memset(heads[DK * h:DK * h + DK, DV * h:DV * h + DV], 1.0).then_inc(s("heads"), 1)
                pool.wait_ge(s("heads"), h + 2)
            pool.memset(S[:, 0, :], 0.0).then_inc(s("heads"), 1)

        @block.scalar
        def _(act):
            act.wait_ge(s("in_g"), 32)
            for n in range(2):
                act.activation(sg[n][:], gT[n][:], ACT.Sigmoid).then_inc(s("sigmoid"), 1)
            act.preload_act_table_set(EXP_LN)
            act.wait_ge(s("gate_mm"), 1)
            bias = col[:, COL["gla_gate_b"]:COL["gla_gate_b"] + 1]
            for h in range(NH):
                hs = slice(h * HALF, (h + 1) * HALF)
                act.activation(e[:, hs], banks[h][:], ACT.Abs, bias=bias)
                act.activation(x[:, hs], banks[h][:], ACT.Identity, bias=bias).then_inc(s("arg"), 1)
            act.wait_ge(s("arg"), 2)
            act.activation(e[:], e[:], ACT.Exp, scale=-1.0).then_inc(s("exp"), 1)
            act.wait_ge(s("exp"), 1)
            act.activation(e[:], e[:], ACT.Ln, bias=1.0).then_inc(s("log"), 1)
            act.wait_ge(s("in_q"), 16)
            act.activation(q[:], q[:], ACT.Copy, scale=float(DK) ** -0.5).then_inc(s("q"), 1)
            act.wait_ge(s("cum"), 1)
            act.activation(qin[:], cum[:], ACT.Exp, scale=-1.0 / 16).then_inc(s("from_start"), 1)
            act.wait_ge(s("to_last"), 1)
            act.activation(kout[:], kout[:], ACT.Exp, scale=-1.0 / 16).then_inc(s("to_end"), 1)
            act.wait_ge(s("softplus"), 1)
            act.activation(e[:, 0:NC], cum[:].rearrange("p (c t) -> p c t", t=C)[:, :, C - 1], ACT.Exp,
                           scale=-1.0 / 16).then_inc(s("decay"), 1)

            def factor(n):
                act.wait_ge(s("diff"), n + 1)
                act.activation(D_[n % 2][:], D_[n % 2][:], ACT.Exp, scale=-1.0 / 16).then_inc(s("factor"), 1)

            factor(0)
            factor(1)
            for m in range(2):
                for h in range(2):
                    act.wait_ge(s("vnat_mm"), 2 * m + h + 1)
                    act.copy(vnat[:, 4 * h:4 * h + 4, m * P:(m + 1) * P],
                             banks[2 * m + h][:].rearrange("p (j f) -> p j f", f=P)).then_inc(s("vnat"), 1)
            for h in range(2):
                act.wait_ge(s("knat_mm"), h + 1)
                act.copy(knat[:, 4 * h:4 * h + 4, :], banks[4 + h][:].rearrange("p (j f) -> p j f", f=P)
                         ).then_inc(s("knat"), 1)
            act.wait_ge(s("zeroed"), 1)
            for n in range(NL):
                act.wait_ge(s("qf"), n + 1)
                if n >= 2:
                    act.wait_ge(s("level_mm"), 4 * (n - 1))
                for h in range(H):
                    rows = slice(DK * h, DK * h + DK)
                    act.copy(qb[n % 2][rows, :, h, :], qf[n % 2][rows, :].rearrange("p (j t) -> p j t", t=C)
                             ).then_inc(s("spread"), 1)
                if n + 2 < NL:
                    factor(n + 2)
            for n in range(4):
                act.wait_ge(s("o_mm"), n + 1)
                act.copy(O[:, 2 * n:2 * n + 2, :], banks[n][:].rearrange("p (j v) -> p j v", v=WV)).then_inc(s("o"), 1)
            act.wait_ge(s("o"), 4)
            act.activation(osq[:, 0:TB, :], O[:, 0:TB, :], ACT.Square).then_inc(s("osq"), 1)
            act.wait_ge(s("mean"), 1)
            act.activation(small[:, 0, :], small[:, 0, :], ACT.Sqrt).then_inc(s("root"), 1)
            for m in range(2):
                for h in range(NH):
                    act.wait_ge(s("back"), 2 * m + h + 1)
                    act.activation(result[m][:, h * HALF:(h + 1) * HALF], banks[4 + 2 * m + h][:], ACT.Copy,
                                   scale=col[:, COL["gla_norm_g"] + m:COL["gla_norm_g"] + m + 1]).then_inc(s("gained"), 1)

        @block.vector
        def _(dve):
            w = lambda name, n=1: dve.wait_ge(s(name), n)
            w("sigmoid", 2)
            for n in range(2):
                dve.tensor_tensor(sg[n][:], sg[n][:], gT[n][:], ALU.mult).then_inc(s("silu"), 1)
            w("arg", 2)
            dve.tensor_scalar(x[:], x[:], -1.0, 0.0, ALU.mult, ALU.max).then_inc(s("rect"), 1)
            w("rect")
            w("log")
            dve.tensor_tensor(x[:], x[:], e[:], ALU.add).then_inc(s("softplus"), 1)
            w("softplus")
            w("start")
            dve.tensor_tensor_scan(cum[:], start[:], x[:], 0.0, ALU.mult, ALU.add).then_inc(s("cum"), 1)
            w("cum")
            c3 = lambda ap: ap.rearrange("p (c t) -> p c t", t=C)
            dve.tensor_tensor(c3(kout[:]), c3(cum[:])[:, :, C - 1:C].to_broadcast([P, NC, C]), c3(cum[:]),
                              ALU.subtract).then_inc(s("to_last"), 1)

            def differences(n):
                m = 1 << n
                v = lambda ap: ap.rearrange("p (b two m) -> p b two m", two=2, m=m)
                cu, d = v(cum[:]), v(D_[n % 2][:])
                nb = T // (2 * m)
                mid = cu[:, :, 0, m - 1:m].to_broadcast([P, nb, m])
                if n >= 2:
                    w("kf", n - 1)
                dve.tensor_tensor(d[:, :, 0, :], mid, cu[:, :, 0, :], ALU.subtract)
                dve.tensor_tensor(d[:, :, 1, :], cu[:, :, 1, :], mid, ALU.subtract).then_inc(s("diff"), 1)

            differences(0)
            w("q")
            w("from_start")
            dve.tensor_tensor(qin[:], qin[:], q[:], ALU.mult).then_inc(s("qin"), 1)
            w("to_end")
            w("in_k", 16)
            dve.tensor_tensor(kout[:], kout[:], k[:], ALU.mult).then_inc(s("kout"), 1)
            w("zeroed")

            def factors(n):
                m = 1 << n
                v = lambda ap, half: ap.rearrange("p (b two m) -> p b two m", two=2, m=m)[:, :, half, :]
                w("factor", n + 1)
                if n >= 2:
                    w("spread", H * (n - 1))
                    w("level_mm", 4 * (n - 1))
                dve.tensor_tensor(qf[n % 2][:].rearrange("p (b m) -> p b m", m=m), v(D_[n % 2][:], 1), v(q[:], 1), ALU.mult
                                  ).then_inc(s("qf"), 1)
                dve.tensor_tensor(v(kf[n % 2][:], 0), v(D_[n % 2][:], 0), v(k[:], 0), ALU.mult).then_inc(s("kf"), 1)

            def take(n):
                w("diagonal", H)
                m = 1 << n
                second = lambda ap: ap.rearrange("p (b two m) -> p b two m", two=2, m=m)[:, :, 1, :]
                msk = second(levels[:, n, :].bitcast(U32)).unsqueeze(1).to_broadcast([P, 2 * H, C // m, m])
                for g in range(4):
                    w("level_mm", 4 * n + g + 1)
                    if n:
                        w("taken", 4 * (n - 1) + g + 1)
                    dst = A[:, 2 * g:2 * g + 2].rearrange("p j h t -> p (j h t)")
                    dve.copy_predicated(second(dst).rearrange("p (j b) m -> p j b m", j=2 * H), msk,
                                        banks[4 * (n % 2) + g][:].rearrange("p (j b m) -> p j b m", j=2 * H, m=m)
                                        ).then_inc(s("taken"), 1)

            w("q")
            dve.tensor_tensor(x[:], q[:], k[:], ALU.mult).then_inc(s("qk"), 1)
            w("own_mm")
            dve.tensor_copy(own[:], banks[7][:, 0:TB * H]).then_inc(s("own"), 1)
            w("own")
            for h in range(H):
                dve.tensor_tensor(A[:, :, h, :], ident[:].unsqueeze(1).to_broadcast([P, TB, P]),
                                  own[:].rearrange("p (j h) -> p h j", h=H)[:, h, :].unsqueeze(2)
                                  .to_broadcast([P, TB, P]), ALU.mult).then_inc(s("diagonal"), 1)
            differences(1)
            factors(0)
            factors(1)
            for n in range(NL):
                if n + 2 < NL:
                    differences(n + 2)
                take(n)
                if n + 2 < NL:
                    factors(n + 2)
            w("heads", H + 2)
            for n in range(8):
                w("kv_mm", n + 1)
                t, c = n // 2, n % 2
                dst = KV[:].rearrange("p (j two) v -> p j two v", two=2)[:, 2 * t:2 * t + 2, c, :]
                dve.tensor_tensor(dst, banks[n][:].rearrange("p (j v) -> p j v", v=WV),
                                  heads[:].unsqueeze(1).to_broadcast([P, 2, WV]), ALU.mult).then_inc(s("kv"), 1)
            w("decay")
            for c in range(NC):
                if c:
                    w("state", c)
                else:
                    w("kv", 8)
                dve.scalar_tensor_tensor(S[:, c + 1, :], S[:, c, :], e[:, c:c + 1], KV[:, c, :],
                                         ALU.mult, ALU.add).then_inc(s("state"), 1)
            w("osq")
            dve.tensor_reduce(small[:, 0, :], osq[:, 0:TB, :].rearrange("p j (h v) -> p (j h) v", v=DV), AX.X, ALU.add
                              ).then_inc(s("ssum"), 1)
            w("ssum")
            dve.tensor_scalar(small[:, 0, :], small[:, 0, :], 1.0 / DV, EPS, ALU.mult, ALU.add).then_inc(s("mean"), 1)
            w("root")
            dve.reciprocal(small[:, 1, :], small[:, 0, :]).then_inc(s("rstd"), 1)
            w("rstd")
            o3 = O[:, 0:TB, :].rearrange("p j (h v) -> p (j h) v", v=DV)
            dve.tensor_tensor(o3, o3, small[:, 1, :].unsqueeze(2).to_broadcast([P, TB * H, DV]), ALU.mult
                              ).then_inc(s("normed"), 1)
            for m in range(2):
                w("gained", 2 * m + 2)
                dve.tensor_tensor(result[m][:], result[m][:], sg[m][:], ALU.mult).then_inc(s("mixed"), 1)

        @block.tensor
        def _(pe):
            w = lambda name, n=1: pe.wait_ge(s(name), n)
            w("in_gd", 32)
            for h in range(NH):
                m = pe.matmul(banks[h][:], gate_up[:], gd[:, h * HALF:(h + 1) * HALF], start=True, stop=True)
            m.then_inc(s("gate_mm"), 1)
            w("in_v", 32)
            for n in range(2):
                for h in range(2):
                    if 2 * n + h < 2:
                        w("arg", 2)
                    for j in range(4):
                        m = pe.transpose(banks[2 * n + h][:, j * P:(j + 1) * P],
                                         vT[n][:, (4 * h + j) * P:(4 * h + j + 1) * P], ident[:])
                    m.then_inc(s("vnat_mm"), 1)
            w("heads", H + 2)
            w("qk")
            for j in range(TB):
                m = pe.matmul(banks[7][:, j * H:(j + 1) * H], x[:, j * P:(j + 1) * P], heads[:, 0::DV],
                              start=True, stop=True)
            m.then_inc(s("own_mm"), 1)
            w("kout")
            for h in range(2):
                for j in range(4):
                    m = pe.transpose(banks[4 + h][:, j * P:(j + 1) * P],
                                     kout[:, (4 * h + j) * P:(4 * h + j + 1) * P], ident[:])
                m.then_inc(s("knat_mm"), 1)
            w("vnat", 4)
            w("knat", 2)
            w("own")
            for n in range(NL):
                w("kf", n + 1)
                w("spread", H * (n + 1))
                for g in range(4):
                    if n >= 2:
                        w("taken", 4 * (n - 2) + g + 1)
                    for j in range(2):
                        t = 2 * g + j
                        m = pe.matmul(banks[4 * (n % 2) + g][:, j * H * C:(j + 1) * H * C],
                                      kf[n % 2][:, t * P:(t + 1) * P],
                                      qb[n % 2][:, t].rearrange("p h t -> p (h t)"), start=True, stop=True)
                    m.then_inc(s("level_mm"), 1)
            for n in range(8):
                t, c = n // 2, n % 2
                w("taken", 4 * (NL - 2 + n // 4) + n % 4 + 1)
                cs = slice(C * c, C * c + C)
                for j in range(2):
                    m = pe.matmul(banks[n][:, j * WV:(j + 1) * WV], knat[cs, 2 * t + j, :], vnat[cs, 2 * t + j, :],
                                  start=True, stop=True)
                m.then_inc(s("kv_mm"), 1)
            w("kv", 8)
            w("qin")
            for n in range(4):
                w("state", min(4 * n + 4, NC))
                for jj in range(2):
                    j = 2 * n + jj
                    o = slice(jj * WV, (jj + 1) * WV)
                    for c in range(2):
                        pe.matmul(banks[n][C * c:C * c + C, o], qin[:, j * P + C * c:j * P + C * c + C],
                                  S[:, 2 * j + c, :], start=True, stop=True)
                    for h in range(H):
                        m = pe.matmul(banks[n][:, jj * WV + DV * h:jj * WV + DV * h + DV], A[:, j, h, :],
                                      vnat[:, j, DV * h:DV * h + DV], start=False, stop=True, skip_group_check=True)
                m.then_inc(s("o_mm"), 1)
            w("normed")
            for m_ in range(2):
                for h in range(2):
                    for jj in range(4):
                        j = 4 * h + jj
                        m = pe.transpose(banks[4 + 2 * m_ + h][:, jj * P:(jj + 1) * P],
                                         O[:, j, m_ * P:(m_ + 1) * P], ident[:])
                    m.then_inc(s("back"), 1)


def stick_breaking(nc, con, args, proj, mixed):
    ident, col = con["ident"], con["col"]
    mask = {name: con["masks"][:, n, :] for n, name in enumerate(MASKS)}
    DH = 64
    QC = T // HALF
    PER = HALF // P
    CAP = float(2 ** 60)
    UNITS = []
    for c in range(QC):
        for kb in range(PER * (c + 1) - 1, -1, -1):
            for h in range(2):
                UNITS.append((h, c, kb, max(0, (kb - PER * c) * P), kb == PER * (c + 1) - 1))
    NU = len(UNITS)
    NZ, AHEAD = 4, 2
    with ExitStack() as st:
        r = Region(nc, st, "sb")
        qd, kd = [r.sb(f"qd{h}", [P, T]) for h in range(2)], [r.sb(f"kd{h}", [P, T]) for h in range(2)]
        vp = r.sb("vp", [P, T])
        kS = [r.sb(f"kS{h}", [P, T], F32R) for h in range(2)]
        qH, qL = [r.sb(f"qH{h}", [P, T], F32R) for h in range(2)], [r.sb(f"qL{h}", [P, T], F32R) for h in range(2)]
        vn = r.sb("vn", [P, TB, P])
        E = [r.sb(f"E{n}", [P, HALF]) for n in range(4)]
        SP = [r.sb(f"SP{n}", [P, HALF]) for n in range(4)]
        R = [[r.sb(f"R{h}{n}", [P, HALF]) for n in range(2)] for h in range(2)]
        W = [r.sb(f"W{n}", [P, HALF]) for n in range(4)]
        tri, ones = r.sb("tri", [P, P]), r.sb("ones", [P, P])
        O, osq = r.sb("O", [P, TB, P]), r.sb("osq", [P, TB, P])
        outT = r.sb("outT", [P, T])
        small = r.sb("small", [P, 2, 2 * TB])
        small_gain = r.sb("gain", [P, 1])
        Z = [r.bank(f"Z{n}") for n in range(NZ)]
        OB = [[r.bank(f"O{h}{c}") for c in range(QC)] for h in range(2)]
        sems = {}

        def s(name):
            if name not in sems:
                sems[name] = r.sem(name)
            return sems[name]

        ENGINES = 5
        block = st.enter_context(nc.Block())

        def pair_end(e, i):
            e.drain().then_inc(s("pair_done"), 1)
            e.wait_ge(s("pair_done"), i * ENGINES + ENGINES)

        def span(u):
            h, c, kb, off, first = UNITS[u]
            return slice(off, HALF)

        @block.sync
        def _(sp):
            with sp.Fori(0, PAIRS) as i:
                for h in range(2):
                    for half in range(2):
                        rows = slice(DH * half, DH * half + DH)
                        sp.dma_start(kd[h][rows, :], proj[bass.ds(i * P + SB_K + DH * h, DH), :]).then_inc(s("in_k"), 16)
                        sp.dma_start(qd[h][rows, :], proj[bass.ds(i * P + SB_Q + DH * h, DH), :]).then_inc(s("in_q"), 16)
                sp.dma_start(vp[:], proj[bass.ds(i * P + SB_V, P), :]).then_inc(s("in_v"), 16)
                sp.wait_ge(s("mixed"), i * 2 + 2)
                sp.sem_inc(s("sp_passed"), 1)
                sp.dma_start(mixed[bass.ds(i * P, P), :], outT[:]).then_inc(s("stored"), 16)
                sp.wait_ge(s("stored"), i * 16 + 16)
                sp.sem_inc(s("pair_done"), 1)
                sp.wait_ge(s("pair_done"), i * ENGINES + ENGINES)
                sp.sem_inc(s("sp_passed"), 1)

        @block.gpsimd
        def _(pool):
            with pool.Fori(0, PAIRS) as i:
                nth = [0, 0]
                for u in range(NU):
                    h, c, kb, off, first = UNITS[u]
                    new, old = R[h][(nth[h] + 1) % 2], R[h][nth[h] % 2]
                    nth[h] += 1
                    pool.wait_ge(s("sp"), i * NU + u + 1)
                    if u >= 4:
                        pool.wait_ge(s("tri_mm"), i * NU + u - 1)
                    if kb > 0:
                        if first:
                            pool.sem_inc(s("pool_passed"), 1)
                            pool.tensor_copy(new[:, off:], SP[u % 4][:, off:]).then_inc(s("sum"), 1)
                        else:
                            pool.wait_ge(s("sum"), i * NU + u - 1)
                            pool.tensor_tensor(new[:, off:], old[:, off:], SP[u % 4][:, off:], ALU.add
                                               ).then_inc(s("sum"), 1)
                        if off:
                            pool.memset(new[:, off - P:off], 0.0)
                    else:
                        pool.sem_inc(s("sum"), 1)
                    if kb >= PER * c:
                        pool.wait_ge(s("weight"), i * NU + u + 1)
                        pool.sem_inc(s("pool_passed"), 1)
                        w = W[u % 4][:, off:off + P]
                        pool.affine_select(out=w, in_=w, compare_op=ALU.is_gt, fill=0.0, base=0,
                                           pattern=[[1, P]], channel_multiplier=-1)
                    pool.drain().then_inc(s("cut"), 1)
                pair_end(pool, i)

        @block.scalar
        def _(act):
            with act.Fori(0, PAIRS) as i:
                act.preload_act_table_set(EXP_LN)
                act.wait_ge(s("in_k"), i * 64 + 64)
                act.wait_ge(s("in_q"), i * 64 + 64)
                for h in range(2):
                    act.copy(kS[h][:], kd[h][:]).then_inc(s("k_high"), 1)
                    act.activation(qH[h][:], qd[h][:], ACT.Copy, scale=DH ** -0.5).then_inc(s("q_high"), 1)
                for n in range(2):
                    act.wait_ge(s("v_mm"), i * 2 + n + 1)
                    act.copy(vn[:, 4 * n:4 * n + 4, :], Z[n][:].rearrange("p (j f) -> p j f", f=P)).then_inc(s("v"), 1)

                def exp_of_z(u):
                    act.wait_ge(s("z"), i * NU + u + 1)
                    if u >= 4:
                        act.wait_ge(s("sp"), i * NU + u - 3)
                    act.activation(E[u % 4][:, span(u)], Z[u % NZ][:, span(u)], ACT.Exp).then_inc(s("exp"), 1)

                def log_of_e(u):
                    act.wait_ge(s("capped"), i * NU + u + 1)
                    act.activation(E[u % 4][:, span(u)], E[u % 4][:, span(u)], ACT.Ln, bias=1.0).then_inc(s("log"), 1)

                def weight(u):
                    act.wait_ge(s("tri_mm"), i * NU + u + 1)
                    if u >= 4:
                        act.wait_ge(s("v_mul"), i * NU + u - 3)
                    act.activation(W[u % 4][:, span(u)], Z[u % NZ][:, span(u)], ACT.Exp).then_inc(s("weight"), 1)

                for u in range(-AHEAD, NU):
                    if u + AHEAD < NU:
                        exp_of_z(u + AHEAD)
                    if u >= 0:
                        weight(u)
                    if u + AHEAD < NU:
                        log_of_e(u + AHEAD)
                for h in range(2):
                    for c in range(QC):
                        act.wait_ge(s("v_mul"), i * NU + NU)
                        act.copy(O[:, PER * c:PER * (c + 1), DH * h:DH * h + DH],
                                 OB[h][c][:, 0:PER * DH].rearrange("p (j v) -> p j v", v=DH)).then_inc(s("o"), 1)
                act.wait_ge(s("o"), i * 4 + 4)
                act.activation(osq[:], O[:], ACT.Square).then_inc(s("osq"), 1)
                act.wait_ge(s("mean"), i + 1)
                act.activation(small[:, 0, :], small[:, 0, :], ACT.Sqrt).then_inc(s("root"), 1)
                act.wait_ge(s("gain"), i + 1)
                for n in range(2):
                    act.wait_ge(s("back"), i * 2 + n + 1)
                    act.activation(outT[:, n * HALF:(n + 1) * HALF], Z[n][:], ACT.Copy, scale=small_gain[:]
                                   ).then_inc(s("mixed"), 1)
                pair_end(act, i)

        @block.vector
        def _(dve):
            dve.tensor_scalar(tri[:], mask["to_diag"], -1.0, None, ALU.mult)
            dve.tensor_scalar(ones[:], mask["ones"], -1.0, None, ALU.mult).then_inc(s("signs"), 1)
            with dve.Fori(0, PAIRS) as i:
                dve.tensor_copy(small_gain[:], col[:, bass.ds(i + COL["sb_norm_g"], 1)]).then_inc(s("gain"), 1)
                for h in range(2):
                    dve.wait_ge(s("k_high"), i * 2 + h + 1)
                    dve.tensor_tensor(kS[h][DH:P, :], kd[h][DH:P, :], kS[h][DH:P, :].bitcast(F32), ALU.subtract
                                      ).then_inc(s("k"), 1)
                    dve.wait_ge(s("q_high"), i * 2 + h + 1)
                    dve.scalar_tensor_tensor(qL[h][:], qd[h][:], DH ** -0.5, qH[h][:].bitcast(F32),
                                             ALU.mult, ALU.subtract).then_inc(s("q"), 1)

                def cap(u):
                    dve.wait_ge(s("exp"), i * NU + u + 1)
                    dve.tensor_scalar(E[u % 4][:, span(u)], E[u % 4][:, span(u)], CAP, None, ALU.min
                                      ).then_inc(s("capped"), 1)

                def softplus(u):
                    h, c, kb, off, first = UNITS[u]
                    dve.wait_ge(s("log"), i * NU + u + 1)
                    if u >= 4:
                        dve.wait_ge(s("tri_mm"), i * NU + u - 3)
                        dve.wait_ge(s("sum"), i * NU + u - 3)
                    diag = kb >= PER * c
                    m = dve.tensor_tensor(SP[u % 4][:, span(u)], Z[u % NZ][:, span(u)], E[u % 4][:, span(u)], ALU.max)
                    if diag:
                        m.then_inc(s("diag"), 1)
                        D = sum(1 for x in UNITS[:u + 1] if x[2] >= PER * x[1])
                        ND = sum(1 for x in UNITS if x[2] >= PER * x[1])
                        dve.wait_ge(s("diag"), i * ND + D)
                        w = SP[u % 4][:, off:off + P]
                        m = dve.tensor_tensor(w, w, mask["above"], ALU.mult)
                    m.then_inc(s("sp"), 1)

                for u in range(NU):
                    cap(u)
                    softplus(u)
                dve.wait_ge(s("osq"), i + 1)
                dve.tensor_reduce(small[:, 0, :], osq[:].rearrange("p j (h v) -> p (j h) v", v=DH), AX.X, ALU.add
                                  ).then_inc(s("ssum"), 1)
                dve.wait_ge(s("ssum"), i + 1)
                dve.tensor_scalar(small[:, 0, :], small[:, 0, :], 1.0 / DH, EPS, ALU.mult, ALU.add).then_inc(s("mean"), 1)
                dve.wait_ge(s("root"), i + 1)
                dve.reciprocal(small[:, 1, :], small[:, 0, :]).then_inc(s("rstd"), 1)
                dve.wait_ge(s("rstd"), i + 1)
                o3 = O[:].rearrange("p j (h v) -> p (j h) v", v=DH)
                dve.tensor_tensor(o3, o3, small[:, 1, :].unsqueeze(2).to_broadcast([P, 2 * TB, DH]), ALU.mult
                                  ).then_inc(s("normed"), 1)
                pair_end(dve, i)

        @block.tensor
        def _(pe):
            pe.wait_ge(s("signs"), 1)
            with pe.Fori(0, PAIRS) as i:
                pe.wait_ge(s("in_v"), i * 16 + 16)
                for n in range(2):
                    for j in range(4):
                        m = pe.transpose(Z[n][:, j * P:(j + 1) * P], vp[:, (4 * n + j) * P:(4 * n + j + 1) * P], ident[:])
                    m.then_inc(s("v_mm"), 1)
                pe.wait_ge(s("k"), i * 2 + 2)
                pe.wait_ge(s("q"), i * 2 + 2)
                pe.wait_ge(s("v"), i * 2 + 2)

                def scores(u):
                    h, c, kb, off, first = UNITS[u]
                    if u >= NZ:
                        pe.wait_ge(s("weight"), i * NU + u - NZ + 1)
                    qs = slice(c * HALF + off, (c + 1) * HALF)
                    pe.matmul(Z[u % NZ][:, span(u)], kS[h][:, kb * P:(kb + 1) * P], qL[h][:, qs], start=True, stop=False)
                    pe.matmul(Z[u % NZ][:, span(u)], kS[h][:, kb * P:(kb + 1) * P], qH[h][:, qs], start=False, stop=True
                              ).then_inc(s("z"), 1)

                nth = [0, 0]

                def sums(u):
                    h, c, kb, off, first = UNITS[u]
                    rd = R[h][nth[h] % 2]
                    nth[h] += 1
                    pe.wait_ge(s("sp"), i * NU + u + 1)
                    z = Z[u % NZ][:, span(u)]
                    m = pe.matmul(z, tri[:], SP[u % 4][:, span(u)], start=False, stop=True, skip_group_check=True)
                    if not first:
                        pe.wait_ge(s("cut"), i * NU + u - 1)
                        m = pe.matmul(z, ones[:], rd[:, span(u)], start=False, stop=True, skip_group_check=True)
                    m.then_inc(s("tri_mm"), 1)

                opened = set()

                def values(u):
                    h, c, kb, off, first = UNITS[u]
                    pe.wait_ge(s("cut"), i * NU + u + 1)
                    pe.wait_ge(s("weight"), i * NU + u + 1)
                    for j in range(off // P, PER):
                        m = pe.matmul(OB[h][c][:, j * DH:(j + 1) * DH], W[u % 4][:, j * P:(j + 1) * P],
                                      vn[:, kb, DH * h:DH * h + DH], start=(h, c) not in opened, stop=True,
                                      skip_group_check=True)
                        opened.add((h, c))
                    m.then_inc(s("v_mul"), 1)

                for u in range(-AHEAD, NU + 1):
                    if u + AHEAD < NU:
                        scores(u + AHEAD)
                    if 0 <= u < NU:
                        sums(u)
                    if u >= 1:
                        values(u - 1)
                pe.wait_ge(s("normed"), i + 1)
                for n in range(2):
                    for j in range(4):
                        m = pe.transpose(Z[n][:, j * P:(j + 1) * P], O[:, 4 * n + j, :], ident[:])
                    m.then_inc(s("back"), 1)
                pair_end(pe, i)


def hybrid_block(nc, args, out):
    proj = nc.dram_tensor("projected", [IN_W, T], F32, kind="Internal").ap()
    mixed = nc.dram_tensor("mixed", [MIX, T], F32, kind="Internal").ap()
    x1 = nc.dram_tensor("x_after_mixers", [T, D], F32, kind="Internal").ap()
    with ExitStack() as st:
        r = Region(nc, st, "all")
        con = {"ident": r.sb("ident", [P, P]), "col": r.sb("col", [P, P])}
        with ExitStack() as mixers:
            m = Region(nc, mixers, "mix")
            con["masks"], con["levels"] = m.sb("masks", [P, len(MASKS), P]), m.sb("levels", [P, 6, P])
            constants(nc, con, args)
            projection(nc, con, args["x"], args["w_in"], proj)
            rwkv(nc, con, args, proj, mixed)
            gla(nc, con, args, proj, mixed)
            stick_breaking(nc, con, args, proj, mixed)
        hH, hL = r.sb("hH", [P, KB, T], F32R), r.sb("hL", [P, KB, T], F32R)
        output_projection(nc, con, args["x"], mixed, args["w_out"], args["post_mix_g"], args["pre_ffn_g"],
                          x1, hH, hL)
        feed_forward(nc, con, x1, args["w_ff1"], args["w_ff2"], args["post_ffn_g"], hH, hL, out)


_INS = ["x", "pre_mix_g", "w_in", "sb_norm_g", "rw_mu", "rw_w0", "rw_w_up", "rw_a0", "rw_a_up", "rw_g_up",
        "rw_k_k", "rw_k_a", "rw_r_k", "rw_gn_g", "rw_gn_b", "gla_gate_up", "gla_gate_b", "gla_norm_g",
        "w_out", "post_mix_g", "pre_ffn_g", "w_ff1", "w_ff2", "post_ffn_g"]


def kernel(**inputs):
    import numpy as np
    import concourse.bacc as bacc
    from concourse.bass_utils import run_bass_kernel_spmd

    nc = bacc.Bacc("TRN2", target_bir_lowering=False, num_devices=1)
    arrays, args = {}, {}
    for name in _INS:
        a = np.ascontiguousarray(inputs[name])
        arrays[f"in_{name}"] = a
        args[name] = nc.dram_tensor(f"in_{name}", a.shape, mybir.dt.from_np(a.dtype), kind="ExternalInput").ap()
    out = nc.dram_tensor("out_x", [1, T, D], F32, kind="ExternalOutput").ap()
    hybrid_block(nc, args, out)
    r = run_bass_kernel_spmd(nc, [arrays], core_ids=[0])
    return r.results[0]["out_x"]
```

```python
from contextlib import ExitStack

import concourse.bass as bass
from concourse import mybir

ALU = mybir.AluOpType
ACT = mybir.ActivationFunctionType
AX = mybir.AxisListType
F32 = mybir.dt.float32
F32R = mybir.dt.float32r
U32 = mybir.dt.uint32


P = 128
D = 1024
T = 1024
KB = D // P
TB = T // P
HALF = 512
NH = T // HALF
SBW = 384
RWW = 384
PAIRS = 3
IN_W = 3216
MIX = 1024
DFF = 4096
EPS = 1e-6
EXP_LN = "natural_log_exp_and_others"
GN_EPS = 64e-5
C = 64

SB_Q, SB_K, SB_V = 0, 384, 768
RW_R, RW_K, RW_V, RW_LOW = 1152, 1536, 1920, 2304
GLA_Q, GLA_K, GLA_V, GLA_GD, GLA_G = 2432, 2560, 2688, 2944, 2960

PARAMS = (("pre_mix_g", 8), ("sb_norm_g", 3), ("rw_w0", 3), ("rw_a0", 3), ("rw_k_k", 3), ("rw_k_a", 3),
          ("rw_r_k", 3), ("rw_gn_g", 3), ("rw_gn_b", 3), ("rw_mu", 10), ("gla_gate_b", 1), ("gla_norm_g", 2))
RW_COLS = ("w0", "a0", "k_k", "k_a", "r_k", "gn_g", "gn_b", "mu_r", "mu_k", "mu_v")


def param_columns():
    at, out = 0, {}
    for name, n in PARAMS:
        out[name] = at
        at += n
    return out, at


COL, NCOL = param_columns()


class Region:

    def __init__(self, nc, stack, tag):
        self.nc, self.stack, self.tag = nc, stack, tag
        self.semaphores, self.numbers = ExitStack(), []
        stack.callback(self.clear)

    def sb(self, name, shape, dt=F32):
        return self.stack.enter_context(self.nc.sbuf_tensor(f"{self.tag}_{name}", shape, dt))

    def bank(self, name, cols=HALF):
        return self.stack.enter_context(self.nc.psum_tensor(f"{self.tag}_ps_{name}", [P, cols], F32))

    def sem(self, name):
        got = self.semaphores.enter_context(self.nc.semaphore(f"{self.tag}_{name}"))
        self.numbers.append(got.num)
        return got

    def clear(self):
        if self.numbers:
            runs = []
            for n in sorted(self.numbers):
                if runs and runs[-1].stop == n:
                    runs[-1] = range(runs[-1].start, n + 1)
                else:
                    runs.append(range(n, n + 1))
            with self.nc.Block() as block:
                @block.sync
                def _(sp):
                    for run in runs:
                        sp.sem_clear(run)
        self.semaphores.close()


MASKS = ("ones", "above", "from_diag", "below", "to_diag", "same16", "same32", "same64",
         "up16", "up64", "upd64", "low16", "low32", "low64")
SB_MASKS = ("ones", "to_diag", "above")


class Rows:

    def __init__(self, nc, stack, x, w_in):
        r = Region(nc, stack, "rows")
        self.xt, self.sq, self.ss = r.sb("xt", [P, TB, D]), r.sb("sq", [P, D]), r.sb("ss", [P, TB])
        self.raw = [r.sb(f"raw{s}", [P, KB, P]) for s in range(2)]
        self.x_in = [r.sem(f"x_in{j}") for j in range(TB)]
        self.w_in = [r.sem(f"w_in{s}") for s in range(2)]
        self.squared, self.mean, self.rooted = r.sem("squared"), r.sem("mean"), r.sem("rooted")
        self.inverse, self.scaled = r.sem("inverse"), r.sem("scaled")
        self.x_d = x.rearrange("b (j p) d -> (b j) p d", p=P)
        self.w_d = w_in.rearrange("l (k p) n -> p (l k) n", p=P)

    def load(self, sp, tiles):
        for j in tiles:
            sp.dma_start(self.xt[:, j, :], self.x_d[j]).then_inc(self.x_in[j], 16)

    def load_weights(self, sp):
        for s in range(2):
            sp.dma_start(self.raw[s][:], self.w_d[:, :, s * P:(s + 1) * P]).then_inc(self.w_in[s], 16)

    def square(self, act):
        for j in range(TB + 1):
            if j < TB:
                act.wait_ge(self.x_in[j], 16)
                if j:
                    act.wait_ge(self.squared, j)
                act.activation(self.sq[:], self.xt[:, j, :], ACT.Square, accum_out=self.ss[:, j:j + 1]
                               ).then_inc(self.squared, 1)
            if j:
                act.wait_ge(self.mean, j)
                act.activation(self.ss[:, j - 1:j], self.ss[:, j - 1:j], ACT.Sqrt).then_inc(self.rooted, 1)

    def average(self, dve, j):
        s = self.ss[:, j:j + 1]
        dve.wait_ge(self.squared, j + 1)
        dve.tensor_scalar(s, s, 1.0 / D, EPS, ALU.mult, ALU.add).then_inc(self.mean, 1)

    def scale(self, dve, j):
        s = self.ss[:, j:j + 1]
        dve.wait_ge(self.rooted, j + 1)
        dve.reciprocal(s, s).then_inc(self.inverse, 1)
        dve.wait_ge(self.inverse, j + 1)
        dve.tensor_scalar(self.xt[:, j, :], self.xt[:, j, :], s, None, ALU.mult).then_inc(self.scaled, 1)


def constants(nc, con, args, first=None):
    ident, masks = con["ident"], con["masks"]
    m = {name: masks[:, n, :] for n, name in enumerate(MASKS)}
    levels = con["levels"]
    with ExitStack() as st:
        r = Region(nc, st, "con")
        rows = r.sb("rows", [P, P])
        same = [r.sb(f"same{n}", [P, P]) for n in range(2)]
        colp = r.bank("colp")
        loaded, zeroed, filled = r.sem("loaded"), r.sem("zeroed"), r.sem("filled")
        turned, made, cut = r.sem("turned"), r.sem("made"), r.sem("cut")
        block = st.enter_context(nc.Block())

        @block.sync
        def _(sp):
            if first:
                first.load(sp, range(0, TB // 2))
            sp.wait_ge(zeroed, 2)
            for name, n in PARAMS:
                at = COL[name]
                sp.dma_start(rows[at:at + n, :],
                             args[name].rearrange("l (n p) -> (l n) p", p=P)).then_inc(loaded, 16)
            if first:
                first.load(sp, range(TB // 2, TB))
                first.load_weights(sp)

        if first:
            @block.scalar
            def _(act):
                first.square(act)

        @block.gpsimd
        def _(pool):
            pool.memset(ident[:], 0.0).then_inc(zeroed, 1)
            pool.memset(rows[:], 0.0).then_inc(zeroed, 1)
            pool.wait_ge(zeroed, 2)
            pool.affine_select(out=ident[:], in_=ident[:], compare_op=ALU.not_equal, fill=1.0, base=0,
                               pattern=[[-1, P]], channel_multiplier=1).then_inc(filled, 1)
            pool.memset(m["ones"], 1.0).then_inc(made, 1)
            done = [1]

            def select(out, in_, compare, base, pattern, step):
                pool.wait_ge(made, done[0])
                pool.affine_select(out=out, in_=in_, compare_op=compare, fill=0.0, base=base,
                                   pattern=pattern, channel_multiplier=step).then_inc(made, 1)
                done[0] += 1

            select(m["above"], m["ones"], ALU.is_gt, 0, [[1, P]], -1)
            select(m["from_diag"], m["ones"], ALU.is_ge, 0, [[1, P]], -1)
            select(m["below"], m["ones"], ALU.is_gt, 0, [[-1, P]], 1)
            select(m["to_diag"], m["ones"], ALU.is_ge, 0, [[-1, P]], 1)

            def blocks(out, size):
                n = P // size
                o = out.rearrange("p (n s) -> p n s", s=size)
                select(o, m["ones"].rearrange("p (n s) -> p n s", s=size), ALU.is_ge, 0, [[-size, n], [0, size]], 1)
                select(o, o, ALU.is_ge, size - 1, [[size, n], [0, size]], -1)

            for size in (16, 32, 64):
                blocks(m[f"same{size}"], size)
            for n in range(6):
                if n >= 1:
                    pool.wait_ge(cut, 2 * n)
                blocks(same[n % 2][:], 2 << n)

        @block.tensor
        def _(pe):
            pe.wait_ge(loaded, 16 * len(PARAMS))
            pe.wait_ge(filled, 1)
            pe.transpose(colp[:, 0:P], rows[:], ident[:]).then_inc(turned, 1)

        @block.vector
        def _(dve):
            SELECTS = 5 + 6
            for n in range(6):
                dve.wait_ge(made, SELECTS + 2 * (n + 1))
                before = ident[:] if n == 0 else same[(n - 1) % 2][:]
                dve.tensor_tensor(levels[:, n, :], same[n % 2][:], before, ALU.subtract).then_inc(cut, 1)
                dve.wait_ge(cut, 2 * n + 1)
                dve.tensor_tensor(levels[:, n, :], levels[:, n, :], m["above"], ALU.mult).then_inc(cut, 1)
                if first:
                    first.average(dve, n)
                    if n:
                        first.scale(dve, n - 1)
            done = 12
            for name, a, b, op in (("up16", "same16", "above", ALU.mult), ("up64", "same64", "above", ALU.mult),
                                   ("upd64", "same64", "from_diag", ALU.mult),
                                   ("low16", "same16", "below", ALU.mult),
                                   ("low64", "same64", "same32", ALU.subtract),
                                   ("low32", "same32", "same16", ALU.subtract),
                                   ("low64", "low64", "below", ALU.mult),
                                   ("low32", "low32", "below", ALU.mult)):
                dve.wait_ge(cut, done)
                dve.tensor_tensor(m[name], m[a], m[b], op).then_inc(cut, 1)
                done += 1
            for n, name in enumerate(SB_MASKS):
                dve.tensor_copy(con["sb_masks"][:, n, :], m[name]).then_inc(cut, 1)
            dve.wait_ge(turned, 1)
            dve.tensor_copy(con["col"][:], colp[:, 0:P]).then_inc(cut, 1)
            if first:
                for j in range(6, TB):
                    first.average(dve, j)
                    first.scale(dve, j - 1)
                first.scale(dve, TB - 1)


def projection(nc, con, first, proj):
    ident, col = con["ident"], con["col"]
    PAIRED = IN_W // (2 * P)
    REST = IN_W - PAIRED * 2 * P
    NARROW = REST - P
    with ExitStack() as st:
        r = Region(nc, st, "prj")
        xt, raw, w_in_s, w_d = first.xt, first.raw, first.w_in, first.w_d
        hH, hL = r.sb("hH", [P, KB, T], F32R), r.sb("hL", [P, KB, T], F32R)
        wH = [r.sb(f"wH{s}", [P, KB, P], F32R) for s in range(2)]
        wL = [r.sb(f"wL{s}", [P, KB, P], F32R) for s in range(2)]
        stage = [r.sb(f"stage{s}", [P, T]) for s in range(2)]
        tbank = [r.bank(f"tb{i}") for i in range(4)]
        bank = [[r.bank(f"b{s}{h}") for h in range(NH)] for s in range(2)]
        turned, high, low = r.sem("turned"), r.sem("high"), r.sem("low")
        w_high, w_low = [r.sem(f"w_high{s}") for s in range(2)], [r.sem(f"w_low{s}") for s in range(2)]
        multiplied = [r.sem(f"mul{s}") for s in range(2)]
        ev0, ev1 = [r.sem(f"ev0_{s}") for s in range(2)], [r.sem(f"ev1_{s}") for s in range(2)]
        stored = [r.sem(f"stored{s}") for s in range(2)]
        block = st.enter_context(nc.Block())

        @block.sync
        def _(sp):
            for s in range(2):
                sp.sem_inc(stored[s], 16)

            def load(s, i, at, n):
                sp.wait_ge(w_high[s], i + 1)
                sp.wait_ge(w_low[s], i + 1)
                sp.dma_start(raw[s][:, :, 0:n], w_d[:, :, bass.ds(at, n)]).then_inc(w_in_s[s], 16)

            def store(s, i, at, n):
                sp.wait_ge(ev0[s], i + 2)
                sp.wait_ge(ev1[s], i + 2)
                sp.dma_start(proj[bass.ds(at, n), :], stage[s][0:n, :]).then_inc(stored[s], 16)

            with sp.Fori(0, PAIRED - 1) as i:
                for s in range(2):
                    load(s, i + 1, (i + 1) * 2 * P + s * P, P)
                for s in range(2):
                    store(s, i, i * 2 * P + s * P, P)
            for s, n in ((0, P), (1, NARROW)):
                load(s, PAIRED, PAIRED * 2 * P + s * P, n)
            for s in range(2):
                store(s, PAIRED - 1, (PAIRED - 1) * 2 * P + s * P, P)
            for s, n in ((0, P), (1, NARROW)):
                store(s, PAIRED, PAIRED * 2 * P + s * P, n)
            for s in range(2):
                sp.wait_ge(stored[s], 16 * (PAIRED + 2))

        @block.scalar
        def _(act):
            for s in range(2):
                act.sem_inc(w_high[s], 1)
                act.sem_inc(ev0[s], 1)
            def block_work(s, i, n):
                act.wait_ge(w_in_s[s], i * 16 + 16)
                act.wait_ge(multiplied[s], i + 1)
                act.copy(wH[s][:, :, 0:n], raw[s][:, :, 0:n]).then_inc(w_high[s], 1)

            for g in range(KB * NH):
                if g == KB:
                    block_work(0, 0, P)
                    block_work(1, 0, P)
                kb, h = g % KB, g // KB
                act.wait_ge(turned, g + 1)
                act.activation(hH[:, kb, h * HALF:(h + 1) * HALF], tbank[g % 4][:], ACT.Copy,
                               scale=col[:, COL["pre_mix_g"] + kb:COL["pre_mix_g"] + kb + 1]).then_inc(high, 1)

            def take(s, i, n):
                act.wait_ge(multiplied[s], i + 2)
                act.wait_ge(stored[s], i * 16 + 16)
                act.copy(stage[s][0:n, 0:HALF], bank[s][0][0:n, :]).then_inc(ev0[s], 1)

            with act.Fori(0, PAIRED - 1) as i:
                for s in range(2):
                    take(s, i, P)
                    block_work(s, i + 1, P)
            for s, n in ((0, P), (1, NARROW)):
                take(s, PAIRED - 1, P)
                block_work(s, PAIRED, n)
            for s, n in ((0, P), (1, NARROW)):
                take(s, PAIRED, n)

        @block.vector
        def _(dve):
            for s in range(2):
                dve.sem_inc(w_low[s], 1)
                dve.sem_inc(ev1[s], 1)
            def split_low(s, i, n):
                dve.wait_ge(w_high[s], i + 2)
                dve.wait_ge(multiplied[s], i + 1)
                dve.tensor_tensor(wL[s][:, :, 0:n], raw[s][:, :, 0:n], wH[s][:, :, 0:n].bitcast(F32),
                                  ALU.subtract).then_inc(w_low[s], 1)

            for g in range(KB * NH):
                if g == KB:
                    split_low(0, 0, P)
                    split_low(1, 0, P)
                kb, h = g % KB, g // KB
                dve.wait_ge(high, g + 1)
                hs = slice(h * HALF, (h + 1) * HALF)
                dve.scalar_tensor_tensor(hL[:, kb, hs], tbank[g % 4][:],
                                         col[:, COL["pre_mix_g"] + kb:COL["pre_mix_g"] + kb + 1],
                                         hH[:, kb, hs].bitcast(F32), ALU.mult, ALU.subtract).then_inc(low, 1)

            def take(s, i, n):
                dve.wait_ge(multiplied[s], i + 2)
                dve.wait_ge(stored[s], i * 16 + 16)
                dve.tensor_copy(stage[s][0:n, HALF:T], bank[s][1][0:n, :]).then_inc(ev1[s], 1)

            with dve.Fori(0, PAIRED - 1) as i:
                for s in range(2):
                    take(s, i, P)
                    split_low(s, i + 1, P)
            for s, n in ((0, P), (1, NARROW)):
                take(s, PAIRED - 1, P)
                split_low(s, PAIRED, n)
            for s, n in ((0, P), (1, NARROW)):
                take(s, PAIRED, n)

        @block.tensor
        def _(pe):
            for s in range(2):
                pe.sem_inc(multiplied[s], 1)
            pe.wait_ge(first.scaled, TB)

            def turn(g):
                kb, h = g % KB, g // KB
                if g >= 4:
                    pe.wait_ge(low, g - 3)
                for q in range(4):
                    j = h * 4 + q
                    m = pe.transpose(tbank[g % 4][:, q * P:(q + 1) * P], xt[:, j, kb * P:(kb + 1) * P], ident[:])
                m.then_inc(turned, 1)

            def half_product(s, h):
                hs = slice(h * HALF, (h + 1) * HALF)
                for kb in range(KB):
                    for q, (w, a) in enumerate(((wL, hH), (wH, hL), (wH, hH))):
                        m = pe.matmul(bank[s][h][:], w[s][:, kb, :], a[:, kb, hs],
                                      start=(kb == 0 and q == 0), stop=(kb == KB - 1 and q == 2))
                return m

            def products(s, i):
                pe.wait_ge(w_low[s], i + 2)
                pe.wait_ge(ev0[s], i + 1)
                pe.wait_ge(ev1[s], i + 1)
                half_product(s, 0)
                half_product(s, 1).then_inc(multiplied[s], 1)

            for g in range(KB + 4):
                turn(g)
            pe.wait_ge(w_low[0], 2)
            half_product(0, 0)
            for g in range(KB + 4, KB * NH):
                turn(g)
            pe.wait_ge(w_low[1], 2)
            half_product(1, 0)
            pe.wait_ge(low, KB * NH)
            for s in range(2):
                half_product(s, 1).then_inc(multiplied[s], 1)
            with pe.Fori(1, PAIRED) as i:
                for s in range(2):
                    products(s, i)
            products(0, PAIRED)
            products(1, PAIRED)


def broadcast_rows(ap, n=P):
    return ap.to_broadcast((n, ap.shape[1]))


class Ahead:

    def __init__(self, nc, stack, mixed, w_out, hH, hL):
        r = Region(nc, stack, "ahead")
        self.wH, self.wL = r.sb("wH", [P, KB, HALF], F32R), r.sb("wL", [P, KB, HALF], F32R)
        self.raw = [r.sb(f"raw{s}", [P, D]) for s in range(2)]
        self.raw_in = [r.sem(f"raw_in{s}") for s in range(2)]
        self.high, self.low = r.sem("high"), r.sem("low")
        self.m_d = mixed.rearrange("(k p) t -> k p t", p=P)
        self.w_d = w_out.rearrange("l (k p) n -> (l k) p n", p=P)
        self.pieces = ([(self.m_d[k], T, hH[:, k, :], hL[:, k, :]) for k in range(SBW // P, KB)]
                       + [(self.w_d[k][:, 0:HALF], HALF, self.wH[:, k, :], self.wL[:, k, :]) for k in range(KB)])

    def load(self, sp):
        for n, (src, width, _, _) in enumerate(self.pieces):
            if n >= 2:
                sp.wait_ge(self.low, n - 1)
            sp.dma_start(self.raw[n % 2][:, 0:width], src).then_inc(self.raw_in[n % 2], 16)

    def split_high(self, act, n):
        _, width, h, _ = self.pieces[n]
        act.wait_ge(self.raw_in[n % 2], 16 * (n // 2 + 1))
        act.copy(h, self.raw[n % 2][:, 0:width]).then_inc(self.high, 1)

    def split_low(self, dve, n):
        _, width, h, l = self.pieces[n]
        dve.wait_ge(self.high, n + 1)
        dve.tensor_tensor(l, self.raw[n % 2][:, 0:width], h.bitcast(F32), ALU.subtract).then_inc(self.low, 1)


def output_projection(nc, con, ahead, x, post_g, pre_g, x1, hH, hL):
    ident = con["ident"]
    with ExitStack() as st:
        r = Region(nc, st, "out")
        raw = [r.sb(f"raw{s}", [P, D]) for s in range(4)]
        mH, mL, wH, wL, m_d, w_d = hH, hL, ahead.wH, ahead.wL, ahead.m_d, ahead.w_d
        half0 = r.sb("half0", [P, TB, HALF])
        y, xt = raw[0:2], raw[2:4]
        postB, preB = r.sb("postB", [P, D]), r.sb("preB", [P, D])
        ss = r.sb("ss", [P, TB, 4])
        bank = [r.bank(f"b{i}") for i in range(4)]
        tbank = [r.bank(f"tb{i}") for i in range(4)]
        raw_in = [r.sem(f"raw_in{s}") for s in range(4)]
        gains = r.sem("gains")
        x_in = [r.sem(f"x_in{s}") for s in range(2)]
        high, low = r.sem("high"), r.sem("low")
        multiplied, kept, squared = r.sem("multiplied"), r.sem("kept"), r.sem("squared")
        mean, root, inv = r.sem("mean"), r.sem("root"), r.sem("inv")
        added, squared1 = r.sem("added"), r.sem("squared1")
        mean1, root1, inv1 = r.sem("mean1"), r.sem("root1"), r.sem("inv1")
        normed, turned, hhigh, hlow, stored = (r.sem("normed"), r.sem("turned"), r.sem("hhigh"),
                                               r.sem("hlow"), r.sem("stored"))
        x_d = x.rearrange("b (j p) d -> (b j) p d", p=P)
        x1_d = x1.rearrange("(j p) d -> j p d", p=P)
        NM = SBW // P
        pieces = [("m", k) for k in range(NM)] + [("w1", k) for k in range(KB)]
        block = st.enter_context(nc.Block())

        def piece(n):
            kind, k = pieces[n]
            width = T if kind == "m" else HALF
            src = raw[n % 4][:, 0:width]
            if kind == "m":
                return src, mH[:, k, :], mL[:, k, :]
            return src, wH[:, k, :], wL[:, k, :]

        @block.sync
        def _(sp):
            for n, (kind, k) in enumerate(pieces):
                if n >= 4:
                    sp.wait_ge(low, n - 3)
                if kind == "m":
                    sp.dma_start(raw[n % 4][:], m_d[k]).then_inc(raw_in[n % 4], 16)
                else:
                    c = int(kind[1]) * HALF
                    sp.dma_start(raw[n % 4][:, 0:HALF], w_d[k][:, c:c + HALF]).then_inc(raw_in[n % 4], 16)
                if n == 3:
                    sp.dma_start(postB[:], broadcast_rows(post_g)).then_inc(gains, 16)
                    sp.dma_start(preB[:], broadcast_rows(pre_g)).then_inc(gains, 16)
            sp.wait_ge(low, len(pieces))
            for j in range(TB):
                if j >= 2:
                    sp.wait_ge(normed, j - 1)
                    sp.wait_ge(stored, 16 * (j - 1))
                sp.dma_start(xt[j % 2][:], x_d[j]).then_inc(x_in[j % 2], 16)
                if j:
                    sp.wait_ge(added, j)
                    sp.dma_start(x1_d[j - 1], xt[(j - 1) % 2][:]).then_inc(stored, 16)
            sp.wait_ge(added, TB)
            sp.dma_start(x1_d[TB - 1], xt[(TB - 1) % 2][:]).then_inc(stored, 16)
            sp.wait_ge(stored, 16 * TB)

        @block.scalar
        def _(act):
            for n in range(len(pieces)):
                act.wait_ge(raw_in[n % 4], 16 * (n // 4 + 1))
                if n == NM:
                    act.wait_ge(multiplied, TB)
                src, dst, _ = piece(n)
                act.copy(dst, src).then_inc(high, 1)
            def residual(j):
                ys = y[j % 2]
                act.wait_ge(kept, j + 1)
                if j == 0:
                    act.wait_ge(low, len(pieces))
                if j >= 2:
                    act.wait_ge(turned, 2 * j - 2)
                act.activation(ys[:, 0:HALF], half0[:, j, :], ACT.Square,
                               accum_out=ss[:, j, 0:1]).then_inc(squared, 1)
                act.wait_ge(multiplied, TB + j + 1)
                act.activation(ys[:, HALF:D], bank[j % 4][:], ACT.Square,
                               accum_out=ss[:, j, 1:2]).then_inc(squared, 1)
                act.wait_ge(mean, j + 1)
                act.activation(ss[:, j, 0:1], ss[:, j, 0:1], ACT.Sqrt).then_inc(root, 1)

            def normed_rows(j):
                act.wait_ge(added, j + 1)
                act.activation(y[j % 2][:], xt[j % 2][:], ACT.Square, accum_out=ss[:, j, 2:3]).then_inc(squared1, 1)
                act.wait_ge(mean1, j + 1)
                act.activation(ss[:, j, 2:3], ss[:, j, 2:3], ACT.Sqrt).then_inc(root1, 1)
                for b in range(2):
                    act.wait_ge(turned, 2 * j + b + 1)
                    act.copy(hH[:, 4 * b:4 * b + 4, j * P:(j + 1) * P],
                             tbank[(2 * j + b) % 4][:].rearrange("p (k t) -> p k t", k=4)).then_inc(hhigh, 1)

            for j in range(TB + 1):
                if j < TB:
                    residual(j)
                if j:
                    normed_rows(j - 1)

        @block.vector
        def _(dve):
            for n in range(NM):
                dve.wait_ge(high, n + 1)
                src, h, l = piece(n)
                dve.tensor_tensor(l, src, h.bitcast(F32), ALU.subtract).then_inc(low, 1)
            for j in range(TB):
                dve.wait_ge(multiplied, j + 1)
                dve.tensor_copy(half0[:, j, :], bank[j % 4][:]).then_inc(kept, 1)
            for n in range(NM, len(pieces)):
                dve.wait_ge(high, n + 1)
                src, h, l = piece(n)
                dve.tensor_tensor(l, src, h.bitcast(F32), ALU.subtract).then_inc(low, 1)
            dve.wait_ge(gains, 32)

            def residual(j):
                ys, xs = y[j % 2], xt[j % 2]
                s0, s1 = ss[:, j, 0:1], ss[:, j, 1:2]
                dve.wait_ge(squared, 2 * j + 2)
                dve.tensor_tensor(s0, s0, s1, ALU.add).then_inc(inv, 1)
                dve.wait_ge(inv, 4 * j + 1)
                dve.tensor_scalar(s0, s0, 1.0 / D, EPS, ALU.mult, ALU.add).then_inc(mean, 1)
                dve.wait_ge(root, j + 1)
                dve.reciprocal(s0, s0).then_inc(inv, 1)
                dve.wait_ge(inv, 4 * j + 2)
                dve.scalar_tensor_tensor(ys[:, 0:HALF], half0[:, j, :], s0, postB[:, 0:HALF],
                                         ALU.mult, ALU.mult).then_inc(inv, 1)
                dve.scalar_tensor_tensor(ys[:, HALF:D], bank[j % 4][:], s0, postB[:, HALF:D],
                                         ALU.mult, ALU.mult).then_inc(inv, 1)
                dve.wait_ge(inv, 4 * j + 4)
                dve.wait_ge(x_in[j % 2], 16 * (j // 2 + 1))
                dve.tensor_tensor(xs[:], xs[:], ys[:], ALU.add).then_inc(added, 1)

            def normed_rows(j):
                s2 = ss[:, j, 2:3]
                dve.wait_ge(squared1, j + 1)
                dve.tensor_scalar(s2, s2, 1.0 / D, EPS, ALU.mult, ALU.add).then_inc(mean1, 1)
                dve.wait_ge(root1, j + 1)
                dve.reciprocal(s2, s2).then_inc(inv1, 1)
                dve.wait_ge(inv1, j + 1)
                dve.scalar_tensor_tensor(y[j % 2][:], xt[j % 2][:], s2, preB[:], ALU.mult, ALU.mult
                                         ).then_inc(normed, 1)

            def take_low(j):
                for b in range(2):
                    dve.wait_ge(hhigh, 2 * j + b + 1)
                    dst = slice(4 * b, 4 * b + 4)
                    dve.tensor_tensor(hL[:, dst, j * P:(j + 1) * P],
                                      tbank[(2 * j + b) % 4][:].rearrange("p (k t) -> p k t", k=4),
                                      hH[:, dst, j * P:(j + 1) * P].bitcast(F32), ALU.subtract).then_inc(hlow, 1)

            for j in range(TB + 1):
                if j < TB:
                    residual(j)
                if j:
                    normed_rows(j - 1)
                    take_low(j - 1)

        @block.tensor
        def _(pe):
            def product(half, j):
                b = bank[j % 4]
                if half == 0 and j >= 4:
                    pe.wait_ge(kept, j - 3)
                if half == 1 and j >= 4:
                    pe.wait_ge(normed, j - 3)
                if half == 1 and j == 0:
                    pe.wait_ge(kept, TB)
                order = list(range(NM, KB)) + list(range(NM)) if half == 0 else list(range(KB))
                for nth, k in enumerate(order):
                    if j == 0 and half == 0 and k < NM:
                        pe.wait_ge(low, k + 1)
                    if j == 0 and half == 1:
                        pe.wait_ge(low, NM + k + 1)
                    for q, (m, w) in enumerate(((mL, wH), (mH, wL), (mH, wH))):
                        i = pe.matmul(b[:], m[:, k, j * P:(j + 1) * P], w[:, k, :],
                                      start=(nth == 0 and q == 0), stop=(nth == KB - 1 and q == 2))
                i.then_inc(multiplied, 1)

            def turn(j):
                pe.wait_ge(normed, j + 1)
                for b in range(2):
                    n = 2 * j + b
                    if n >= 4:
                        pe.wait_ge(hlow, n - 3)
                    for k in range(4):
                        kb = 4 * b + k
                        i = pe.transpose(tbank[n % 4][:, k * P:(k + 1) * P],
                                         y[j % 2][:, kb * P:(kb + 1) * P], ident[:])
                    i.then_inc(turned, 1)

            for j in range(TB):
                product(0, j)
            for j in range(TB):
                product(1, j)
                if j >= 2:
                    turn(j - 2)
            turn(TB - 2)
            turn(TB - 1)


def feed_forward(nc, con, x1, w1, w2, post_g, hH, hL, out):
    FB = 4
    NE = DFF // (FB * P)
    with ExitStack() as st:
        r = Region(nc, st, "ffn")
        raw1 = [r.sb(f"raw1_{s}", [P, KB, P]) for s in range(2)]
        w1H = [r.sb(f"w1H{s}", [P, KB, P], F32R) for s in range(2)]
        w1L = [r.sb(f"w1L{s}", [P, KB, P], F32R) for s in range(2)]
        raw2 = [r.sb(f"raw2_{s}", [P, D]) for s in range(2)]
        w2H, w2L = r.sb("w2H", [P, FB, D], F32R), r.sb("w2L", [P, FB, D], F32R)
        gH, gL = r.sb("gH", [P, FB, T], F32R), r.sb("gL", [P, FB, T], F32R)
        relu, g32 = r.sb("relu", [P, HALF]), r.sb("g32", [P, HALF])
        acc = r.sb("acc", [P, TB, D])
        postB = r.sb("postB", [P, D])
        ss = r.sb("ss", [P, TB])
        bank = [[r.bank(f"b{s}{h}") for h in range(NH)] for s in range(2)]
        ybank = [r.bank(f"y{i}") for i in range(4)]
        xt = [raw1[s][:].rearrange("p k c -> p (k c)") for s in range(2)]
        w1_in = [r.sem(f"w1_in{s}") for s in range(2)]
        w2_in = [r.sem(f"w2_in{s}") for s in range(2)]
        w1_high, w1_low = [r.sem(f"w1_high{s}") for s in range(2)], [r.sem(f"w1_low{s}") for s in range(2)]
        w2_high, w2_low = r.sem("w2_high"), r.sem("w2_low")
        hidden = [r.sem(f"hidden{s}") for s in range(2)]
        rectified, squared, g_high, g_low = r.sem("rectified"), r.sem("squared"), r.sem("g_high"), r.sem("g_low")
        summed, added, cleared, used = r.sem("summed"), r.sem("added"), r.sem("cleared"), r.sem("used")
        gains, x_in = r.sem("gains"), [r.sem(f"x_in{s}") for s in range(2)]
        ysq, mean, root, inv, final = r.sem("ysq"), r.sem("mean"), r.sem("root"), r.sem("inv"), r.sem("final")
        stored = r.sem("stored")
        w1_d = w1.rearrange("l (k p) n -> p (l k) n", p=P)
        x1_d = x1.rearrange("(j p) d -> j p d", p=P)
        o_d = out.rearrange("b (j p) d -> (b j) p d", p=P)
        w2_flat = w2.rearrange("l f n -> (l f) n")
        block = st.enter_context(nc.Block())
        G = TB * 2

        @block.sync
        def _(sp):
            sp.dma_start(postB[:], broadcast_rows(post_g)).then_inc(gains, 16)

            def load1(s, use, at):
                sp.wait_ge(w1_high[s], use + 1)
                sp.wait_ge(w1_low[s], use + 1)
                sp.dma_start(raw1[s][:], w1_d[:, :, bass.ds(at, P)]).then_inc(w1_in[s], 16)

            def load2(s, use, total, at):
                sp.wait_ge(w2_low, total)
                sp.dma_start(raw2[s][:], w2_flat[bass.ds(at, P), :]).then_inc(w2_in[s], 16)

            for s in range(2):
                load1(s, 0, s * P)

            def slice_loads(e, last):
                for i in range(FB):
                    load2(i % 2, e * 2 + i // 2, e * FB + i + 1, e * (FB * P) + i * P)
                    if i < 2:
                        load1(i, e * 2 + 1, e * (FB * P) + (i + 2) * P)
                    elif not last:
                        load1(i - 2, e * 2 + 2, e * (FB * P) + (i + 2) * P)

            with sp.Fori(0, NE - 1) as e:
                slice_loads(e, False)
            slice_loads(NE - 1, True)
            for j in range(TB):
                if j < 2:
                    sp.wait_ge(w1_high[j], 2 * NE + 1)
                    sp.wait_ge(w1_low[j], 2 * NE + 1)
                else:
                    sp.wait_ge(final, j - 1)
                sp.dma_start(xt[j % 2], x1_d[j]).then_inc(x_in[j % 2], 16)
                if j:
                    sp.wait_ge(final, j)
                    sp.dma_start(o_d[j - 1], acc[:, j - 1, :]).then_inc(stored, 16)
            sp.wait_ge(final, TB)
            sp.dma_start(o_d[TB - 1], acc[:, TB - 1, :]).then_inc(stored, 16)
            sp.wait_ge(stored, 16 * TB)

        W2_AT = {0: (0, 1), 1: (2,), 2: (3,), 3: ()}

        @block.scalar
        def _(act):
            for s in range(2):
                act.sem_inc(w1_high[s], 1)

            def split1(s, use):
                act.wait_ge(w1_in[s], use * 16 + 16)
                act.wait_ge(hidden[s], use + 1)
                act.copy(w1H[s][:], raw1[s][:]).then_inc(w1_high[s], 1)

            def split2(i, e):
                act.wait_ge(w2_in[i % 2], (e * 2 + i // 2) * 16 + 16)
                if i == 0:
                    act.wait_ge(used, e + 1)
                act.copy(w2H[:, i, :], raw2[i % 2][:]).then_inc(w2_high, 1)

            for s in range(2):
                split1(s, 0)

            def slice_work(e, last):
                for i in range(FB):
                    for m in W2_AT[i]:
                        split2(m, e)
                    act.wait_ge(hidden[i % 2], e * 2 + i // 2 + 2)
                    for h in range(NH):
                        n = e * (2 * FB) + 2 * i + h
                        act.activation(relu[:], bank[i % 2][h][:], ACT.Relu).then_inc(rectified, 1)
                        act.wait_ge(rectified, n + 1)
                        act.wait_ge(g_low, n + 1)
                        act.activation(g32[:], relu[:], ACT.Square).then_inc(squared, 1)
                        act.wait_ge(squared, n + 1)
                    if i < 2:
                        split1(i, e * 2 + 1)
                    elif not last:
                        split1(i - 2, e * 2 + 2)

            with act.Fori(0, NE - 1) as e:
                slice_work(e, False)
            slice_work(NE - 1, True)
            for j in range(TB):
                act.wait_ge(added, G * (NE - 1) + 2 * (j + 1) + 1)
                if j:
                    act.wait_ge(ysq, j)
                act.activation(raw2[0][:], acc[:, j, :], ACT.Square,
                               accum_out=ss[:, j:j + 1]).then_inc(ysq, 1)
                act.wait_ge(mean, j + 1)
                act.activation(ss[:, j:j + 1], ss[:, j:j + 1], ACT.Sqrt).then_inc(root, 1)

        @block.gpsimd
        def _(pool):
            pool.memset(acc[:], 0.0).then_inc(cleared, 1)

        @block.vector
        def _(dve):
            for s in range(2):
                dve.sem_inc(w1_low[s], 1)
            dve.sem_inc(w2_low, 2)
            dve.sem_inc(g_low, 1)
            dve.sem_inc(added, 1)
            dve.wait_ge(cleared, 1)

            def split1(s, use):
                dve.wait_ge(w1_high[s], use + 2)
                dve.wait_ge(hidden[s], use + 1)
                dve.tensor_tensor(w1L[s][:], raw1[s][:], w1H[s][:].bitcast(F32), ALU.subtract).then_inc(w1_low[s], 1)

            def split2(i, e):
                dve.wait_ge(w2_high, e * FB + i + 1)
                dve.tensor_tensor(w2L[:, i, :], raw2[i % 2][:], w2H[:, i, :].bitcast(F32),
                                  ALU.subtract).then_inc(w2_low, 1)

            for s in range(2):
                split1(s, 0)

            def slice_work(e, last):
                for i in range(FB):
                    for m in W2_AT[i]:
                        split2(m, e)
                    for h in range(NH):
                        n = e * (2 * FB) + 2 * i + h
                        hs = slice(h * HALF, (h + 1) * HALF)
                        dve.wait_ge(squared, n + 1)
                        dve.tensor_copy(gH[:, i, hs], g32[:]).then_inc(g_high, 1)
                        dve.wait_ge(g_high, n + 1)
                        dve.tensor_tensor(gL[:, i, hs], g32[:], gH[:, i, hs].bitcast(F32),
                                          ALU.subtract).then_inc(g_low, 1)
                    if i < 2:
                        split1(i, e * 2 + 1)
                    elif not last:
                        split1(i - 2, e * 2 + 2)
                for g in range(G):
                    j, dh = g // 2, g % 2
                    ds = slice(dh * HALF, (dh + 1) * HALF)
                    dve.wait_ge(summed, e * G + g + 1)
                    dve.tensor_tensor(acc[:, j, ds], acc[:, j, ds], ybank[g % 4][:], ALU.add).then_inc(added, 1)
                    if last and dh == 1 and j >= 1:
                        finish(j - 1)
                if last:
                    finish(TB - 1)

            def finish(j):
                s0 = ss[:, j:j + 1]
                if j == 0:
                    dve.wait_ge(gains, 16)
                dve.wait_ge(ysq, j + 1)
                dve.tensor_scalar(s0, s0, 1.0 / D, EPS, ALU.mult, ALU.add).then_inc(mean, 1)
                dve.wait_ge(root, j + 1)
                dve.reciprocal(s0, s0).then_inc(inv, 1)
                dve.wait_ge(inv, 2 * j + 1)
                dve.scalar_tensor_tensor(acc[:, j, :], acc[:, j, :], s0, postB[:], ALU.mult, ALU.mult).then_inc(inv, 1)
                dve.wait_ge(inv, 2 * j + 2)
                dve.wait_ge(x_in[j % 2], 16 * (j // 2 + 1))
                dve.tensor_tensor(acc[:, j, :], acc[:, j, :], xt[j % 2], ALU.add).then_inc(final, 1)

            with dve.Fori(0, NE - 1) as e:
                slice_work(e, False)
            slice_work(NE - 1, True)

        @block.tensor
        def _(pe):
            for s in range(2):
                pe.sem_inc(hidden[s], 1)
            pe.sem_inc(used, 1)

            def hidden_block(e, i, first=False):
                s = i % 2
                pe.wait_ge(w1_low[s], e * 2 + i // 2 + 2)
                if not first:
                    pe.wait_ge(rectified, e * (2 * FB) + 2 * (i - 1))
                for h in range(NH):
                    hs = slice(h * HALF, (h + 1) * HALF)
                    for k in range(KB):
                        for q, (w, a) in enumerate(((w1L, hH), (w1H, hL), (w1H, hH))):
                            m = pe.matmul(bank[s][h][:], w[s][:, k, :], a[:, k, hs],
                                          start=(k == 0 and q == 0), stop=(k == KB - 1 and q == 2))
                m.then_inc(hidden[s], 1)

            def second_product(e):
                for g in range(G):
                    j, dh = g // 2, g % 2
                    ts, ds = slice(j * P, (j + 1) * P), slice(dh * HALF, (dh + 1) * HALF)
                    pe.wait_ge(added, e * G + g - 2 if g >= 4 else e * G + 1)
                    for i in range(FB):
                        if g < 2:
                            pe.wait_ge(g_low, e * (2 * FB) + 2 * i + 3)
                            pe.wait_ge(w2_low, e * FB + i + 3)
                        for q, (a, w) in enumerate(((gL, w2H), (gH, w2L), (gH, w2H))):
                            m = pe.matmul(ybank[g % 4][:], a[:, i, ts], w[:, i, ds],
                                          start=(i == 0 and q == 0), stop=(i == FB - 1 and q == 2))
                    m.then_inc(summed, 1)
                pe.wait_ge(summed, e * G + G)
                pe.sem_inc(used, 1)

            hidden_block(0, 0, first=True)
            hidden_block(0, 1, first=True)
            hidden_block(0, 2)
            hidden_block(0, 3)
            with pe.Fori(0, NE - 1) as e:
                hidden_block(e + 1, 0)
                second_product(e)
                for i in range(1, FB):
                    hidden_block(e + 1, i)
            second_product(NE - 1)


def rwkv(nc, con, args, proj, mixed):
    ident, col = con["ident"], con["col"]
    mask = {name: con["masks"][:, n, :] for n, name in enumerate(MASKS)}
    NG = 4
    NC = T // C
    NT = TB // 2
    DECAY = 0.6065306597126334
    NPC = len(RW_COLS)
    B16 = 16
    with ExitStack() as st:
        r = Region(nc, st, "rw")
        raw = {n: r.sb(f"raw_{n}", [P, T + 1]) for n in "rkv"}
        low_raw, low = r.sb("low_raw", [P, T + 1]), r.sb("low", [P, T])
        up, start = r.sb("up", [P, P]), r.sb("start", [P, T])
        pc, rest = r.sb("pc", [P, NPC]), r.sb("rest", [P, 4])
        b = [r.sb(f"b{n}", [P, T]) for n in range(11)]
        bonus, gate_up = r.sb("bonus", [P, T]), r.sb("gate_up", [P, P])
        at_head, rt_head = r.sb("at_head", [P, 2, T]), r.sb("rt_head", [P, 2, T])
        wc, gn = r.sb("wc", [P, NC]), r.sb("gn", [P, 2])
        nat = {n: r.sb(f"nat_{n}", [P, TB, P]) for n in "bkv"}
        aw = r.sb("aw", [P, TB, 2, 2, C])
        state = r.sb("state", [P, NC + 1, C])
        small = r.sb("small", [P, 4, 2 * TB])
        slots = {n: r.sb(n, [P, NG, NT, P]) for n in
                 ("s0", "s3", "lo32", "lo64", "ak", "rb", "rk", "R", "gu")}
        NB = NG * NT
        diag, back16 = r.sb("diag", [P, NB, B16]), r.sb("back16", [P, NB, B16])
        mine, inverse = r.sb("mine", [P, B16, B16]), r.sb("inverse", [P, B16, B16])
        unit16 = r.sb("unit16", [P, B16, B16])
        work16 = slots["s0"][:, 0, 0:2].rearrange("p j c -> p (j c)").rearrange("p (s t) -> p s t", t=B16)
        diag_d = nc.dram_tensor("rw_diagonal_blocks", [P, NB, B16], F32, kind="Internal").ap()
        back_d = nc.dram_tensor("rw_inverted_blocks", [P, NB, B16], F32, kind="Internal").ap()
        sets = [{n: slots[n][:, g] for n in slots} for g in range(NG)]
        banks = [r.bank(f"b{n}") for n in range(8)]
        rs_, ks_, vs_ = b[0], b[1], b[2]

        def part(slot, n):
            return slots[slot][:, 2 * n:2 * n + 2].rearrange("p a j c -> p (a j c)")

        QT = part("lo32", 0).rearrange("p (j t) -> p j t", t=P)
        MT = part("lo32", 1).rearrange("p (c k) -> p c k", k=C)
        KW = part("lo64", 0).rearrange("p (c v) -> p c v", v=C)
        y_flat, out, y_sq = part("lo64", 1), part("ak", 0), part("ak", 1)
        Y = y_flat.rearrange("p (j f) -> p j f", f=P)
        sems = {}

        def s(name):
            if name not in sems:
                sems[name] = r.sem(name)
            return sems[name]

        low_in, low_cut = s("low_in"), s("low_cut")
        pc_at = {n: k for k, n in enumerate(RW_COLS)}

        def param(name):
            return pc[:, pc_at[name]:pc_at[name] + 1]

        def halves(ap):
            return [ap[:, h * HALF:(h + 1) * HALF] for h in range(NH)]

        ORDER = ("xd", "ak", "rb", "rk", "ld", "wv", "z32", "rt16", "r32", "rt32", "z64", "r64", "gu", "qt")

        def bank_of(name, g):
            return banks[2 * g + (ORDER.index(name) % 2 if name != "y" else 0)]

        def of_head(h):
            return mask["same64"][:, C * h:C * h + 1]

        def every_second(ap, g, c):
            h, th = g // 2, g % 2
            return ap.rearrange("p (j two) k -> p j two k", two=2)[C * h:C * h + C, NT * th:NT * (th + 1), c, :]

        block = st.enter_context(nc.Block())
        LAST = PAIRS - 1

        SCAN, SIDE, TURN = banks[1:4:2], banks[5:8:2], {"a": (1, 3), "b": (0, 2), "k": (1, 3), "v": (0, 2)}
        GATE = (banks[4], banks[6])

        @block.sync
        def _(sp):
            sp.sem_inc(s("stored"), 16)
            sp.dma_start(low_raw[:, 1:T + 1], proj[RW_LOW:RW_LOW + P, :]).then_inc(low_in, 16)

            def load(k, reused):
                if reused:
                    sp.wait_ge(s("pre_w"), k)
                    sp.wait_ge(s("pre_a"), k)
                for part_, p0, p1 in (("rw_w_up", 0, 32), ("rw_a_up", 32, 64)):
                    sp.dma_start(up[p0:p1, :], args[part_].rearrange("l p n -> (l p) n")[:, bass.ds(k * P, P)]
                                 ).then_inc(s("in_up"), 16)
                for n, at in (("k", RW_K), ("r", RW_R), ("v", RW_V)):
                    if reused:
                        sp.wait_ge(s("shift_" + n), k)
                    sp.dma_start(raw[n][:, 1:T + 1], proj[bass.ds(k * P + at, P), :]).then_inc(s("in_" + n), 16)

            def finish(i):
                sp.wait_ge(s("mixed"), i + 1)
                sp.sem_inc(s("sp_passed"), 1)
                sp.dma_start(mixed[bass.ds(i * P + SBW, P), :], out).then_inc(s("stored"), 16)

            def load_gate(i):
                sp.dma_start(gate_up[64:128, :], args["rw_g_up"].rearrange("l p n -> (l p) n")[:, bass.ds(i * P, P)]
                             ).then_inc(s("in_gate"), 16)

            def blocks(i):
                sp.wait_ge(s("diag"), i * NG + NG)
                sp.sem_inc(s("sp_passed"), 1)
                sp.dma_start(diag_d, diag[:]).then_inc(s("diag_out"), 16)
                sp.wait_ge(s("diag_out"), i * 16 + 16)
                for n in range(P // B16):
                    rows = slice(n * B16, n * B16 + B16)
                    sp.dma_start(mine[rows], diag_d[rows].rearrange("s n t -> n s t")).then_inc(s("diag_in"), 16)
                sp.wait_ge(s("inverse"), i + 1)
                sp.sem_inc(s("sp_passed"), 1)
                for n in range(P // B16):
                    rows = slice(n * B16, n * B16 + B16)
                    sp.dma_start(back_d[rows].rearrange("s n t -> n s t"), inverse[rows]).then_inc(s("back_out"), 16)
                sp.wait_ge(s("back_out"), i * (16 * P // B16) + 16 * P // B16)
                sp.dma_start(back16[:], back_d).then_inc(s("back_in"), 16)

            load(0, False)
            load_gate(0)
            with sp.Fori(0, LAST) as i:
                load(i + 1, True)
                blocks(i)
                finish(i)
                sp.wait_ge(s("gate_mm"), i + 1)
                load_gate(i + 1)
            blocks(LAST)
            finish(LAST)
            sp.wait_ge(s("stored"), 16 * PAIRS + 16)

        @block.gpsimd
        def _(pool):
            for n in "rkv":
                pool.memset(raw[n][:, 0:1], 0.0)
            pool.memset(low_raw[:, 0:1], 0.0)
            pool.memset(state[:, 0, :], 0.0)
            pool.memset(unit16[:], 0.0)
            pool.memset(start[:], 1.0).then_inc(s("cleared"), 1)
            pool.wait_ge(s("cleared"), 1)
            pool.memset(start[:].rearrange("p (c t) -> p c t", t=C)[:, :, 0:1], 0.0).then_inc(s("cleared"), 1)
            pool.memset(unit16[:].rearrange("p s t -> p (s t)")[:, 0::B16 + 1], 1.0).then_inc(s("cleared"), 1)

            def prepare(k):
                for n, dst in (("r", rs_), ("v", vs_)):
                    pool.wait_ge(s("in_" + n), k * 16 + 16)
                    pool.tensor_tensor(dst[:], raw[n][:, 0:T], raw[n][:, 1:T + 1], ALU.subtract
                                       ).then_inc(s("part_" + n), 1)
                pool.wait_ge(s("rt"), k + 1)
                for h in range(2):
                    pool.tensor_tensor(rt_head[:, h, :], b[7][:], of_head(h).to_broadcast([P, T]), ALU.mult
                                       ).then_inc(s("rt_head"), 1)

            prepare(0)

            def core(i):
                pool.wait_ge(s("bonus_made"), i + 1)
                pool.wait_ge(s("biased"), i + 1)
                pool.sem_inc(s("pool_passed"), 1)
                pool.tensor_copy(bonus[:], b[4][:]).then_inc(s("bonus"), 1)

            with pool.Fori(0, LAST) as i:
                core(i)
                pool.wait_ge(s("m_ld"), i * NG + NG)
                prepare(i + 1)
            core(LAST)

        @block.scalar
        def _(act):
            act.wait_ge(low_in, 16)
            act.wait_ge(low_cut, 1)
            act.activation(low[:], low_raw[:, 1:T + 1], ACT.Copy, scale=rest[:, 3:4]).then_inc(s("low_part"), 1)
            act.wait_ge(low_cut, 2)
            act.activation(low[0:32, :], low[0:32, :], ACT.Tanh)
            act.activation(low[64:128, :], low[64:128, :], ACT.Sigmoid).then_inc(s("low_done"), 1)

            def scan_step(i, c):
                act.wait_ge(s("step_mm"), i * NC + c + 1)
                if c == 0:
                    act.wait_ge(s("wc"), i + 1)
                act.activation(state[:, c + 1, :], SCAN[c % 2][:, 0:C], ACT.Copy, scale=wc[:, c:c + 1]
                               ).then_inc(s("step"), 1)

            def own_share(k):
                act.wait_ge(s("cols"), k + 1)
                act.wait_ge(s("in_k"), k * 16 + 16)
                act.activation(ks_[:], raw["k"][:, 1:T + 1], ACT.Copy, scale=rest[:, 1:2]).then_inc(s("part_k"), 1)

            def early(k):
                for n, dst, bias in (("w", b[3], "w0"), ("a", b[4], "a0")):
                    act.wait_ge(s("pre_" + n), k + 1)
                    if n == "a" and not isinstance(k, int):
                        act.wait_ge(s("bonus"), k)
                    for h in range(2):
                        act.activation(halves(dst)[h], SIDE[h][:], ACT.Sigmoid, bias=param(bias)
                                       ).then_inc(s("sig_" + n), 1)
                act.preload_act_table_set(EXP_LN)
                act.wait_ge(s("shift_k"), k + 1)
                act.activation(b[6][:], ks_[:], ACT.Square, scale=param("k_k")).then_inc(s("ksq"), 1)

            def late(k, scan):
                def step(c):
                    if scan is not None:
                        scan_step(scan, c)

                step(0)
                act.wait_ge(s("norm_kept"), k + 1)
                act.activation(b[6][:], b[6][:], ACT.Ln).then_inc(s("ln"), 1)
                act.wait_ge(s("ln"), k + 1)
                step(1)
                act.activation(b[6][:], b[6][:], ACT.Exp, scale=-0.5).then_inc(s("rn"), 1)
                step(2)
                step(3)
                act.wait_ge(s("cumx"), k + 1)
                act.activation(b[8][:], b[8][:], ACT.Exp, scale=-DECAY).then_inc(s("ex"), 1)
                step(4)
                act.activation(b[10][:], b[7][:], ACT.Exp, scale=DECAY).then_inc(s("en"), 1)
                step(5)
                if scan is not None:
                    act.wait_ge(s("wc"), k)
                act.activation(b[9][:], b[7][:], ACT.Exp, scale=-DECAY).then_inc(s("ep"), 1)
                for c in range(6, NC):
                    step(c)

            def take_turned(n, k):
                for h in range(2):
                    act.wait_ge(s("nat_mm_" + n), k * 2 + h + 1)
                    tiles = slice(4 * h, 4 * h + 4)
                    if n == "a":
                        dst, src = aw[:, tiles, :, 0, :], banks[TURN[n][h]][:].rearrange("p (j h f) -> p j h f", h=2, f=C)
                    else:
                        dst, src = nat[n][:, tiles, :], banks[TURN[n][h]][:].rearrange("p (j f) -> p j f", f=P)
                    act.copy(dst, src).then_inc(s("nat_" + n), 1)

            def apart(k):
                act.wait_ge(s("at"), k + 1)
                for h in range(2):
                    act.activation(at_head[:, h, :], b[8][:], ACT.Copy, scale=of_head(h)).then_inc(s("at_head"), 1)

            def core(i, more):
                def take(name, slot):
                    for g in range(NG):
                        act.wait_ge(s("m_" + name), i * NG + g + 1)
                        act.copy(sets[g][slot], bank_of(name, g)[:].rearrange("p (j c) -> p j c", c=P)
                                 ).then_inc(s("t_" + name), 1)

                if more:
                    own_share(i + 1)
                for g in range(NG):
                    act.wait_ge(s("m_wv"), i * NG + g + 1)
                    act.copy(aw[:, NT * (g % 2):NT * (g % 2) + NT, g // 2, 1, :],
                             bank_of("wv", g)[:, 0:NT * C].rearrange("p (j v) -> p j v", v=C)).then_inc(s("t_wv"), 1)
                if more:
                    early(i + 1)
                take("z32", "s0")
                take("rt16", "s3")
                take("rt32", "s3")
                take("z64", "s0")
                take("gu", "gu")
                for g in range(NG):
                    h, th = g // 2, g % 2
                    hs = slice(C * h, C * h + C)
                    act.wait_ge(s("t_mt"), i * NG + g + 1)
                    for c in range(2):
                        m = act.copy(every_second(KW, g, c),
                                     banks[2 * g + c][hs, :].rearrange("p (j f) -> p j f", f=P)[:, :, C:P])
                    m.then_inc(s("t_kw"), 1)

            def norm(i, last):
                for th in range(2):
                    act.wait_ge(s(f"m_y{th}"), i + 1)
                    for h in range(2):
                        act.copy(Y[:, 4 * th:4 * th + 4, C * h:C * h + C],
                                 bank_of("y", 2 * h + th)[:, 0:NT * C].rearrange("p (j v) -> p j v", v=C)
                                 ).then_inc(s("y"), 1)
                if not last:
                    take_turned("a", i + 1)
                    take_turned("b", i + 1)
                act.wait_ge(s("centred"), i + 1)
                act.activation(y_sq, y_flat, ACT.Square).then_inc(s("ysq"), 1)
                if not last:
                    apart(i + 1)
                    take_turned("k", i + 1)
                act.wait_ge(s("var"), i + 1)
                act.activation(small[:, 1, :], small[:, 1, :], ACT.Ln).then_inc(s("root"), 1)
                act.wait_ge(s("root"), i * 2 + 1)
                act.activation(small[:, 2, :], small[:, 1, :], ACT.Exp, scale=-0.5).then_inc(s("root"), 1)
                act.wait_ge(s("gn"), i + 1)
                for h in range(2):
                    act.wait_ge(s("back"), i * 2 + h + 1)
                    act.activation(halves(out)[h], SIDE[h][:], ACT.Identity, scale=gn[:, 0:1],
                                   bias=gn[:, 1:2]).then_inc(s("affine"), 1)
                if not last:
                    take_turned("v", i + 1)

            own_share(0)
            early(0)
            late(0, None)
            apart(0)
            for n in "abkv":
                take_turned(n, 0)
            with act.Fori(0, LAST) as i:
                core(i, True)
                late(i + 1, i)
                norm(i, False)
            core(LAST, False)
            for c in range(NC):
                scan_step(LAST, c)
            norm(LAST, True)

        @block.vector
        def _(dve):
            mu_low = col[:, COL["rw_mu"] + 9:COL["rw_mu"] + 10]
            dve.sem_inc(s("biased"), 1)
            dve.tensor_scalar(rest[:, 3:4], mu_low, -1.0, 1.0, ALU.mult, ALU.add).then_inc(low_cut, 1)
            dve.wait_ge(s("low_part"), 1)
            dve.wait_ge(s("cleared"), 3)
            dve.scalar_tensor_tensor(low[:], low_raw[:, 0:T], mu_low, low[:], ALU.mult, ALU.add).then_inc(low_cut, 1)
            all_columns = col[:, COL["rw_w0"]:COL["rw_w0"] + 3 * NPC].rearrange("p (n q) -> p n q", q=3)

            def columns(k):
                dve.tensor_copy(pc[:].rearrange("p (n o) -> p n o", o=1), all_columns[:, :, bass.ds(k, 1)]
                                ).then_inc(s("cols_raw"), 1)
                dve.wait_ge(s("cols_raw"), k + 1)
                dve.tensor_scalar(rest[:, 0:3], pc[:, 7:10], -1.0, 1.0, ALU.mult, ALU.add).then_inc(s("cols"), 1)

            def early(k):
                dve.wait_ge(s("part_k"), k + 1)
                dve.scalar_tensor_tensor(ks_[:], raw["k"][:, 0:T], param("mu_k"), ks_[:],
                                         ALU.mult, ALU.add).then_inc(s("shift_k"), 1)
                dve.wait_ge(s("shift_k"), k + 1)
                dve.tensor_scalar(b[5][:], ks_[:], param("k_k"), None, ALU.mult).then_inc(s("kx"), 1)

            def keep_norms(k):
                dve.wait_ge(s("norm_mm"), k + 1)
                for h in range(2):
                    m = dve.tensor_scalar(halves(b[6])[h], SIDE[h][:], 1e-12, None, ALU.max)
                m.then_inc(s("norm_kept"), 1)

            def late(k):
                def one(name):
                    dve.wait_ge(s(name), k + 1)

                def shift(n, dst):
                    one("part_" + n)
                    dve.scalar_tensor_tensor(dst[:], dst[:], param("mu_" + n), raw[n][:, 1:T + 1],
                                             ALU.mult, ALU.add).then_inc(s("shift_" + n), 1)

                dve.wait_ge(s("sig_w"), k * 2 + 2)
                dve.tensor_tensor_scan(b[7][:], start[:], b[3][:], 0.0, ALU.mult, ALU.add).then_inc(s("cum"), 1)
                one("cum")
                dve.tensor_tensor(b[8][:], b[7][:], b[3][:], ALU.subtract).then_inc(s("cumx"), 1)
                one("rn")
                one("kx")
                dve.tensor_tensor(b[5][:], b[5][:], b[6][:], ALU.mult).then_inc(s("kk"), 1)
                one("kk")
                dve.wait_ge(s("sig_a"), k * 2 + 2)
                dve.tensor_tensor(b[6][:], b[5][:], b[4][:], ALU.mult).then_inc(s("bvec"), 1)
                one("cumx")
                dve.tensor_scalar(b[3][:], b[4][:], -1.0, param("k_a"), ALU.add, ALU.mult).then_inc(s("am"), 1)
                one("ex")
                dve.scalar_tensor_tensor(b[8][:], b[5][:], -1.0, b[8][:], ALU.mult, ALU.mult).then_inc(s("at"), 1)
                one("am")
                dve.scalar_tensor_tensor(b[3][:], b[3][:], 1.0, ks_[:], ALU.add, ALU.mult).then_inc(s("km"), 1)
                one("bvec")
                one("en")
                dve.tensor_tensor(b[6][:], b[6][:], b[10][:], ALU.mult).then_inc(s("bt"), 1)
                shift("r", rs_)
                one("km")
                one("bt")
                dve.tensor_tensor(b[10][:], b[10][:], b[3][:], ALU.mult).then_inc(s("kt"), 1)
                one("shift_r")
                dve.scalar_tensor_tensor(b[4][:], rs_[:], param("r_k"), b[3][:], ALU.mult, ALU.mult
                                         ).then_inc(s("rkk"), 1)
                one("ep")
                dve.tensor_tensor(b[7][:], rs_[:], b[9][:], ALU.mult).then_inc(s("rt"), 1)
                shift("v", vs_)
                one("bonus_mm")
                one("shift_v")
                for h in range(2):
                    m = dve.tensor_tensor(halves(b[4])[h], halves(vs_)[h], SIDE[h][:], ALU.mult)
                m.then_inc(s("bonus_made"), 1)

            def invert(i):
                dve.wait_ge(s("diag_in"), i * (16 * P // B16) + 16 * P // B16)
                R = inverse[:]
                dve.tensor_copy(R, unit16[:]).then_inc(s("column"), 1)
                for t in range(1, B16):
                    dve.wait_ge(s("column"), i * (2 * B16 - 2) + 2 * t - 1)
                    dve.tensor_tensor(work16[:, 0:t, 0:t], R[:, 0:t, 0:t],
                                      mine[:, 0:t, t].unsqueeze(1).to_broadcast([P, t, t]), ALU.mult
                                      ).then_inc(s("column"), 1)
                    dve.wait_ge(s("column"), i * (2 * B16 - 2) + 2 * t)
                    dve.tensor_reduce(R[:, 0:t, t], work16[:, 0:t, 0:t], AX.X, ALU.add
                                      ).then_inc(s("column" if t < B16 - 1 else "inverse"), 1)

            def core(i, more):
                dve.tensor_copy(wc[:], b[9][:].rearrange("p (c t) -> p c t", t=C)[:, :, C - 1]
                                ).then_inc(s("wc"), 1)
                dve.tensor_copy(gn[:].rearrange("p (n o) -> p n o", o=1),
                                all_columns[:, pc_at["gn_g"]:pc_at["gn_g"] + 2, bass.ds(i, 1)]).then_inc(s("gn"), 1)
                if more:
                    columns(i + 1)

                def grp(name, g):
                    dve.wait_ge(s(name), i * NG + g + 1)

                def masked(name, outs):
                    for g in range(NG):
                        grp("m_" + name, g)
                        for slot, m in outs:
                            k = dve.tensor_tensor(sets[g][slot], bank_of(name, g)[:].rearrange("p (j c) -> p j c", c=P),
                                                  mask[m].unsqueeze(1).to_broadcast([P, NT, P]), ALU.mult)
                        k.then_inc(s("t_" + name), 1)

                def add_to_r(name, before):
                    for g in range(NG):
                        grp("m_" + name, g)
                        grp("t_" + before, g)
                        R = sets[g]["R"]
                        dve.tensor_tensor(R, R, bank_of(name, g)[:].rearrange("p (j c) -> p j c", c=P), ALU.add
                                          ).then_inc(s("t_" + name), 1)

                for g in range(NG):
                    grp("m_xd", g)
                    dve.tensor_tensor(sets[g]["s0"], bank_of("xd", g)[:].rearrange("p (j c) -> p j c", c=P),
                                      mask["up16"].unsqueeze(1).to_broadcast([P, NT, P]), ALU.mult
                                      ).then_inc(s("t_xd"), 1)
                    grp("t_xd", g)
                    dve.tensor_reduce(diag[:, NT * g:NT * g + NT, :],
                                      sets[g]["s0"].rearrange("p j (n c) -> p j c n", c=B16), AX.X, ALU.add
                                      ).then_inc(s("diag"), 1)
                dve.wait_ge(s("stored"), i * 16 + 16)
                masked("ak", (("ak", "up64"),))
                masked("rb", (("rb", "upd64"),))
                masked("rk", (("rk", "upd64"),))
                if more:
                    early(i + 1)
                invert(i)
                masked("ld", (("lo32", "low32"), ("lo64", "low64")))
                dve.wait_ge(s("back_in"), i * 16 + 16)
                for g in range(NG):
                    in_blocks = lambda ap: ap.rearrange("p (n c) -> p n c", c=B16)
                    dve.tensor_tensor(sets[g]["R"].rearrange("p j (n c) -> p j n c", c=B16),
                                      back16[:, NT * g:NT * g + NT, :].unsqueeze(2)
                                      .to_broadcast([P, NT, P // B16, B16]),
                                      in_blocks(mask["same16"]).unsqueeze(1).to_broadcast([P, NT, P // B16, B16]),
                                      ALU.mult).then_inc(s("t_r16"), 1)
                if more:
                    keep_norms(i + 1)
                add_to_r("r32", "r16")
                add_to_r("r64", "r32")
                for g in range(NG):
                    h, th = g // 2, g % 2
                    hs, js = slice(C * h, C * h + C), slice(NT * th, NT * th + NT)
                    grp("m_qt", g)
                    dve.tensor_tensor(QT[hs, js, :], bank_of("qt", g)[hs, :].rearrange("p (j t) -> p j t", t=P),
                                      b[7][hs, th * HALF:(th + 1) * HALF].rearrange("p (j t) -> p j t", t=P),
                                      ALU.add).then_inc(s("t_qt"), 1)
                for g in range(NG):
                    h, th = g // 2, g % 2
                    hs = slice(C * h, C * h + C)
                    grp("m_mk", g)
                    for c in range(2):
                        m = dve.tensor_tensor(every_second(MT, g, c),
                                              banks[2 * g + c][hs, :].rearrange("p (j f) -> p j f", f=P)[:, :, 0:C],
                                              ident[hs, hs].unsqueeze(1).to_broadcast([C, NT, C]), ALU.add)
                    m.then_inc(s("t_mt"), 1)

            def norm(i):
                def one(name):
                    dve.wait_ge(s(name), i + 1)

                dve.wait_ge(s("y"), i * NG + NG)
                y3 = y_flat.rearrange("p (n v) -> p n v", v=C)
                bc = lambda q: small[:, q, :].unsqueeze(2).to_broadcast([P, 2 * TB, C])
                dve.tensor_reduce(small[:, 0, :], y3, AX.X, ALU.add).then_inc(s("ysum"), 1)
                one("ysum")
                dve.tensor_scalar(small[:, 0, :], small[:, 0, :], 1.0 / C, None, ALU.mult).then_inc(s("mean"), 1)
                one("mean")
                dve.tensor_tensor(y3, y3, bc(0), ALU.subtract).then_inc(s("centred"), 1)
                one("ysq")
                dve.tensor_reduce(small[:, 1, :], y_sq.rearrange("p (n v) -> p n v", v=C), AX.X, ALU.add
                                  ).then_inc(s("vsum"), 1)
                one("vsum")
                dve.tensor_scalar(small[:, 1, :], small[:, 1, :], 1.0 / C, GN_EPS, ALU.mult, ALU.add
                                  ).then_inc(s("var"), 1)
                dve.wait_ge(s("root"), i * 2 + 2)
                dve.tensor_tensor(y3, y3, bc(2), ALU.mult).then_inc(s("normed"), 1)
                dve.wait_ge(s("affine"), i * 2 + 2)
                one("bonus")
                dve.tensor_tensor(out, out, bonus[:], ALU.add).then_inc(s("biased"), 1)
                dve.wait_ge(s("biased"), i + 2)
                one("gate_mm")
                for h in range(2):
                    m = dve.tensor_tensor(halves(out)[h], halves(out)[h], GATE[h][:], ALU.mult)
                m.then_inc(s("mixed"), 1)

            columns(0)
            early(0)
            keep_norms(0)
            late(0)
            with dve.Fori(0, LAST) as i:
                core(i, True)
                late(i + 1)
                norm(i)
            core(LAST, False)
            norm(LAST)

        @block.tensor
        def _(pe):
            pe.wait_ge(s("low_done"), 1)
            pe.wait_ge(low_cut, 2)

            def low_rank(k, n):
                if n == "w":
                    pe.wait_ge(s("in_up"), k * 32 + 32)
                else:
                    pe.wait_ge(s("sig_w"), k * 2 + 2)
                p0, p1 = (0, 32) if n == "w" else (32, 64)
                for h in range(NH):
                    m = pe.matmul(SIDE[h][:], up[p0:p1, :], halves(low)[h][p0:p1, :], start=True, stop=True)
                m.then_inc(s("pre_" + n), 1)

            def norms(k):
                pe.wait_ge(s("ksq"), k + 1)
                pe.wait_ge(s("sig_a"), k * 2 + 2)
                for h in range(NH):
                    m = pe.matmul(SIDE[h][:], mask["same64"], halves(b[6])[h], start=True, stop=True)
                m.then_inc(s("norm_mm"), 1)

            def bonuses(k):
                pe.wait_ge(s("rkk"), k + 1)
                pe.wait_ge(s("norm_kept"), k + 1)
                for h in range(NH):
                    m = pe.matmul(SIDE[h][:], mask["same64"], halves(b[4])[h], start=True, stop=True)
                m.then_inc(s("bonus_mm"), 1)

            def turn(n, k):
                src, made = {"a": (b[8], "at"), "b": (b[6], "bt"), "k": (b[10], "kt"), "v": (vs_, "shift_v")}[n]
                pe.wait_ge(s(made), k + 1)
                if n in "kv":
                    pe.wait_ge(s("nat_a" if n == "k" else "nat_b"), k * 2 + 2)
                for h in range(2):
                    for q in range(4):
                        j = 4 * h + q
                        m = pe.transpose(banks[TURN[n][h]][:, q * P:(q + 1) * P], src[:, j * P:(j + 1) * P], ident[:])
                    m.then_inc(s("nat_mm_" + n), 1)

            def core(i, after, more):
                def one(name):
                    pe.wait_ge(s(name), i + 1)

                for n in "abkv":
                    pe.wait_ge(s("nat_" + n), i * 2 + 2)
                one("bonus_made")
                if after:
                    pe.wait_ge(s("affine"), i * 2)
                    pe.wait_ge(s("mixed"), i)
                one("rt")

                def grp(name, g):
                    pe.wait_ge(s(name), i * NG + g + 1)

                def step(name, needs, product):
                    n = ORDER.index(name)
                    for g in range(NG):
                        if n >= 2:
                            grp("t_" + ORDER[n - 2], g)
                        for need in needs:
                            grp("t_" + need, g)
                        bk = bank_of(name, g)
                        for j in range(NT):
                            m = product(g, sets[g], j, bk)
                        m.then_inc(s("m_" + name), 1)

                def scores(left, right):
                    def product(g, q, j, bk):
                        h, th = g // 2, g % 2
                        ts = slice((NT * th + j) * P, (NT * th + j + 1) * P)
                        l, r_ = [x[:, h, ts] if x in (at_head, rt_head) else x[:, ts] for x in (left, right)]
                        return pe.matmul(bk[:, j * P:(j + 1) * P], l, r_, start=True, stop=True)
                    return product

                def square(left, right):
                    def product(g, q, j, bk):
                        return pe.matmul(bk[:, j * P:(j + 1) * P], q[left][:, j, :], q[right][:, j, :],
                                         start=True, stop=True)
                    return product

                def turned(src):
                    def product(g, q, j, bk):
                        return pe.transpose(bk[:, j * P:(j + 1) * P], q[src][:, j, :], ident[:])
                    return product

                def tile_of(g, j):
                    return NT * (g % 2) + j, slice(C * (g // 2), C * (g // 2) + C)

                pe.wait_ge(s("at_head"), i * 2 + 2)
                step("xd", (), scores(b[6], at_head))
                step("ak", (), scores(b[10], at_head))
                pe.wait_ge(s("rt_head"), i * 2 + 2)
                step("rb", (), scores(b[6], rt_head))
                step("rk", (), scores(b[10], rt_head))
                step("ld", (), scores(at_head, b[6]))

                def keys_values(g, q, j, bk):
                    t, hs = tile_of(g, j)
                    return pe.matmul(bk[:, j * C:(j + 1) * C], q["ak"][:, j, :], nat["v"][:, t, hs], start=True, stop=True)

                step("wv", ("ak",), keys_values)
                if more:
                    pe.wait_ge(s("t_wv"), i * NG + NG)
                    low_rank(i + 1, "w")
                    low_rank(i + 1, "a")
                    norms(i + 1)
                step("z32", ("ld", "r16"), square("lo32", "R"))
                if more:
                    pe.wait_ge(s("norm_kept"), i + 2)
                step("rt16", ("r16",), turned("R"))
                step("r32", ("z32", "rt16"), square("s3", "s0"))
                step("rt32", ("r32",), turned("R"))
                step("z64", (), square("lo64", "R"))
                step("r64", ("z64", "rt32"), square("s3", "s0"))

                def updates(g, q, j, bk):
                    t, hs = tile_of(g, j)
                    return pe.matmul(bk[:, j * P:(j + 1) * P], q["R"][:, j, :],
                                     aw[:, t, g // 2].rearrange("p q f -> p (q f)"), start=True, stop=True)

                step("gu", ("wv", "r64"), updates)

                def readers(g, q, j, bk):
                    t, hs = tile_of(g, j)
                    return pe.matmul(bk[hs, j * P:(j + 1) * P], q["gu"][:, j, 0:C], q["rb"][:, j, :], start=True, stop=True)

                step("qt", ("gu", "rb"), readers)

                for g in range(NG):
                    q = sets[g]
                    grp("t_gu", g)
                    grp("t_qt", g)
                    pe.sem_inc(s("pe_passed"), 1)
                    for c in range(2):
                        cs = slice(C * c, C * c + C)
                        for j in range(NT):
                            t, hs = tile_of(g, j)
                            m = pe.matmul(banks[2 * g + c][hs, j * P:j * P + C], q["gu"][cs, j, 0:C],
                                          nat["b"][cs, t, hs], start=True, stop=True)
                            o = banks[2 * g + c][hs, j * P + C:(j + 1) * P]
                            pe.matmul(o, nat["b"][cs, t, hs], q["gu"][cs, j, C:P], start=True, stop=False)
                            m = pe.matmul(o, nat["k"][cs, t, hs], nat["v"][cs, t, hs], start=False, stop=True)
                    m.then_inc(s("m_mk"), 1)
            def scan_step(i, c):
                if c == 0:
                    pe.wait_ge(s("t_mt"), i * NG + NG)
                    pe.wait_ge(s("t_kw"), i * NG + NG)
                    pe.sem_inc(s("pe_passed"), 1)
                for h in range(2):
                    hs = slice(C * h, C * h + C)
                    pe.matmul(SCAN[c % 2][hs, 0:C], ident[hs, hs], KW[hs, c, :], start=True, stop=False)
                if c:
                    pe.wait_ge(s("step"), i * NC + c)
                    pe.sem_inc(s("pe_passed"), 1)
                for h in range(2):
                    hs = slice(C * h, C * h + C)
                    m = pe.matmul(SCAN[c % 2][hs, 0:C], MT[hs, c, :], state[hs, c, :], start=False, stop=True)
                m.then_inc(s("step_mm"), 1)

            def outputs(i, n):
                t, h = n // 2, n % 2
                if n == 0:
                    pe.wait_ge(s("t_rk"), i * NG + NG)
                    pe.sem_inc(s("pe_passed"), 1)
                th, j = t // NT, t % NT
                o = slice(j * C, (j + 1) * C)
                q, bk, hs = sets[2 * h + th], bank_of("y", 2 * h + th), slice(C * h, C * h + C)
                pe.matmul(bk[:, o], q["rb"][:, j, :], q["gu"][:, j, C:P], start=True, stop=False)
                pe.matmul(bk[:, o], q["rk"][:, j, :], nat["v"][:, t, hs], start=False, stop=True)
                for c in range(2):
                    cs = slice(C * c, C * c + C)
                    m = pe.matmul(bk[cs, o], QT[hs, t, cs], state[hs, 2 * t + c, :], start=False, stop=True,
                                  skip_group_check=True)
                if h == 1 and j == NT - 1:
                    m.then_inc(s(f"m_y{th}"), 1)

            def finish(i, last):
                if not last:
                    bonuses(i + 1)
                    pe.wait_ge(s("step"), i * NC + NC)
                    turn("a", i + 1)
                pe.wait_ge(s("y"), i * NG + NG)
                pe.wait_ge(s("in_gate"), i * 16 + 16)
                for h in range(NH):
                    m = pe.matmul(GATE[h][:], gate_up[64:128, :], halves(low)[h][64:128, :], start=True, stop=True)
                m.then_inc(s("gate_mm"), 1)
                if not last:
                    turn("b", i + 1)
                    turn("k", i + 1)
                    pe.wait_ge(s("bonus_made"), i + 2)
                pe.wait_ge(s("normed"), i + 1)
                for h in range(2):
                    for q in range(4):
                        j = 4 * h + q
                        m = pe.transpose(SIDE[h][:, q * P:(q + 1) * P], Y[:, j, :], ident[:])
                    m.then_inc(s("back"), 1)
                if not last:
                    turn("v", i + 1)

            low_rank(0, "w")
            low_rank(0, "a")
            norms(0)
            bonuses(0)
            for n in "abkv":
                turn(n, 0)
            core(0, False, True)
            def scan(i):
                for c in range(NC):
                    scan_step(i, c)
                    if c:
                        outputs(i, c - 1)
                outputs(i, NC - 1)

            with pe.Fori(0, LAST - 1) as i:
                scan(i)
                finish(i, False)
                core(i + 1, True, True)
            scan(LAST - 1)
            finish(LAST - 1, False)
            core(LAST, True, False)
            scan(LAST)
            finish(LAST, True)


def gla(nc, con, args, proj, mixed):
    ident, col, levels = con["ident"], con["col"], con["levels"]
    NL = 6
    H, DK, DV = 4, 32, 64
    NC = T // C
    WV = H * DV
    with ExitStack() as st:
        r = Region(nc, st, "gla")
        q, k = r.sb("q", [P, T]), r.sb("k", [P, T])
        vT = [r.sb(f"vT{n}", [P, T]) for n in range(2)]
        gT = [r.sb(f"gT{n}", [P, T]) for n in range(2)]
        sg = [r.sb(f"sg{n}", [P, T]) for n in range(2)]
        gd, gate_up = r.sb("gd", [16, T]), r.sb("gup", [16, P])
        x, e, cum, start = r.sb("x", [P, T]), r.sb("e", [P, T]), r.sb("cum", [P, T]), r.sb("start", [P, T])
        D_ = [r.sb(f"D{n}", [P, T]) for n in range(2)]
        qf = [r.sb(f"qf{n}", [P, T // 2]) for n in range(2)]
        result = [r.sb(f"result{n}", [P, T]) for n in range(2)]
        own = r.sb("own", [P, T // P * H])
        qb = [r.sb(f"qb{n}", [P, TB, H, C]) for n in range(2)]
        kf = [r.sb(f"kf{n}", [P, T]) for n in range(2)]
        qin, kout = r.sb("qin", [P, T]), r.sb("kout", [P, T])
        A = r.sb("A", [P, TB, H, P])
        knat, vnat = r.sb("knat", [P, TB, P]), r.sb("vnat", [P, TB, WV])
        heads = r.sb("heads", [P, WV])
        KV = r.sb("KV", [P, NC, WV])
        S = r.sb("S", [P, NC + 1, WV])
        small = r.sb("small", [P, 2, TB * H])
        O, osq = KV, S
        banks = [r.bank(f"b{n}") for n in range(8)]
        sems = {}

        def s(name):
            if name not in sems:
                sems[name] = r.sem(name)
            return sems[name]

        block = st.enter_context(nc.Block())
        LOADS = [(q, GLA_Q, P, "q"), (k, GLA_K, P, "k"), (vT[0], GLA_V, P, "v"), (vT[1], GLA_V + P, P, "v"),
                 (gT[0], GLA_G, P, "g"), (gT[1], GLA_G + P, P, "g")]

        @block.sync
        def _(sp):
            sp.dma_start(gd[:], proj[GLA_GD:GLA_GD + 16, :]).then_inc(s("in_gd"), 16)
            sp.dma_start(gate_up[:], args["gla_gate_up"].rearrange("l p n -> (l p) n")).then_inc(s("in_gd"), 16)
            for dst, at, n, name in LOADS:
                sp.dma_start(dst[:], proj[at:at + n, :]).then_inc(s("in_" + name), 16)
            for n in range(2):
                sp.wait_ge(s("mixed"), n + 1)
                sp.dma_start(mixed[SBW + RWW + n * P:SBW + RWW + (n + 1) * P, :], result[n][:]).then_inc(s("stored"), 16)
            sp.wait_ge(s("stored"), 32)

        @block.gpsimd
        def _(pool):
            pool.memset(start[:], 1.0).then_inc(s("ones"), 1)
            pool.wait_ge(s("ones"), 1)
            pool.memset(start[:].rearrange("p (c t) -> p c t", t=C)[:, :, 0:1], 0.0).then_inc(s("start"), 1)
            for n in range(2):
                pool.memset(qb[n][:].rearrange("p j h t -> p (j h t)"), 0.0)
                m = pool.memset(kf[n][:], 0.0)
            m.then_inc(s("zeroed"), 1)
            pool.memset(heads[:], 0.0).then_inc(s("heads"), 1)
            pool.wait_ge(s("heads"), 1)
            for h in range(H):
                pool.memset(heads[DK * h:DK * h + DK, DV * h:DV * h + DV], 1.0).then_inc(s("heads"), 1)
                pool.wait_ge(s("heads"), h + 2)
            pool.memset(S[:, 0, :], 0.0).then_inc(s("heads"), 1)

        @block.scalar
        def _(act):
            act.wait_ge(s("in_g"), 32)
            for n in range(2):
                act.activation(sg[n][:], gT[n][:], ACT.Sigmoid).then_inc(s("sigmoid"), 1)
            act.preload_act_table_set(EXP_LN)
            act.wait_ge(s("gate_mm"), 1)
            bias = col[:, COL["gla_gate_b"]:COL["gla_gate_b"] + 1]
            for h in range(NH):
                hs = slice(h * HALF, (h + 1) * HALF)
                act.activation(e[:, hs], banks[h][:], ACT.Abs, bias=bias)
                act.activation(x[:, hs], banks[h][:], ACT.Identity, bias=bias).then_inc(s("arg"), 1)
            act.wait_ge(s("arg"), 2)
            act.activation(e[:], e[:], ACT.Exp, scale=-1.0).then_inc(s("exp"), 1)
            act.wait_ge(s("exp"), 1)
            act.activation(e[:], e[:], ACT.Ln, bias=1.0).then_inc(s("log"), 1)
            act.wait_ge(s("in_q"), 16)
            act.activation(q[:], q[:], ACT.Copy, scale=float(DK) ** -0.5).then_inc(s("q"), 1)
            act.wait_ge(s("cum"), 1)
            act.activation(qin[:], cum[:], ACT.Exp, scale=-1.0 / 16).then_inc(s("from_start"), 1)
            act.wait_ge(s("to_last"), 1)
            act.activation(kout[:], kout[:], ACT.Exp, scale=-1.0 / 16).then_inc(s("to_end"), 1)
            act.wait_ge(s("softplus"), 1)
            act.activation(e[:, 0:NC], cum[:].rearrange("p (c t) -> p c t", t=C)[:, :, C - 1], ACT.Exp,
                           scale=-1.0 / 16).then_inc(s("decay"), 1)

            def factor(n):
                act.wait_ge(s("diff"), n + 1)
                act.activation(D_[n % 2][:], D_[n % 2][:], ACT.Exp, scale=-1.0 / 16).then_inc(s("factor"), 1)

            factor(0)
            factor(1)
            for m in range(2):
                for h in range(2):
                    act.wait_ge(s("vnat_mm"), 2 * m + h + 1)
                    act.copy(vnat[:, 4 * h:4 * h + 4, m * P:(m + 1) * P],
                             banks[2 * m + h][:].rearrange("p (j f) -> p j f", f=P)).then_inc(s("vnat"), 1)
            for h in range(2):
                act.wait_ge(s("knat_mm"), h + 1)
                act.copy(knat[:, 4 * h:4 * h + 4, :], banks[4 + h][:].rearrange("p (j f) -> p j f", f=P)
                         ).then_inc(s("knat"), 1)
            act.wait_ge(s("zeroed"), 1)
            for n in range(NL):
                act.wait_ge(s("qf"), n + 1)
                if n >= 2:
                    act.wait_ge(s("level_mm"), 4 * (n - 1))
                for h in range(H):
                    rows = slice(DK * h, DK * h + DK)
                    act.copy(qb[n % 2][rows, :, h, :], qf[n % 2][rows, :].rearrange("p (j t) -> p j t", t=C)
                             ).then_inc(s("spread"), 1)
                if n + 2 < NL:
                    factor(n + 2)
            for n in range(4):
                act.wait_ge(s("o_mm"), n + 1)
                act.copy(O[:, 2 * n:2 * n + 2, :], banks[n][:].rearrange("p (j v) -> p j v", v=WV)).then_inc(s("o"), 1)
            act.wait_ge(s("o"), 4)
            act.activation(osq[:, 0:TB, :], O[:, 0:TB, :], ACT.Square).then_inc(s("osq"), 1)
            act.wait_ge(s("mean"), 1)
            act.activation(small[:, 0, :], small[:, 0, :], ACT.Sqrt).then_inc(s("root"), 1)
            for m in range(2):
                for h in range(NH):
                    act.wait_ge(s("back"), 2 * m + h + 1)
                    act.activation(result[m][:, h * HALF:(h + 1) * HALF], banks[4 + 2 * m + h][:], ACT.Copy,
                                   scale=col[:, COL["gla_norm_g"] + m:COL["gla_norm_g"] + m + 1]).then_inc(s("gained"), 1)

        @block.vector
        def _(dve):
            w = lambda name, n=1: dve.wait_ge(s(name), n)
            w("sigmoid", 2)
            for n in range(2):
                dve.tensor_tensor(sg[n][:], sg[n][:], gT[n][:], ALU.mult).then_inc(s("silu"), 1)
            w("arg", 2)
            dve.tensor_scalar(x[:], x[:], -1.0, 0.0, ALU.mult, ALU.max).then_inc(s("rect"), 1)
            w("rect")
            w("log")
            dve.tensor_tensor(x[:], x[:], e[:], ALU.add).then_inc(s("softplus"), 1)
            w("softplus")
            w("start")
            dve.tensor_tensor_scan(cum[:], start[:], x[:], 0.0, ALU.mult, ALU.add).then_inc(s("cum"), 1)
            w("cum")
            c3 = lambda ap: ap.rearrange("p (c t) -> p c t", t=C)
            dve.tensor_tensor(c3(kout[:]), c3(cum[:])[:, :, C - 1:C].to_broadcast([P, NC, C]), c3(cum[:]),
                              ALU.subtract).then_inc(s("to_last"), 1)

            def differences(n):
                m = 1 << n
                v = lambda ap: ap.rearrange("p (b two m) -> p b two m", two=2, m=m)
                cu, d = v(cum[:]), v(D_[n % 2][:])
                nb = T // (2 * m)
                mid = cu[:, :, 0, m - 1:m].to_broadcast([P, nb, m])
                if n >= 2:
                    w("kf", n - 1)
                dve.tensor_tensor(d[:, :, 0, :], mid, cu[:, :, 0, :], ALU.subtract)
                dve.tensor_tensor(d[:, :, 1, :], cu[:, :, 1, :], mid, ALU.subtract).then_inc(s("diff"), 1)

            differences(0)
            w("q")
            w("from_start")
            dve.tensor_tensor(qin[:], qin[:], q[:], ALU.mult).then_inc(s("qin"), 1)
            w("to_end")
            w("in_k", 16)
            dve.tensor_tensor(kout[:], kout[:], k[:], ALU.mult).then_inc(s("kout"), 1)
            w("zeroed")

            def factors(n):
                m = 1 << n
                v = lambda ap, half: ap.rearrange("p (b two m) -> p b two m", two=2, m=m)[:, :, half, :]
                w("factor", n + 1)
                if n >= 2:
                    w("spread", H * (n - 1))
                    w("level_mm", 4 * (n - 1))
                dve.tensor_tensor(qf[n % 2][:].rearrange("p (b m) -> p b m", m=m), v(D_[n % 2][:], 1), v(q[:], 1), ALU.mult
                                  ).then_inc(s("qf"), 1)
                dve.tensor_tensor(v(kf[n % 2][:], 0), v(D_[n % 2][:], 0), v(k[:], 0), ALU.mult).then_inc(s("kf"), 1)

            def take(n):
                w("diagonal", H)
                m = 1 << n
                second = lambda ap: ap.rearrange("p (b two m) -> p b two m", two=2, m=m)[:, :, 1, :]
                msk = second(levels[:, n, :].bitcast(U32)).unsqueeze(1).to_broadcast([P, 2 * H, C // m, m])
                for g in range(4):
                    w("level_mm", 4 * n + g + 1)
                    if n:
                        w("taken", 4 * (n - 1) + g + 1)
                    dst = A[:, 2 * g:2 * g + 2].rearrange("p j h t -> p (j h t)")
                    dve.copy_predicated(second(dst).rearrange("p (j b) m -> p j b m", j=2 * H), msk,
                                        banks[4 * (n % 2) + g][:].rearrange("p (j b m) -> p j b m", j=2 * H, m=m)
                                        ).then_inc(s("taken"), 1)

            w("q")
            dve.tensor_tensor(x[:], q[:], k[:], ALU.mult).then_inc(s("qk"), 1)
            w("own_mm")
            dve.tensor_copy(own[:], banks[7][:, 0:TB * H]).then_inc(s("own"), 1)
            w("own")
            for h in range(H):
                dve.tensor_tensor(A[:, :, h, :], ident[:].unsqueeze(1).to_broadcast([P, TB, P]),
                                  own[:].rearrange("p (j h) -> p h j", h=H)[:, h, :].unsqueeze(2)
                                  .to_broadcast([P, TB, P]), ALU.mult).then_inc(s("diagonal"), 1)
            differences(1)
            factors(0)
            factors(1)
            for n in range(NL):
                if n + 2 < NL:
                    differences(n + 2)
                take(n)
                if n + 2 < NL:
                    factors(n + 2)
            w("heads", H + 2)
            for n in range(8):
                w("kv_mm", n + 1)
                t, c = n // 2, n % 2
                dst = KV[:].rearrange("p (j two) v -> p j two v", two=2)[:, 2 * t:2 * t + 2, c, :]
                dve.tensor_tensor(dst, banks[n][:].rearrange("p (j v) -> p j v", v=WV),
                                  heads[:].unsqueeze(1).to_broadcast([P, 2, WV]), ALU.mult).then_inc(s("kv"), 1)
            w("decay")
            for c in range(NC):
                if c:
                    w("state", c)
                else:
                    w("kv", 8)
                dve.scalar_tensor_tensor(S[:, c + 1, :], S[:, c, :], e[:, c:c + 1], KV[:, c, :],
                                         ALU.mult, ALU.add).then_inc(s("state"), 1)
            w("osq")
            dve.tensor_reduce(small[:, 0, :], osq[:, 0:TB, :].rearrange("p j (h v) -> p (j h) v", v=DV), AX.X, ALU.add
                              ).then_inc(s("ssum"), 1)
            w("ssum")
            dve.tensor_scalar(small[:, 0, :], small[:, 0, :], 1.0 / DV, EPS, ALU.mult, ALU.add).then_inc(s("mean"), 1)
            w("root")
            dve.reciprocal(small[:, 1, :], small[:, 0, :]).then_inc(s("rstd"), 1)
            w("rstd")
            o3 = O[:, 0:TB, :].rearrange("p j (h v) -> p (j h) v", v=DV)
            dve.tensor_tensor(o3, o3, small[:, 1, :].unsqueeze(2).to_broadcast([P, TB * H, DV]), ALU.mult
                              ).then_inc(s("normed"), 1)
            for m in range(2):
                w("gained", 2 * m + 2)
                dve.tensor_tensor(result[m][:], result[m][:], sg[m][:], ALU.mult).then_inc(s("mixed"), 1)

        @block.tensor
        def _(pe):
            w = lambda name, n=1: pe.wait_ge(s(name), n)
            w("in_gd", 32)
            for h in range(NH):
                m = pe.matmul(banks[h][:], gate_up[:], gd[:, h * HALF:(h + 1) * HALF], start=True, stop=True)
            m.then_inc(s("gate_mm"), 1)
            w("in_v", 32)
            for n in range(2):
                for h in range(2):
                    if 2 * n + h < 2:
                        w("arg", 2)
                    for j in range(4):
                        m = pe.transpose(banks[2 * n + h][:, j * P:(j + 1) * P],
                                         vT[n][:, (4 * h + j) * P:(4 * h + j + 1) * P], ident[:])
                    m.then_inc(s("vnat_mm"), 1)
            w("heads", H + 2)
            w("qk")
            for j in range(TB):
                m = pe.matmul(banks[7][:, j * H:(j + 1) * H], x[:, j * P:(j + 1) * P], heads[:, 0::DV],
                              start=True, stop=True)
            m.then_inc(s("own_mm"), 1)
            w("kout")
            for h in range(2):
                for j in range(4):
                    m = pe.transpose(banks[4 + h][:, j * P:(j + 1) * P],
                                     kout[:, (4 * h + j) * P:(4 * h + j + 1) * P], ident[:])
                m.then_inc(s("knat_mm"), 1)
            w("vnat", 4)
            w("knat", 2)
            w("own")
            for n in range(NL):
                w("kf", n + 1)
                w("spread", H * (n + 1))
                for g in range(4):
                    if n >= 2:
                        w("taken", 4 * (n - 2) + g + 1)
                    for j in range(2):
                        t = 2 * g + j
                        m = pe.matmul(banks[4 * (n % 2) + g][:, j * H * C:(j + 1) * H * C],
                                      kf[n % 2][:, t * P:(t + 1) * P],
                                      qb[n % 2][:, t].rearrange("p h t -> p (h t)"), start=True, stop=True)
                    m.then_inc(s("level_mm"), 1)
            for n in range(8):
                t, c = n // 2, n % 2
                w("taken", 4 * (NL - 2 + n // 4) + n % 4 + 1)
                cs = slice(C * c, C * c + C)
                for j in range(2):
                    m = pe.matmul(banks[n][:, j * WV:(j + 1) * WV], knat[cs, 2 * t + j, :], vnat[cs, 2 * t + j, :],
                                  start=True, stop=True)
                m.then_inc(s("kv_mm"), 1)
            w("kv", 8)
            w("qin")
            for n in range(4):
                w("state", min(4 * n + 4, NC))
                for jj in range(2):
                    j = 2 * n + jj
                    o = slice(jj * WV, (jj + 1) * WV)
                    for c in range(2):
                        pe.matmul(banks[n][C * c:C * c + C, o], qin[:, j * P + C * c:j * P + C * c + C],
                                  S[:, 2 * j + c, :], start=True, stop=True)
                    for h in range(H):
                        m = pe.matmul(banks[n][:, jj * WV + DV * h:jj * WV + DV * h + DV], A[:, j, h, :],
                                      vnat[:, j, DV * h:DV * h + DV], start=False, stop=True, skip_group_check=True)
                m.then_inc(s("o_mm"), 1)
            w("normed")
            for m_ in range(2):
                for h in range(2):
                    for jj in range(4):
                        j = 4 * h + jj
                        m = pe.transpose(banks[4 + 2 * m_ + h][:, jj * P:(jj + 1) * P],
                                         O[:, j, m_ * P:(m_ + 1) * P], ident[:])
                    m.then_inc(s("back"), 1)


def stick_breaking(nc, con, args, proj, mixed, ahead=None):
    ident, col = con["ident"], con["col"]
    mask = {name: con["sb_masks"][:, n, :] for n, name in enumerate(SB_MASKS)}
    DH = 64
    QC = T // HALF
    PER = HALF // P
    CAP = float(2 ** 60)
    UNITS = []
    for c in range(QC):
        for kb in range(PER * (c + 1) - 1, -1, -1):
            for h in range(2):
                UNITS.append((h, c, kb, max(0, (kb - PER * c) * P), kb == PER * (c + 1) - 1))
    NU = len(UNITS)
    NZ, AHEAD = 4, 2
    with ExitStack() as st:
        r = Region(nc, st, "sb")
        qd, kd = [r.sb(f"qd{h}", [P, T]) for h in range(2)], [r.sb(f"kd{h}", [P, T]) for h in range(2)]
        vp = r.sb("vp", [P, T])
        kS = [r.sb(f"kS{h}", [P, T], F32R) for h in range(2)]
        qH, qL = [r.sb(f"qH{h}", [P, T], F32R) for h in range(2)], [r.sb(f"qL{h}", [P, T], F32R) for h in range(2)]
        vn = r.sb("vn", [P, TB, P])
        E = [r.sb(f"E{n}", [P, HALF]) for n in range(4)]
        SP = [r.sb(f"SP{n}", [P, HALF]) for n in range(4)]
        R = [[r.sb(f"R{h}{n}", [P, HALF]) for n in range(2)] for h in range(2)]
        W = [r.sb(f"W{n}", [P, HALF]) for n in range(4)]
        tri, ones = r.sb("tri", [P, P]), r.sb("ones", [P, P])
        O, osq = r.sb("O", [P, TB, P]), r.sb("osq", [P, TB, P])
        outT = r.sb("outT", [P, T])
        small = r.sb("small", [P, 2, 2 * TB])
        small_gain = r.sb("gain", [P, 1])
        Z = [r.bank(f"Z{n}") for n in range(NZ)]
        OB = [[r.bank(f"O{h}{c}") for c in range(QC)] for h in range(2)]
        sems = {}

        def s(name):
            if name not in sems:
                sems[name] = r.sem(name)
            return sems[name]

        ND = sum(1 for x in UNITS if x[2] >= PER * x[1])
        LAST = PAIRS - 1
        SQUARE_AT, MEAN_AT, ROOT_AT, SCALE_AT, BACK_AT = 0, 3, 2, 5, 6
        SPLIT_AT = BACK_AT + 2
        BACK = (OB[0][1], OB[1][1])

        block = st.enter_context(nc.Block())

        def span(u):
            h, c, kb, off, first = UNITS[u]
            return slice(off, HALF)

        @block.sync
        def _(sp):
            sp.sem_inc(s("stored"), 16)

            def load(i, reused):
                if reused:
                    sp.wait_ge(s("k"), i * 2)
                    sp.wait_ge(s("q"), i * 2)
                    sp.wait_ge(s("v_mm"), i * 2)
                for h in range(2):
                    for half in range(2):
                        rows = slice(DH * half, DH * half + DH)
                        sp.dma_start(kd[h][rows, :], proj[bass.ds(i * P + SB_K + DH * h, DH), :]).then_inc(s("in_k"), 16)
                        sp.dma_start(qd[h][rows, :], proj[bass.ds(i * P + SB_Q + DH * h, DH), :]).then_inc(s("in_q"), 16)
                sp.dma_start(vp[:], proj[bass.ds(i * P + SB_V, P), :]).then_inc(s("in_v"), 16)

            def store(i):
                sp.wait_ge(s("mixed"), i * 2 + 2)
                sp.sem_inc(s("sp_passed"), 1)
                sp.dma_start(mixed[bass.ds(i * P, P), :], outT[:]).then_inc(s("stored"), 16)

            load(0, False)
            with sp.Fori(0, LAST) as i:
                load(i + 1, True)
                store(i)
            if ahead:
                ahead.load(sp)
            store(LAST)
            sp.wait_ge(s("stored"), 16 * PAIRS + 16)

        @block.gpsimd
        def _(pool):
            def units(i, later):
                nth = [0, 0]
                for u in range(NU):
                    h, c, kb, off, first = UNITS[u]
                    new, old = R[h][(nth[h] + 1) % 2], R[h][nth[h] % 2]
                    nth[h] += 1
                    pool.wait_ge(s("sp"), i * NU + u + 1)
                    if u >= 4 or later:
                        pool.wait_ge(s("tri_mm"), i * NU + u - 1)
                    if kb > 0:
                        if first:
                            pool.sem_inc(s("pool_passed"), 1)
                            pool.tensor_copy(new[:, off:], SP[u % 4][:, off:]).then_inc(s("sum"), 1)
                        else:
                            pool.wait_ge(s("sum"), i * NU + u - 1)
                            pool.tensor_tensor(new[:, off:], old[:, off:], SP[u % 4][:, off:], ALU.add
                                               ).then_inc(s("sum"), 1)
                        if off:
                            pool.memset(new[:, off - P:off], 0.0)
                    else:
                        pool.sem_inc(s("sum"), 1)
                    if kb >= PER * c:
                        pool.wait_ge(s("weight"), i * NU + u + 1)
                        pool.sem_inc(s("pool_passed"), 1)
                        w = W[u % 4][:, off:off + P]
                        pool.affine_select(out=w, in_=w, compare_op=ALU.is_gt, fill=0.0, base=0,
                                           pattern=[[1, P]], channel_multiplier=-1)
                    pool.drain().then_inc(s("cut"), 1)

            units(0, False)
            with pool.Fori(1, PAIRS) as i:
                units(i, True)

        @block.scalar
        def _(act):
            def split(i, h, later):
                act.wait_ge(s("in_k"), i * 64 + 64)
                act.wait_ge(s("in_q"), i * 64 + 64)
                if later:
                    act.wait_ge(s("z"), i * NU)
                act.copy(kS[h][:], kd[h][:]).then_inc(s("k_high"), 1)
                act.activation(qH[h][:], qd[h][:], ACT.Copy, scale=DH ** -0.5).then_inc(s("q_high"), 1)

            def take_outputs(i):
                act.wait_ge(s("v_mul"), i * NU + NU)
                for h in range(2):
                    for c in range(QC):
                        act.copy(O[:, PER * c:PER * (c + 1), DH * h:DH * h + DH],
                                 OB[h][c][:, 0:PER * DH].rearrange("p (j v) -> p j v", v=DH)).then_inc(s("o"), 1)

            def square(i):
                act.wait_ge(s("o"), i * 4 + 4)
                act.activation(osq[:], O[:], ACT.Square).then_inc(s("osq"), 1)

            def root(i):
                act.wait_ge(s("mean"), i + 1)
                act.activation(small[:, 0, :], small[:, 0, :], ACT.Ln).then_inc(s("root"), 1)
                act.wait_ge(s("root"), i * 2 + 1)
                act.activation(small[:, 1, :], small[:, 0, :], ACT.Exp, scale=-0.5).then_inc(s("root"), 1)

            def gain(i):
                act.wait_ge(s("gain"), i + 1)
                act.wait_ge(s("stored"), i * 16 + 16)
                for n in range(2):
                    act.wait_ge(s("back"), i * 2 + n + 1)
                    act.activation(outT[:, n * HALF:(n + 1) * HALF], BACK[n][:], ACT.Copy, scale=small_gain[:]
                                   ).then_inc(s("mixed"), 1)

            def units(i, later, last):
                for n in range(2):
                    act.wait_ge(s("v_mm"), i * 2 + n + 1)
                    act.copy(vn[:, 4 * n:4 * n + 4, :], Z[n][:].rearrange("p (j f) -> p j f", f=P)).then_inc(s("v"), 1)

                def exp_of_z(u):
                    act.wait_ge(s("z"), i * NU + u + 1)
                    if u >= 4 or later:
                        act.wait_ge(s("sp"), i * NU + u - 3)
                    act.activation(E[u % 4][:, span(u)], Z[u % NZ][:, span(u)], ACT.Exp).then_inc(s("exp"), 1)

                def log_of_e(u):
                    act.wait_ge(s("capped"), i * NU + u + 1)
                    act.activation(E[u % 4][:, span(u)], E[u % 4][:, span(u)], ACT.Ln, bias=1.0).then_inc(s("log"), 1)

                def weight(u):
                    act.wait_ge(s("tri_mm"), i * NU + u + 1)
                    if u >= 4 or later:
                        act.wait_ge(s("v_mul"), i * NU + u - 3)
                    act.activation(W[u % 4][:, span(u)], Z[u % NZ][:, span(u)], ACT.Exp).then_inc(s("weight"), 1)

                for u in range(-AHEAD, NU):
                    if u + AHEAD < NU:
                        exp_of_z(u + AHEAD)
                    if u >= 0:
                        weight(u)
                    if u + AHEAD < NU:
                        log_of_e(u + AHEAD)
                    elif not last:
                        split(i + 1, u + AHEAD - NU, True)
                    if last and ahead and 0 <= u - SPLIT_AT < len(ahead.pieces):
                        ahead.split_high(act, u - SPLIT_AT)
                    if later and u == SQUARE_AT:
                        square(i - 1)
                    if later and u == ROOT_AT:
                        root(i - 1)
                    if later and u == BACK_AT:
                        gain(i - 1)
                take_outputs(i)

            act.preload_act_table_set(EXP_LN)
            for h in range(2):
                split(0, h, False)
            units(0, False, False)
            with act.Fori(1, LAST) as i:
                units(i, True, False)
            units(LAST, True, True)
            square(LAST)
            root(LAST)
            gain(LAST)

        @block.vector
        def _(dve):
            dve.tensor_scalar(tri[:], mask["to_diag"], -1.0, None, ALU.mult)
            dve.tensor_scalar(ones[:], mask["ones"], -1.0, None, ALU.mult).then_inc(s("signs"), 1)

            def split(i):
                for h in range(2):
                    dve.wait_ge(s("k_high"), i * 2 + h + 1)
                    dve.tensor_tensor(kS[h][DH:P, :], kd[h][DH:P, :], kS[h][DH:P, :].bitcast(F32), ALU.subtract
                                      ).then_inc(s("k"), 1)
                    dve.wait_ge(s("q_high"), i * 2 + h + 1)
                    dve.scalar_tensor_tensor(qL[h][:], qd[h][:], DH ** -0.5, qH[h][:].bitcast(F32),
                                             ALU.mult, ALU.subtract).then_inc(s("q"), 1)

            def mean(i):
                dve.tensor_copy(small_gain[:], col[:, bass.ds(i + COL["sb_norm_g"], 1)]).then_inc(s("gain"), 1)
                dve.wait_ge(s("osq"), i + 1)
                dve.tensor_reduce(small[:, 0, :], osq[:].rearrange("p j (h v) -> p (j h) v", v=DH), AX.X, ALU.add
                                  ).then_inc(s("ssum"), 1)
                dve.wait_ge(s("ssum"), i + 1)
                dve.tensor_scalar(small[:, 0, :], small[:, 0, :], 1.0 / DH, EPS, ALU.mult, ALU.add).then_inc(s("mean"), 1)

            def scale(i):
                dve.wait_ge(s("root"), i * 2 + 2)
                o3 = O[:].rearrange("p j (h v) -> p (j h) v", v=DH)
                dve.tensor_tensor(o3, o3, small[:, 1, :].unsqueeze(2).to_broadcast([P, 2 * TB, DH]), ALU.mult
                                  ).then_inc(s("normed"), 1)

            def units(i, later, last=False):
                def cap(u):
                    dve.wait_ge(s("exp"), i * NU + u + 1)
                    dve.tensor_scalar(E[u % 4][:, span(u)], E[u % 4][:, span(u)], CAP, None, ALU.min
                                      ).then_inc(s("capped"), 1)

                def softplus(u):
                    h, c, kb, off, first = UNITS[u]
                    dve.wait_ge(s("log"), i * NU + u + 1)
                    if u >= 4 or later:
                        dve.wait_ge(s("tri_mm"), i * NU + u - 3)
                        dve.wait_ge(s("sum"), i * NU + u - 3)
                    diag = kb >= PER * c
                    m = dve.tensor_tensor(SP[u % 4][:, span(u)], Z[u % NZ][:, span(u)], E[u % 4][:, span(u)], ALU.max)
                    if diag:
                        m.then_inc(s("diag"), 1)
                        D = sum(1 for x in UNITS[:u + 1] if x[2] >= PER * x[1])
                        dve.wait_ge(s("diag"), i * ND + D)
                        w = SP[u % 4][:, off:off + P]
                        m = dve.tensor_tensor(w, w, mask["above"], ALU.mult)
                    m.then_inc(s("sp"), 1)

                for u in range(NU):
                    cap(u)
                    softplus(u)
                    if last and ahead and 0 <= u - AHEAD - SPLIT_AT < len(ahead.pieces):
                        ahead.split_low(dve, u - AHEAD - SPLIT_AT)
                    if later and u == MEAN_AT:
                        mean(i - 1)
                    if later and u == SCALE_AT:
                        scale(i - 1)

            split(0)
            units(0, False)
            with dve.Fori(1, LAST) as i:
                split(i)
                units(i, True)
            split(LAST)
            units(LAST, True, last=True)
            mean(LAST)
            scale(LAST)

        @block.tensor
        def _(pe):
            pe.wait_ge(s("signs"), 1)

            def back(i):
                pe.wait_ge(s("normed"), i + 1)
                for n in range(2):
                    for j in range(4):
                        m = pe.transpose(BACK[n][:, j * P:(j + 1) * P], O[:, 4 * n + j, :], ident[:])
                    m.then_inc(s("back"), 1)

            def units(i, later):
                pe.wait_ge(s("in_v"), i * 16 + 16)
                if later:
                    pe.wait_ge(s("weight"), i * NU)
                for n in range(2):
                    for j in range(4):
                        m = pe.transpose(Z[n][:, j * P:(j + 1) * P], vp[:, (4 * n + j) * P:(4 * n + j + 1) * P], ident[:])
                    m.then_inc(s("v_mm"), 1)
                pe.wait_ge(s("k"), i * 2 + 2)
                pe.wait_ge(s("q"), i * 2 + 2)
                pe.wait_ge(s("v"), i * 2 + 2)

                def scores(u):
                    h, c, kb, off, first = UNITS[u]
                    if u >= NZ:
                        pe.wait_ge(s("weight"), i * NU + u - NZ + 1)
                    qs = slice(c * HALF + off, (c + 1) * HALF)
                    pe.matmul(Z[u % NZ][:, span(u)], kS[h][:, kb * P:(kb + 1) * P], qL[h][:, qs], start=True, stop=False)
                    pe.matmul(Z[u % NZ][:, span(u)], kS[h][:, kb * P:(kb + 1) * P], qH[h][:, qs], start=False, stop=True
                              ).then_inc(s("z"), 1)

                nth = [0, 0]

                def sums(u):
                    h, c, kb, off, first = UNITS[u]
                    rd = R[h][nth[h] % 2]
                    nth[h] += 1
                    pe.wait_ge(s("sp"), i * NU + u + 1)
                    z = Z[u % NZ][:, span(u)]
                    m = pe.matmul(z, tri[:], SP[u % 4][:, span(u)], start=False, stop=True, skip_group_check=True)
                    if not first:
                        pe.wait_ge(s("cut"), i * NU + u - 1)
                        m = pe.matmul(z, ones[:], rd[:, span(u)], start=False, stop=True, skip_group_check=True)
                    m.then_inc(s("tri_mm"), 1)

                opened = set()

                def values(u):
                    h, c, kb, off, first = UNITS[u]
                    pe.wait_ge(s("cut"), i * NU + u + 1)
                    pe.wait_ge(s("weight"), i * NU + u + 1)
                    if later and (h, c) == (0, 0) and first:
                        pe.wait_ge(s("o"), i * 4)
                    if later and (h, c) == (0, 1) and first:
                        pe.wait_ge(s("mixed"), i * 2)
                    for j in range(off // P, PER):
                        m = pe.matmul(OB[h][c][:, j * DH:(j + 1) * DH], W[u % 4][:, j * P:(j + 1) * P],
                                      vn[:, kb, DH * h:DH * h + DH], start=(h, c) not in opened, stop=True,
                                      skip_group_check=True)
                        opened.add((h, c))
                    m.then_inc(s("v_mul"), 1)

                for u in range(-AHEAD, NU + 1):
                    if u + AHEAD < NU:
                        scores(u + AHEAD)
                    if 0 <= u < NU:
                        sums(u)
                    if u >= 1:
                        values(u - 1)
                    if later and u == BACK_AT:
                        back(i - 1)

            units(0, False)
            with pe.Fori(1, PAIRS) as i:
                units(i, True)
            pe.wait_ge(s("o"), PAIRS * 4)
            back(LAST)


def hybrid_block(nc, args, out):
    proj = nc.dram_tensor("projected", [IN_W, T], F32, kind="Internal").ap()
    mixed = nc.dram_tensor("mixed", [MIX, T], F32, kind="Internal").ap()
    x1 = nc.dram_tensor("x_after_mixers", [T, D], F32, kind="Internal").ap()
    with ExitStack() as st:
        r = Region(nc, st, "all")
        con = {"ident": r.sb("ident", [P, P]), "col": r.sb("col", [P, P]),
               "sb_masks": r.sb("sb_masks", [P, len(SB_MASKS), P])}
        with ExitStack() as mixers:
            m = Region(nc, mixers, "mix")
            con["masks"], con["levels"] = m.sb("masks", [P, len(MASKS), P]), m.sb("levels", [P, 6, P])
            with ExitStack() as rows:
                first = Rows(nc, rows, args["x"], args["w_in"])
                constants(nc, con, args, first)
                projection(nc, con, first, proj)
            rwkv(nc, con, args, proj, mixed)
            gla(nc, con, args, proj, mixed)
        hH, hL = r.sb("hH", [P, KB, T], F32R), r.sb("hL", [P, KB, T], F32R)
        with ExitStack() as output:
            ahead = Ahead(nc, output, mixed, args["w_out"], hH, hL)
            stick_breaking(nc, con, args, proj, mixed, ahead)
            output_projection(nc, con, ahead, args["x"], args["post_mix_g"], args["pre_ffn_g"], x1, hH, hL)
        feed_forward(nc, con, x1, args["w_ff1"], args["w_ff2"], args["post_ffn_g"], hH, hL, out)


_INS = ["x", "pre_mix_g", "w_in", "sb_norm_g", "rw_mu", "rw_w0", "rw_w_up", "rw_a0", "rw_a_up", "rw_g_up",
        "rw_k_k", "rw_k_a", "rw_r_k", "rw_gn_g", "rw_gn_b", "gla_gate_up", "gla_gate_b", "gla_norm_g",
        "w_out", "post_mix_g", "pre_ffn_g", "w_ff1", "w_ff2", "post_ffn_g"]


def kernel(**inputs):
    import numpy as np
    import concourse.bacc as bacc
    from concourse.bass_utils import run_bass_kernel_spmd

    nc = bacc.Bacc("TRN2", target_bir_lowering=False, num_devices=1)
    arrays, args = {}, {}
    for name in _INS:
        a = np.ascontiguousarray(inputs[name])
        arrays[f"in_{name}"] = a
        args[name] = nc.dram_tensor(f"in_{name}", a.shape, mybir.dt.from_np(a.dtype), kind="ExternalInput").ap()
    out = nc.dram_tensor("out_x", [1, T, D], F32, kind="ExternalOutput").ap()
    hybrid_block(nc, args, out)
    r = run_bass_kernel_spmd(nc, [arrays], core_ids=[0])
    return r.results[0]["out_x"]
```
